# Optimizing a Trainium2 kernel written in Bass

```python
import jax, jax.numpy as jnp
from jax import lax
import numpy as np

D_MODEL = 1024
BATCH = 1
SEQ = 256
DEPTH = 2
DEC_BATCH = 8
DEC_SEQ = 4
PAST_LEN = 1024
PAGE_SIZE = 128

HEAD_DIM = 64
ROT_DIM = HEAD_DIM // 4
ROPE_THETA = 500000.0
EPS = 1e-6
BLK = 128
NEG = -1e30

H_A = 8
Q_LORA = 384
KV_LORA = 256
NOPE_A = 64
ROPE_A = 32
V_A = 64
MLA_SCALE = (NOPE_A + ROPE_A) ** -0.5

H_B = 8
DIL_PATTERNS = ((128, 1), (512, 4), (2048, 16))
B_WINDOW = 2048

H_C = 16
KV_C = 4
C_WINDOW = 128

F_DENSE = 2816
N_EXPERTS = 8
TOP_K = 2
F_EXPERT = 3584

N_AB = (DEPTH + 1) // 2
N_C = DEPTH // 2
OFF_KV = Q_LORA
OFF_KR = Q_LORA + KV_LORA
OFF_B = Q_LORA + KV_LORA + ROPE_A
D_IN_AB = OFF_B + 3 * H_B * HEAD_DIM
D_CAT_AB = H_A * V_A + H_B * HEAD_DIM
D_QKV_C = (H_C + 2 * KV_C) * HEAD_DIM

kernel_name = 'hybrid_mla_dilated_swa_sink_moe_step'

F32 = jnp.float32

def rms_norm(x, g):
    xf = x.astype(F32)
    y = xf * lax.rsqrt(jnp.mean(xf * xf, axis=-1, keepdims=True) + EPS)
    return (y * g.astype(F32)).astype(x.dtype)

def modulate(h, shift, scale):
    return h * (1 + scale[:, None, :]) + shift[:, None, :]

def rope(x, pos, rot):
    half = rot // 2
    inv = ROPE_THETA ** (-jnp.arange(half, dtype=F32) / half)
    ang = pos.astype(F32)[:, None] * inv[None, :]
    cos = jnp.cos(ang)[:, None, :]
    sin = jnp.sin(ang)[:, None, :]
    xr = x[..., :rot].astype(F32)
    x1 = xr[..., :half]
    x2 = xr[..., half:]
    xr = jnp.concatenate([x1 * cos - x2 * sin, x2 * cos + x1 * sin], axis=-1).astype(x.dtype)
    return jnp.concatenate([xr, x[..., rot:]], axis=-1)

def banded_attn(q, k, v, max_dist, sink):
    n, L, hq, dh = q.shape
    g = k.shape[2]
    r = hq // g
    nb = -(-L // BLK)
    lp = nb * BLK
    pad = lp - L
    qb = jnp.pad(q, ((0, 0), (0, pad), (0, 0), (0, 0))).reshape(n, nb, BLK, g, r, dh)

    def band(t):
        tp = jnp.pad(t, ((0, 0), (BLK, pad), (0, 0), (0, 0)))
        prev = tp[:, :lp].reshape(n, nb, BLK, g, dh)
        cur = tp[:, BLK:].reshape(n, nb, BLK, g, dh)
        return jnp.concatenate([prev, cur], axis=2)

    kb = band(k)
    vb = band(v)
    s = jnp.einsum('nbqgrd,nbkgd->nbgrqk', qb, kb, preferred_element_type=F32) * dh ** -0.5
    a = jnp.arange(BLK)[:, None]
    bi = jnp.arange(2 * BLK)[None, :]
    dist = a - bi + BLK
    band_ok = (dist >= 0) & (dist <= max_dist)
    real = (jnp.arange(nb)[:, None, None] > 0) | (bi >= BLK)[None]
    mask = (band_ok[None] & real)[None, :, None, None]
    s = jnp.where(mask, s, NEG)
    m = jnp.max(s, axis=-1, keepdims=True)
    if sink is not None:
        snk = sink.astype(F32).reshape(g, r)[None, None, :, :, None, None]
        m = jnp.maximum(m, snk)
    p = jnp.exp(s - m)
    l = jnp.sum(p, axis=-1, keepdims=True)
    if sink is not None:
        l = l + jnp.exp(snk - m)
    o = jnp.einsum('nbgrqk,nbkgd->nbqgrd', p / l, vb.astype(F32)).reshape(n, lp, hq, dh)[:, :L]
    lse = (m + jnp.log(l))[..., 0].transpose(0, 1, 4, 2, 3).reshape(n, lp, hq)[:, :L]
    return o, lse

def combine_dilations(outs, lses):
    wts = jax.nn.softmax(jnp.stack(lses, axis=0), axis=0)[..., None]
    return jnp.sum(wts * jnp.stack(outs, axis=0), axis=0)

def dilated_prompt(q, k, v):
    b, s, h, dh = q.shape
    outs, lses = [], []
    for w, d in DIL_PATTERNS:
        L = s // d

        def to_res(t):
            return t.reshape(b, L, d, h, dh).transpose(0, 2, 1, 3, 4).reshape(b * d, L, h, dh)

        o, lse = banded_attn(to_res(q), to_res(k), to_res(v), w // d, None)
        outs.append(o.reshape(b, d, L, h, dh).transpose(0, 2, 1, 3, 4).reshape(b, s, h, dh))
        lses.append(lse.reshape(b, d, L, h).transpose(0, 2, 1, 3).reshape(b, s, h))
    return combine_dilations(outs, lses)

def dilated_sample(q, k_all, v_all, buf_len):
    t = q.shape[1]
    dh = q.shape[-1]
    outs, lses = [], []
    for w, d in DIL_PATTERNS:
        j = w // d + 1
        idx = buf_len + jnp.arange(t)[:, None] - d * jnp.arange(j)[None, :]
        valid = idx >= 0
        idx = jnp.maximum(idx, 0)
        kg = k_all[:, idx]
        vg = v_all[:, idx]
        s = jnp.einsum('bthd,btjhd->bthj', q, kg, preferred_element_type=F32) * dh ** -0.5
        s = jnp.where(valid[None, :, None, :], s, NEG)
        m = jnp.max(s, axis=-1, keepdims=True)
        p = jnp.exp(s - m)
        l = jnp.sum(p, axis=-1, keepdims=True)
        outs.append(jnp.einsum('bthj,btjhd->bthd', p / l, vg.astype(F32)))
        lses.append((m + jnp.log(l))[..., 0])
    return combine_dilations(outs, lses)

def window_sink_sample(q, k_all, v_all, buf_len, sink):
    bd, t, hq, dh = q.shape
    g = k_all.shape[2]
    r = hq // g
    lk = k_all.shape[1]
    qg = q.reshape(bd, t, g, r, dh)
    s = jnp.einsum('btgrd,bkgd->bgrtk', qg, k_all, preferred_element_type=F32) * dh ** -0.5
    dist = buf_len + jnp.arange(t)[:, None] - jnp.arange(lk)[None, :]
    mask = (dist >= 0) & (dist < C_WINDOW)
    s = jnp.where(mask, s, NEG)
    snk = sink.astype(F32).reshape(g, r)[None, :, :, None, None]
    m = jnp.maximum(jnp.max(s, axis=-1, keepdims=True), snk)
    p = jnp.exp(s - m)
    l = jnp.sum(p, axis=-1, keepdims=True) + jnp.exp(snk - m)
    o = jnp.einsum('bgrtk,bkgd->btgrd', p / l, v_all.astype(F32))
    return o.reshape(bd, t, hq, dh)

def mla_prompt(q_lat, q_rope, ckv, krope):
    b, s, h, c = q_lat.shape
    nq = s // BLK
    qlb = q_lat.reshape(b, nq, BLK, h, c).transpose(1, 0, 2, 3, 4)
    qrb = q_rope.reshape(b, nq, BLK, h, ROPE_A).transpose(1, 0, 2, 3, 4)
    kpos = jnp.arange(s)

    def one(args):
        i, ql, qr = args
        sc = (jnp.einsum('bqhc,bkc->bhqk', ql, ckv, preferred_element_type=F32)
              + jnp.einsum('bqhr,bkr->bhqk', qr, krope, preferred_element_type=F32)) * MLA_SCALE
        qpos = i * BLK + jnp.arange(BLK)
        mask = kpos[None, :] <= qpos[:, None]
        p = jax.nn.softmax(jnp.where(mask, sc, NEG), axis=-1)
        return jnp.einsum('bhqk,bkc->bqhc', p, ckv.astype(F32)).astype(q_lat.dtype)

    o = lax.map(one, (jnp.arange(nq), qlb, qrb))
    return o.transpose(1, 0, 2, 3, 4).reshape(b, s, h, c)

def mla_sample(q_lat, q_rope, ckv_all, krope_all, past_len):
    t = q_lat.shape[1]
    lk = ckv_all.shape[1]
    sc = (jnp.einsum('bthc,bkc->bhtk', q_lat, ckv_all, preferred_element_type=F32)
          + jnp.einsum('bthr,bkr->bhtk', q_rope, krope_all, preferred_element_type=F32)) * MLA_SCALE
    mask = jnp.arange(lk)[None, :] <= past_len + jnp.arange(t)[:, None]
    p = jax.nn.softmax(jnp.where(mask, sc, NEG), axis=-1)
    return jnp.einsum('bhtk,bkc->bthc', p, ckv_all.astype(F32)).astype(q_lat.dtype)

def mixer_ab(h, pos, P, i, past):
    bx, t, _ = h.shape
    z = h @ P['w_in_ab'][i]
    q = (rms_norm(z[..., :OFF_KV], P['g_q_a'][i]) @ P['w_q_b'][i]).reshape(bx, t, H_A, NOPE_A + ROPE_A)
    q_nope = q[..., :NOPE_A]
    q_rope = rope(q[..., NOPE_A:], pos, ROPE_A)
    ckv = rms_norm(z[..., OFF_KV:OFF_KR], P['g_kv_a'][i])
    krope = rope(z[..., OFF_KR:OFF_B][:, :, None, :], pos, ROPE_A)[:, :, 0]
    w_uk = P['w_kv_b'][i][..., :NOPE_A]
    w_uv = P['w_kv_b'][i][..., NOPE_A:]
    q_lat = jnp.einsum('bthn,chn->bthc', q_nope, w_uk)
    zb = z[..., OFF_B:].reshape(bx, t, 3, H_B, HEAD_DIM)
    qb = rope(zb[:, :, 0], pos, ROT_DIM)
    kb = rope(zb[:, :, 1], pos, ROT_DIM)
    vb = zb[:, :, 2]
    if past is None:
        o_lat = mla_prompt(q_lat, q_rope, ckv, krope)
        o_b = dilated_prompt(qb, kb, vb)
        lb = min(B_WINDOW, t)
        st = (ckv, krope, kb[:, t - lb:], vb[:, t - lb:])
    else:
        pt = past['page_table']
        ckv_all = jnp.concatenate([past['ckv'][i][pt].reshape(bx, -1, KV_LORA), ckv], axis=1)
        krope_all = jnp.concatenate([past['krope'][i][pt].reshape(bx, -1, ROPE_A), krope], axis=1)
        o_lat = mla_sample(q_lat, q_rope, ckv_all, krope_all, past['past_len'])
        kb_all = jnp.concatenate([past['bk'][i], kb], axis=1)
        vb_all = jnp.concatenate([past['bv'][i], vb], axis=1)
        o_b = dilated_sample(qb, kb_all, vb_all, past['bk'].shape[2])
        st = (ckv, krope, kb, vb)
    o_a = jnp.einsum('bthc,chv->bthv', o_lat, w_uv).reshape(bx, t, H_A * V_A)
    o_b = o_b.astype(h.dtype).reshape(bx, t, H_B * HEAD_DIM)
    out = jnp.concatenate([o_a, o_b], axis=-1) @ P['w_out_ab'][i]
    return out, st

def mixer_c(h, pos, P, i, past):
    bx, t, _ = h.shape
    z = h @ P['w_qkv_c'][i]
    q = rope(z[..., :H_C * HEAD_DIM].reshape(bx, t, H_C, HEAD_DIM), pos, ROT_DIM)
    k = rope(z[..., H_C * HEAD_DIM:(H_C + KV_C) * HEAD_DIM].reshape(bx, t, KV_C, HEAD_DIM), pos, ROT_DIM)
    v = z[..., (H_C + KV_C) * HEAD_DIM:].reshape(bx, t, KV_C, HEAD_DIM)
    if past is None:
        o, _ = banded_attn(q, k, v, C_WINDOW - 1, P['sinks_c'][i])
        lc = min(C_WINDOW, t)
        st = (k[:, t - lc:], v[:, t - lc:])
    else:
        k_all = jnp.concatenate([past['ck'][i], k], axis=1)
        v_all = jnp.concatenate([past['cv'][i], v], axis=1)
        o = window_sink_sample(q, k_all, v_all, past['ck'].shape[2], P['sinks_c'][i])
        st = (k, v)
    out = o.astype(h.dtype).reshape(bx, t, H_C * HEAD_DIM) @ P['w_out_c'][i]
    return out, st

def swiglu(h, w_in, w_out):
    gu = h @ w_in
    f = w_out.shape[0]
    return (jax.nn.silu(gu[..., :f]) * gu[..., f:]) @ w_out

def moe_swiglu(h, w_router, b_router, w_in, w_out):
    logits = jnp.einsum('btd,de->bte', h, w_router, preferred_element_type=F32) + b_router.astype(F32)
    top_v, top_i = lax.top_k(logits, TOP_K)
    gates = jax.nn.softmax(top_v, axis=-1)
    dense_gate = jnp.sum(jax.nn.one_hot(top_i, N_EXPERTS, dtype=F32) * gates[..., None], axis=-2)
    out = jnp.zeros(h.shape, F32)
    for e in range(N_EXPERTS):
        out = out + dense_gate[..., e:e + 1] * swiglu(h, w_in[e], w_out[e]).astype(F32)
    return out.astype(h.dtype)

def trunk(x, c, pos, P, past):
    cs = jax.nn.silu(c)
    st = {'ckv': [], 'krope': [], 'bk': [], 'bv': [], 'ck': [], 'cv': []}
    for l in range(DEPTH):
        i = l // 2
        mod = cs @ P['w_ada'][l] + P['b_ada'][l]
        sh1, sc1, gt1, sh2, sc2, gt2 = jnp.split(mod, 6, axis=-1)
        h = modulate(rms_norm(x, P['g_pre_mix'][l]), sh1, sc1)
        if l % 2 == 0:
            mix, (ckv, krope, bk, bv) = mixer_ab(h, pos, P, i, past)
            st['ckv'].append(ckv)
            st['krope'].append(krope)
            st['bk'].append(bk)
            st['bv'].append(bv)
        else:
            mix, (ck, cv) = mixer_c(h, pos, P, i, past)
            st['ck'].append(ck)
            st['cv'].append(cv)
        x = x + gt1[:, None, :] * rms_norm(mix, P['g_post_mix'][l])
        h = modulate(rms_norm(x, P['g_pre_ffn'][l]), sh2, sc2)
        if l % 2 == 0:
            f = swiglu(h, P['w_ffd_in'][i], P['w_ffd_out'][i])
        else:
            f = moe_swiglu(h, P['w_router'][i], P['b_router'][i], P['w_moe_in'][i], P['w_moe_out'][i])
        x = x + gt2[:, None, :] * rms_norm(f, P['g_post_ffn'][l])
    return x, {name: jnp.stack(v, axis=0) for name, v in st.items()}

def setup_inputs(seed: int = 0) -> dict:
    key = jax.random.key(seed)
    keys = jax.random.split(key, 40)
    cnt = [0]

    def nk():
        k = keys[cnt[0]]
        cnt[0] += 1
        return k

    def nrm(shape, scale):
        return jax.random.normal(nk(), shape, F32) * scale

    def gain(shape):
        return 1.0 + 0.05 * jax.random.normal(nk(), shape, F32)

    n_pages = PAST_LEN // PAGE_SIZE
    n_used = DEC_BATCH * n_pages
    n_pool = n_used + n_used // 4
    lbuf_b = min(B_WINDOW, PAST_LEN)
    lbuf_c = min(C_WINDOW, PAST_LEN)
    d = D_MODEL
    inp = {}
    inp['x_prompt'] = nrm((BATCH, SEQ, d), 1.0)
    inp['x_sample'] = nrm((DEC_BATCH, DEC_SEQ, d), 1.0)
    inp['c_prompt'] = nrm((BATCH, d), 1.0)
    inp['c_sample'] = nrm((DEC_BATCH, d), 1.0)
    inp['cache_mla_ckv'] = nrm((N_AB, n_pool, PAGE_SIZE, KV_LORA), 1.0)
    inp['cache_mla_krope'] = nrm((N_AB, n_pool, PAGE_SIZE, ROPE_A), 1.0)
    inp['cache_b_k'] = nrm((N_AB, DEC_BATCH, lbuf_b, H_B, HEAD_DIM), 1.0)
    inp['cache_b_v'] = nrm((N_AB, DEC_BATCH, lbuf_b, H_B, HEAD_DIM), 1.0)
    inp['cache_c_k'] = nrm((N_C, DEC_BATCH, lbuf_c, KV_C, HEAD_DIM), 1.0)
    inp['cache_c_v'] = nrm((N_C, DEC_BATCH, lbuf_c, KV_C, HEAD_DIM), 1.0)
    inp['page_table'] = jax.random.permutation(nk(), n_pool)[:n_used].reshape(DEC_BATCH, n_pages).astype(jnp.int32)
    inp['w_ada'] = nrm((DEPTH, d, 6 * d), 0.5 * d ** -0.5)
    inp['b_ada'] = nrm((DEPTH, 6 * d), 0.02)
    inp['g_pre_mix'] = gain((DEPTH, d))
    inp['g_post_mix'] = gain((DEPTH, d))
    inp['g_pre_ffn'] = gain((DEPTH, d))
    inp['g_post_ffn'] = gain((DEPTH, d))
    inp['w_in_ab'] = nrm((N_AB, d, D_IN_AB), d ** -0.5)
    inp['g_q_a'] = gain((N_AB, Q_LORA))
    inp['w_q_b'] = nrm((N_AB, Q_LORA, H_A * (NOPE_A + ROPE_A)), Q_LORA ** -0.5)
    inp['g_kv_a'] = gain((N_AB, KV_LORA))
    inp['w_kv_b'] = nrm((N_AB, KV_LORA, H_A, NOPE_A + V_A), KV_LORA ** -0.5)
    inp['w_out_ab'] = nrm((N_AB, D_CAT_AB, d), D_CAT_AB ** -0.5)
    inp['w_ffd_in'] = nrm((N_AB, d, 2 * F_DENSE), d ** -0.5)
    inp['w_ffd_out'] = nrm((N_AB, F_DENSE, d), F_DENSE ** -0.5)
    inp['w_qkv_c'] = nrm((N_C, d, D_QKV_C), d ** -0.5)
    inp['sinks_c'] = nrm((N_C, H_C), 1.0)
    inp['w_out_c'] = nrm((N_C, H_C * HEAD_DIM, d), (H_C * HEAD_DIM) ** -0.5)
    inp['w_router'] = nrm((N_C, d, N_EXPERTS), d ** -0.5)
    inp['b_router'] = nrm((N_C, N_EXPERTS), 0.01)
    inp['w_moe_in'] = nrm((N_C, N_EXPERTS, d, 2 * F_EXPERT), d ** -0.5)
    inp['w_moe_out'] = nrm((N_C, N_EXPERTS, F_EXPERT, d), F_EXPERT ** -0.5)
    return inp

def reference(x_prompt, x_sample, c_prompt, c_sample, cache_mla_ckv, cache_mla_krope, cache_b_k, cache_b_v,
              cache_c_k, cache_c_v, page_table, w_ada, b_ada, g_pre_mix, g_post_mix, g_pre_ffn, g_post_ffn,
              w_in_ab, g_q_a, w_q_b, g_kv_a, w_kv_b, w_out_ab, w_ffd_in, w_ffd_out, w_qkv_c, sinks_c, w_out_c,
              w_router, b_router, w_moe_in, w_moe_out):
    P = dict(w_ada=w_ada, b_ada=b_ada, g_pre_mix=g_pre_mix, g_post_mix=g_post_mix, g_pre_ffn=g_pre_ffn,
             g_post_ffn=g_post_ffn, w_in_ab=w_in_ab, g_q_a=g_q_a, w_q_b=w_q_b, g_kv_a=g_kv_a, w_kv_b=w_kv_b,
             w_out_ab=w_out_ab, w_ffd_in=w_ffd_in, w_ffd_out=w_ffd_out, w_qkv_c=w_qkv_c, sinks_c=sinks_c,
             w_out_c=w_out_c, w_router=w_router, b_router=b_router, w_moe_in=w_moe_in, w_moe_out=w_moe_out)
    past_len = page_table.shape[1] * PAGE_SIZE
    pos_p = jnp.arange(x_prompt.shape[1])
    pos_s = past_len + jnp.arange(x_sample.shape[1])
    y_prompt, sp = trunk(x_prompt, c_prompt, pos_p, P, None)
    past = dict(ckv=cache_mla_ckv, krope=cache_mla_krope, bk=cache_b_k, bv=cache_b_v, ck=cache_c_k,
                cv=cache_c_v, page_table=page_table, past_len=past_len)
    y_sample, ss = trunk(x_sample, c_sample, pos_s, P, past)
    return (y_prompt, y_sample, sp['ckv'], sp['krope'], sp['bk'], sp['bv'], sp['ck'], sp['cv'],
            ss['ckv'], ss['krope'], ss['bk'], ss['bv'], ss['ck'], ss['cv'])


_drawn_inputs = setup_inputs


def setup_inputs(seed=0):
    import zlib

    import numpy as np

    out = dict(_drawn_inputs(seed))
    spreads = {}
    factors = {'sinks_c': 5.94, 'g_q_a': 5.22, 'b_router': 2.938}
    for name, (base, spread) in spreads.items():
        noise = np.random.default_rng([zlib.crc32(name.encode()), seed]).standard_normal(out[name].shape)
        drawn = base * np.exp(spread * noise) if base else spread * noise
        out[name] = __import__('jax').numpy.asarray(drawn.astype(out[name].dtype))
    for name, factor in factors.items():
        out[name] = (out[name] * factor).astype(out[name].dtype)
    return out
```

```python
from contextlib import ExitStack

import numpy as np
import concourse.bass as bass
from concourse import mybir

F32 = mybir.dt.float32
I32 = mybir.dt.int32
U32 = mybir.dt.uint32
ALU = mybir.AluOpType
ACT = mybir.ActivationFunctionType
AX_X = mybir.AxisListType.X

D, P, KD = 1024, 128, 8
NTP, NB, TS = 256, 8, 4
NS = NB * TS
NT = NTP + NS
TILES = [(0, 128), (128, 128), (256, 32)]
PAST, PAGE = 1024, 128
NPG = PAST // PAGE
QL, KV, NOPE, RA, HA, HD = 384, 256, 64, 32, 8, 64
HC, GC = 16, 4
FD, NE, FE = 2816, 8, 3584
MLA_SCALE = float(NOPE + RA) ** -0.5
HD_SCALE = float(HD) ** -0.5
EPS, NEG = 1e-6, -1e30
THETA = 500000.0
CAP = 96
MAXPASS = -(-NT // CAP)

SLOT = 4096
NSLOT = 4
OSLOT = 14 * 256
BCOLS = 5 * 128

C_ID, C_ONE, C_UP, C_IC, C_I8 = 0, 128, 256, 384, 384 + CAP
C_RA = C_I8 + 8
C_RB = C_RA + 3 * 64
C_CM = C_RB + 3 * 32
C_EPS = C_CM + 128
NCST = C_EPS + 1
M_A, M_B, M_C, M_SB, M_NA, M_NB = 0, 384, 768, 1152, 1152 + BCOLS, 1152 + BCOLS + 256
NMSK = M_NB + 256


def shape_constants():
    f = np.float32
    c = np.zeros((P, NCST), f)
    c[:, C_ID:C_ID + 128] = np.eye(P)
    c[:, C_ONE:C_ONE + 128] = 1
    c[:, C_UP:C_UP + 128] = np.triu(np.ones((P, P)), 1)
    c[:, C_IC:C_IC + CAP] = np.arange(CAP)
    c[:, C_I8:C_I8 + 8] = np.arange(8)
    c[:, C_EPS] = EPS
    pos = [np.arange(128), 128 + np.arange(128), PAST + np.arange(128) % TS]
    for half, at in ((RA // 2, C_RA), (HD // 8, C_RB)):
        inv = f(THETA) ** (-np.arange(half, dtype=f) / f(half))
        for t in range(3):
            ang = pos[t].astype(f)[:, None] * inv.astype(f)[None, :]
            cos, sin = np.cos(ang).astype(f), np.sin(ang).astype(f)
            c[:, at + t * 4 * half:at + (t + 1) * 4 * half] = np.concatenate([cos, cos, -sin, sin], 1)
    r = np.arange(64) % TS
    c[:64, C_CM:C_CM + 128] = np.where(np.arange(128)[None] > r[:, None], 0, NEG)

    def count(dist):
        n = np.zeros(dist.shape)
        for w, d in ((128, 1), (512, 4), (2048, 16)):
            n += (dist >= 0) & (dist <= w) & (dist % d == 0)
        return np.where(n > 0, np.log(np.maximum(n, 1)), NEG)

    m = np.zeros((P, NMSK), f)
    q, k = np.arange(128)[:, None], np.arange(128)[None]
    dist = np.concatenate([q - k, q + 128 - k, q - k], 1)
    m[:, M_A:M_A + 384] = np.where(dist >= 0, 0, NEG)
    m[:, M_B:M_B + 384] = count(dist)
    m[:, M_C:M_C + 384] = np.where((dist >= 0) & (dist < 128), 0, NEG)
    p = np.arange(128)
    keys = np.concatenate([p // 4 * 16 + p % 4] + [512 + 4 * p + i for i in range(4)])
    t = (np.arange(32) % TS)[:, None]
    m[:32, M_SB:M_SB + BCOLS] = count(PAST + t - keys[None])
    kb, kt = np.arange(NS)[None] // TS, np.arange(NS)[None] % TS
    for b in range(NB):
        m[:64, M_NA + 32 * b:M_NA + 32 * b + 32] = np.where((kb == b) & (kt <= r[:, None]), 0, NEG)
        m[:32, M_NB + 32 * b:M_NB + 32 * b + 32] = np.where(kb == b, count(t - kt), NEG)
    return c, m


def ring_plan():
    plan = [("ada0", j, 1) for j in range(12)]
    plan += [("in_ab", j, 1) for j in range(5)]
    plan += [("q_b", 0, 1)]
    for i in range(8):
        plan += [("bk", i, 2), ("bv", i, 2), ("mla", i, 2 * NPG)]
    plan += [("out_ab", j, 1) for j in range(2)]
    plan += [("ffd_in", j, 2) for j in range(11)]
    plan += [("ffd_out", j, 1) for j in range(8)]
    plan += [("ada1", j, 1) for j in range(12)]
    plan += [("qkv_c", j, 1) for j in range(3)]
    plan += [("c_cache", 0, 2)]
    plan += [("out_c", j, 4) for j in range(2)]
    at, arrived, total = {}, {}, [0] * NSLOT
    for n, (kind, j, dmas) in enumerate(plan):
        total[n % NSLOT] += 16 * dmas
        at[(kind, j)] = n
        arrived[n] = total[n % NSLOT]
    return plan, at, arrived, total


def units_of_layer0():
    out = []
    for i in range(8):
        out += [("Bs", i), ("Bp", i), ("As", i), ("Ap", i)]
    return out


def units_of_layer1():
    out = []
    for i in range(8):
        out += [("Cs", i), ("Cp", 2 * i), ("Cp", 2 * i + 1)]
    return out


def build(nc, t_in, t_out):
    plan, at, arrived, ring_total = ring_plan()
    NPLAN = len(plan)
    units = units_of_layer0() + units_of_layer1()
    NU0 = len(units_of_layer0())
    NU = len(units)
    rows_of = {"Ap": 128, "Bp": 128, "Cp": 128, "As": 32, "Bs": 32, "Cs": 64}
    ktiles_of = {"As": NPG, "Bs": 5, "Cs": 1}

    ctx = ExitStack()
    with ctx:
        def sb(name, shape, dt=F32):
            return ctx.enter_context(nc.sbuf_tensor(name, shape, dt))

        def sem(name):
            return ctx.enter_context(nc.semaphore(name))

        ring = sb("ring", [P, NSLOT, SLOT])
        mix = sb("mix", [P, 4 * OSLOT])
        xT = sb("xT", [P, KD, NT])
        work = sb("work", [P, 3 * KD * NT])
        z = sb("z", [P, 6624])
        o_or_q = sb("o_or_q", [P, KD * NT])
        rinv = sb("rinv", [P, NT])
        rstd = sb("rstd", [P, NT])
        mod = sb("mod", [P, 2, 48, 9])
        coef = sb("coef", [P, 4, KD, 9])
        cst = sb("cst", [P, NCST])
        gqkv = sb("gqkv", [P, QL + KV])
        vecT = sb("vecT", [P, 160])
        csT = sb("csT", [P, KD, 9])
        sinks = sb("sinks", [P, HC])
        nsinks = sb("nsinks", [P, HC])
        sinkr = sb("sinkr", [64, 1])
        nsinkr = sb("nsinkr", [64, 1])
        brout = sb("brout", [P, NE])
        wrout = sb("wrout", [P, KD, NE])
        ptab = sb("ptab", [1, NB * NPG], I32)
        nmax = sb("nmax", [P, 2, 2])
        lsum = sb("lsum", [P, 2, 4])
        rl = sb("rl", [P, 2, 2])
        ss = sb("ss", [P, 3, 6])

        hT = work[:, 0:2304].rearrange("p (k n) -> p k n", k=KD)
        fT = work[:, 2304:4608].rearrange("p (k n) -> p k n", k=KD)
        sq = work[:, 4608:6912].rearrange("p (k n) -> p k n", k=KD)
        qhT = work[0:96, 0:2304].rearrange("p (h n) -> p h n", h=HA)
        qlT = work[:, 2304:6912].rearrange("p (c h n) -> p c h n", c=2, h=HA)
        xtok = z[:, 0:3072].rearrange("p (t n) -> p t n", t=3)
        ctok = z[0:9, 3072:4096]
        cstok = z[0:9, 4096:5120]
        vecA = z[0:96, 5120:5248]
        vecB = z[0:64, 5248:5376]
        z_qk = z[:, 0:3072].rearrange("p (t n) -> p t n", t=3)
        z_v = z[:, 3072:4608].rearrange("p (t n) -> p t n", t=3)
        z_ckv = z[:, 4608:5376].rearrange("p (t n) -> p t n", t=3)
        z_kr = z[:, 5376:5472 + 192].rearrange("p (t n) -> p t n", t=3)
        z_qa = o_or_q[:, 0:1152].rearrange("p (t n) -> p t n", t=3)
        rtmp = o_or_q[:, 1152:2304]
        rtmp2 = z[:, 5664:6624]
        qls = z[:, 5664:6176].rearrange("p (c b n) -> p c b n", c=2, b=NB)
        qhs = z[:, 6176:6432].rearrange("p (b n) -> p b n", b=NB)
        z2 = o_or_q[:, :].rearrange("p (t n) -> p t n", t=3)
        z_c = z[:, 0:4608].rearrange("p (t n) -> p t n", t=3)
        oT = o_or_q[:, :].rearrange("p (k n) -> p k n", k=KD)
        kcT = z[:, 0:3072]
        kcT_c = z[:, 5120:5376].rearrange("p (j n) -> p j n", j=2)
        actd = z[:, 0:22 * NT].rearrange("p (f n) -> p f n", f=22)

        m_at = [0]

        def mixview(n):
            m_at[0] += n
            return mix[:, m_at[0] - n:m_at[0]]

        msk = mixview(NMSK)
        qkT = mixview(4032)
        qT0 = qkT[:, 0:1152].rearrange("p (k n) -> p k n", k=4)
        kT0 = qkT[:, 1152:2304].rearrange("p (k n) -> p k n", k=4)
        ckvT = qkT[:, 2304:2880].rearrange("p (k n) -> p k n", k=2)
        qnT = qkT[:, 2880:3744].rearrange("p (k n) -> p k n", k=3)
        krT = qkT[:, 3744:4032]
        qT1 = qkT[:, 0:2304].rearrange("p (k n) -> p k n", k=8)
        kT1 = qkT[:, 2304:2880].rearrange("p (k n) -> p k n", k=2)
        wukT = mixview(2048).rearrange("p (h c) -> p h c", h=HA)
        kvb = mixview(2048).rearrange("p (c n) -> p c n", c=2)
        scores = mixview(2112).rearrange("p (b n) -> p b n", b=2)
        probsT = mixview(768).rearrange("p (b n) -> p b n", b=2)
        qbd = mixview(1024)
        qbd0 = qbd.rearrange("p (b j n) -> p b j n", b=NB, j=4)
        qbd1 = qbd.rearrange("p (b j n) -> p b j n", b=NB, j=2)
        oring = mix[:, 0:4 * OSLOT].rearrange("p (s n) -> p s n", s=4)

        htok = z[:, 0:3072].rearrange("p (t n) -> p t n", t=3)
        acte = z[:, 3072:3072 + 28 * CAP].rearrange("p (f n) -> p f n", f=28)
        hsel = z[:, 3072 + 28 * CAP:3072 + 36 * CAP].rearrange("p (k n) -> p k n", k=KD)
        oeT = work[:, 4608:4608 + KD * CAP].rearrange("p (k n) -> p k n", k=KD)
        otok = work[0:CAP, 4608 + KD * CAP:4608 + KD * CAP + D]
        pick = o_or_q[:, 0:3 * CAP].rearrange("p (t n) -> p t n", t=3)
        pickg = o_or_q[:, 288:288 + 3 * CAP].rearrange("p (t n) -> p t n", t=3)
        putT = o_or_q[0:CAP, 576:576 + 2 * NT].rearrange("p (b n) -> p b n", b=2)
        sil = o_or_q[:, 1152:1152 + 4 * CAP].rearrange("p (b f n) -> p b f n", b=2, f=2)
        rt = o_or_q[:, 1536:2304]
        logit = rt[:, 0:24].rearrange("p (t n) -> p t n", t=3)
        top = rt[:, 24:48].rearrange("p (t n) -> p t n", t=3)
        topi = rt[:, 48:72].bitcast(U32).rearrange("p (t n) -> p t n", t=3)
        topf = rt[:, 72:78].rearrange("p (t n) -> p t n", t=3)
        gate = rt[:, 84:96].rearrange("p (t n) -> p t n", t=3)
        oh = rt[:, 96:144].rearrange("p (w t n) -> p w t n", w=2, t=3)
        mask = rt[:, 144:168].rearrange("p (t n) -> p t n", t=3)
        gates = rt[:, 168:195].rearrange("p (n t) -> p n t", t=3)
        posm = rt[:, 195:222].rearrange("p (n t) -> p n t", t=3)
        cur = rt[:, 222:228].rearrange("p (w t) -> p w t", w=2)
        pm_t = rt[:, 232:256].rearrange("p (t n) -> p t n", t=3)
        cnt = rt[:, 256:264]
        passes = rt[:, 265:266]
        passes_i = rt[:, 267:268].bitcast(I32)
        silu_d = z[:, 22 * NT:23 * NT]

        ps = ctx.enter_context(nc.psum_tensor("ps", [P, 8 * 512], F32))

        def bank(i, n=512, at_=0, rows=P):
            return ps[0:rows, 512 * i + at_:512 * i + at_ + n]

        ident = cst[:, C_ID:C_ID + 128]
        ones = cst[:, C_ONE:C_ONE + 128]

        s_in = [sem(f"ring_in{i}") for i in range(NSLOT)]
        s_ld, s_ldm = sem("loaded"), sem("loaded_vectors")
        s_xload = sem("x_loaded")
        s_pt = sem("page_table_loaded")
        x_tp, x_cp = sem("x_transposed"), sem("x_copied")
        c_silu, c_tp, c_cp = sem("c_silu"), sem("c_transposed"), sem("c_copied")
        sq_done, stat_done, std_done = sem("squares_done"), sem("sums_done"), sem("std_done")
        h_done, x_upd = sem("h_done"), sem("x_updated")
        ada_done = sem("ada_done")
        z_done, z_cp, z_rdy = sem("z_done"), sem("z_copied"), sem("z_ready")
        t_done, t_cp = sem("mixer_transposes_done"), sem("mixer_transposes_copied")
        q_done, q_cp, q_rope = sem("q_done"), sem("q_copied"), sem("q_roped")
        qn_rdy = sem("qn_ready")
        bd_rdy = sem("block_diagonal_ready")
        kt_tp = [sem("cache_transposed_even"), sem("cache_transposed_odd")]
        kt_cp = [sem("cache_copied_even"), sem("cache_copied_odd")]
        sc_done, sc_cp, mx_done, ex_done, pr_done = (sem("scores_done"), sem("scores_copied"), sem("max_done"),
                                                     sem("exp_done"), sem("probs_done"))
        pt_tp, pt_cp, pv_done, pv_cp = (sem("probs_transposed"), sem("probsT_copied"), sem("pv_done"),
                                        sem("pv_copied"))
        oa_done, oa_cp = sem("oa_done"), sem("oa_copied")
        f_done, f_cp = sem("f_done"), sem("f_copied")
        gu_done, si_done, act_done = sem("gate_up_done"), sem("silu_done"), sem("act_done")
        y_tp, y_cp, s_out = sem("y_transposed"), sem("y_copied"), sem("stored")
        s_out0 = sem("stored_layer0")
        s_out1 = sem("stored_layer1")
        chain_v, chain_a = sem("vector_chain"), sem("scalar_chain")
        htok_tp, htok_cp, lg_done, lg_cp = sem("htok_transposed"), sem("htok_copied"), sem("logits_done"), sem("logits_copied")
        ge_done, msk_done, pos_done, pass_rdy = sem("gate_exp_done"), sem("route_masks_done"), sem("positions_done"), sem("passes_ready")
        e_gu, e_si, e_act = sem("e_gate_up_done"), sem("e_silu_done"), sem("e_act_done")
        e_in, e_used = [sem(f"oring_in{i}") for i in range(4)], sem("oring_used")
        e_ocp = sem("e_out_copied")
        e_tp, e_tcp = sem("e_out_transposed"), sem("e_out_tok_copied")
        e_cb, e_add = sem("combine_done"), sem("combine_added")
        e_pick, e_gat, e_gcpA, e_gcpV = sem("pick_ready"), sem("gathered"), sem("gather_copied_act"), sem("gather_copied_vec")
        e_ptp, e_pcp = sem("put_transposed"), sem("put_copied")
        chain_e = sem("vector_chain_experts")

        def copy_keys(copy, kind, i, b):
            if kind == "As":
                copy(kcT[:, 0:2048].rearrange("p (c n) -> p c n", c=2)[:, :, 128 * i:128 * i + 128],
                     bank(b, 256).rearrange("p (c n) -> p c n", c=2))
                return copy(kcT[64:96, 2048 + 128 * i:2176 + 128 * i], ps[64:96, 512 * b + 256:512 * b + 384])
            if kind == "Bs":
                return copy(kcT[:, 0:2560].rearrange("p (j n) -> p j n", j=4)[:, :, 128 * i:128 * i + 128],
                            bank(b).rearrange("p (j n) -> p j n", j=4))
            return copy(kcT_c, bank(b, 256).rearrange("p (j n) -> p j n", j=2))

        block = ctx.enter_context(nc.Block())

        unit_at = {unit: u for u, unit in enumerate(units)}
        used = []
        for kind, j, _n in plan:
            used.append({
                "ada0": (ada_done, j + 1), "ada1": (ada_done, 13 + j), "in_ab": (z_done, 3 * (j + 1)), "q_b": (q_done, 6),
                "bk": (sc_done, unit_at.get(("Bs", j), 0) + 1),
                "bv": (pv_done, unit_at.get(("Bs", j), 0) + 1),
                "mla": (pv_done, unit_at.get(("As", j), 0) + 1),
                "out_ab": (f_done, 4 * (j + 1)), "ffd_in": (gu_done, 2 * (j + 1)), "ffd_out": (f_done, 9 + j),
                "qkv_c": (z_done, 18 + 3 * j), "c_cache": (pv_done, unit_at["Cs", NB - 1] + 1), "out_c": (f_done, 20 + 4 * j),
            }[kind])

        def slot_of(kind, j):
            return at[(kind, j)] % NSLOT

        def chunk(kind, j, off, n):
            return ring[:, slot_of(kind, j), off:off + n]

        @block.sync
        def _(sp):
            sp.dma_start(xtok[:, 0:2, :], t_in["x_prompt"][0].rearrange("(t p) d -> p t d", p=P)).then_inc(s_xload, 16)
            sp.dma_start(cst[:, :], t_in["cst"][:, :]).then_inc(s_xload, 16)
            sp.dma_start(xtok[0:NS, 2, :], t_in["x_sample"].rearrange("b t d -> (b t) d")).then_inc(s_xload, 16)
            sp.dma_start(ctok[0:1, :], t_in["c_prompt"]).then_inc(s_xload, 16)
            sp.dma_start(ctok[1:9, :], t_in["c_sample"]).then_inc(s_xload, 16)
            sp.dma_start(vecA, t_in["b_ada"].rearrange("l (m p) -> (l m) p", p=P)).then_inc(s_ldm, 16)
            for i, name in enumerate(("g_pre_mix", "g_post_mix", "g_pre_ffn", "g_post_ffn")):
                sp.dma_start(vecB[16 * i:16 * i + 16, :], t_in[name].rearrange("l (m p) -> (l m) p", p=P)).then_inc(s_ldm, 16)

            def free(n):
                if n >= NSLOT:
                    sp.wait_ge(*used[n - NSLOT])

            def ada(l):
                w = t_in["w_ada"][l].rearrange("(k p) m -> p k m", p=P)
                n0 = at[(f"ada{l}", 0)]
                for j in range(4):
                    free(n0 + j)
                    sp.dma_start(chunk(f"ada{l}", j, 0, 4096).rearrange("p (k m) -> p k m", k=KD),
                                 w[:, :, 512 * j:512 * j + 512]).then_inc(s_in[(n0 + j) % NSLOT], 16)
                with sp.Fori(1, 3) as i:
                    for q in range(4):
                        sp.wait_ge(ada_done, 4 * i + (12 * l + q - 3))
                        sp.dma_start(ring[:, (n0 + q) % NSLOT, :].rearrange("p (k m) -> p k m", k=KD),
                                     w[:, :, bass.ds(2048 * i + 512 * q, 512)]).then_inc(s_in[(n0 + q) % NSLOT], 16)

            def put(kind, j):
                n = at[(kind, j)]
                free(n)
                s = s_in[n % NSLOT]
                if kind == "in_ab":
                    c0, w = ((0, 384), (384, 288), (672, 512), (1184, 512), (1696, 512))[j]
                    sp.dma_start(chunk(kind, j, 0, 8 * w).rearrange("p (k m) -> p k m", k=KD),
                                 t_in["w_in_ab"][0].rearrange("(k p) m -> p k m", p=P)[:, :, c0:c0 + w]).then_inc(s, 16)
                elif kind == "q_b":
                    sp.dma_start(chunk(kind, j, 0, 2304).rearrange("p (k m) -> p k m", k=3),
                                 t_in["w_q_b"][0].rearrange("(k p) m -> p k m", p=P)).then_inc(s, 16)
                elif kind in ("bk", "bv"):
                    src = t_in["cache_b_k" if kind == "bk" else "cache_b_v"][0, j].rearrange("s h d -> s (h d)")
                    sp.dma_start(chunk(kind, j, 0, 512),
                                 src[0:512, :].rearrange("(g r) n -> g r n", r=16)[:, 0:4, :]).then_inc(s, 16)
                    sp.dma_start(chunk(kind, j, 512, 2048), src[512:1024, :].rearrange("(p i) n -> p (i n)", i=4)).then_inc(s, 16)
                elif kind == "mla":
                    ck, kr = t_in["cache_mla_ckv"][0], t_in["cache_mla_krope"][0]
                    with sp.Fori(0, NPG) as i:
                        page = sp.value_load(ptab[0:1, bass.ds(NPG * j + i, 1)], min_val=0, max_val=ck.shape[0] - 1)
                        sp.dma_start(ring[:, n % NSLOT, bass.ds(256 * i, 256)],
                                     ck[bass.ds(page, 1), :, :].rearrange("a s c -> (a s) c")).then_inc(s, 16)
                        sp.dma_start(ring[:, n % NSLOT, bass.ds(2048 + 64 + 96 * i, 32)],
                                     kr[bass.ds(page, 1), :, :].rearrange("a s c -> (a s) c")).then_inc(s, 16)
                elif kind == "out_ab":
                    sp.dma_start(chunk(kind, j, 0, 4096).rearrange("p (k m) -> p k m", k=KD),
                                 t_in["w_out_ab"][0].rearrange("(k p) m -> p k m", p=P)[:, :, 512 * j:512 * j + 512]).then_inc(s, 16)
                elif kind == "ffd_in":
                    w = t_in["w_ffd_in"][0].rearrange("(k p) (g m) -> p k g m", p=P, g=2)
                    for g in range(2):
                        sp.dma_start(chunk(kind, j, 2048 * g, 2048).rearrange("p (k m) -> p k m", k=KD),
                                     w[:, :, g, 256 * j:256 * j + 256]).then_inc(s, 16)
                elif kind == "ffd_out":
                    sp.dma_start(chunk(kind, j, 0, 2816).rearrange("p (f m) -> p f m", f=22),
                                 t_in["w_ffd_out"][0].rearrange("(f p) m -> p f m", p=P)[:, :, 128 * j:128 * j + 128]).then_inc(s, 16)
                elif kind == "qkv_c":
                    sp.dma_start(chunk(kind, j, 0, 4096).rearrange("p (k m) -> p k m", k=KD),
                                 t_in["w_qkv_c"][0].rearrange("(k p) m -> p k m", p=P)[:, :, 512 * j:512 * j + 512]).then_inc(s, 16)
                elif kind == "c_cache":
                    for w, name in enumerate(("cache_c_k", "cache_c_v")):
                        sp.dma_start(chunk(kind, j, 2048 * w, 2048).rearrange("p (b n) -> p b n", b=NB),
                                     t_in[name][0].rearrange("b s h d -> s b (h d)")).then_inc(s, 16)
                elif kind == "out_c":
                    w = t_in["w_out_c"][0].rearrange("(b r d) m -> b d r m", r=4, d=64)
                    for a in range(2):
                        for jj in range(2):
                            sp.dma_start(ring[64 * a:64 * a + 64, n % NSLOT, 2048 * jj:2048 * jj + 2048].rearrange("p (r m) -> p r m", r=4),
                                         w[2 * jj + a, :, :, 512 * j:512 * j + 512]).then_inc(s, 16)

            ada(0)
            sp.wait_ge(s_pt, 16)
            for kind, j, _n in plan[12:at[("ada1", 0)]]:
                put(kind, j)
            ada(1)
            for kind, j, _n in plan[at[("ada1", 0)] + 12:]:
                put(kind, j)

            wi = t_in["w_moe_in"][0].rearrange("e (k p) m -> p e k m", p=P)
            wo = t_in["w_moe_out"][0].rearrange("e (f p) m -> p e f m", p=P)

            def expert_loads(it, i, half):
                e = 2 * i + half

                def put_in(j):
                    c = 14 * half + j
                    sl = (NPLAN + c) % NSLOT
                    sp.wait_ge(e_gu, 28 * it + (c + 1))
                    for g in range(2):
                        src = wi[:, bass.ds(e, 1), :, g * FE + 256 * j:g * FE + 256 * j + 256].rearrange("p a k m -> p (a k) m")
                        sp.dma_start(ring[:, sl, 2048 * g:2048 * g + 2048].rearrange("p (k m) -> p k m", k=KD),
                                     src).then_inc(s_in[sl], 16)

                def put_out(q):
                    sp.wait_ge(e_used, 16 * it + (8 * half + q + 1))
                    src = wo[:, bass.ds(e, 1), 14 * (q % 2):14 * (q % 2) + 14, 256 * (q // 2):256 * (q // 2) + 256]
                    sp.dma_start(oring[:, q % 4, :].rearrange("p (f m) -> p f m", f=14),
                                 src.rearrange("p a f m -> p (a f) m")).then_inc(e_in[q % 4], 16)

                for j in range(4):
                    put_in(j)
                for q in range(4):
                    put_out(q)
                for j in range(4, 14):
                    put_in(j)
                for q in range(4, 8):
                    put_out(q)

            def pass_body(it0):
                with sp.Fori(0, NE // 2) as i:
                    for half in range(2):
                        expert_loads(it0 + i, i, half)

            pass_body(0)
            sp.wait_ge(pass_rdy, 1)
            npass = sp.value_load(passes_i[0:1, :], min_val=1, max_val=MAXPASS)
            with sp.If(npass > 1):
                with sp.Fori(1, npass) as p_:
                    pass_body(4 * p_)

        @block.gpsimd
        def _(gp):
            gp.dma_start(ptab[:, :], t_in["page_table"].rearrange("b g -> (b g)").rearrange("(a n) -> a n", a=1)).then_inc(s_pt, 16)
            gp.dma_start(gqkv[:, 0:QL], t_in["g_q_a"].broadcast_to([P, QL])).then_inc(s_ld, 16)
            gp.dma_start(gqkv[:, QL:QL + KV], t_in["g_kv_a"].broadcast_to([P, KV])).then_inc(s_ld, 16)
            gp.dma_start(sinks[:, :], t_in["sinks_c"].broadcast_to([P, HC])).then_inc(s_ld, 16)
            gp.dma_start(brout[:, :], t_in["b_router"].broadcast_to([P, NE])).then_inc(s_ld, 16)
            with nc.allow_non_contiguous_dma(reason="64 single values"):
                gp.dma_start(sinkr[:, :], t_in["sinks_c"].rearrange("a (h o) -> h a o", o=1).broadcast_to([HC, TS, 1])).then_inc(s_ld, 16)
            gp.dma_start(wrout[:, :, :], t_in["w_router"][0].rearrange("(k p) e -> p k e", p=P)).then_inc(s_ld, 16)
            gp.dma_start(kvb[:, :, :], t_in["w_kv_b"][0].rearrange("(c p) h n -> p c (h n)", p=P)).then_inc(s_ld, 16)
            gp.dma_start(msk, t_in["msk"][:, :]).then_inc(s_ld, 16)

            def store(dst, src, s):
                gp.dma_start(dst, src).then_inc(s, 16)

            gp.wait_ge(z_rdy, 5)
            gp.wait_ge(z_cp, 15)
            store(t_out["p_ckv"].rearrange("(t p) c -> p t c", p=P), z_ckv[:, 0:2, :], s_out0)
            store(t_out["p_kr"].rearrange("(t p) c -> p t c", p=P), z_kr[:, 0:2, 64:96], s_out0)
            store(t_out["p_bk"].rearrange("(t p) c -> p t c", p=P), z_qk[:, 0:2, 512:1024], s_out0)
            store(t_out["p_bv"].rearrange("(t p) c -> p t c", p=P), z_v[:, 0:2, :], s_out0)
            store(t_out["s_ckv"][:, :], z_ckv[0:NS, 2, :], s_out0)
            store(t_out["s_kr"][:, :], z_kr[0:NS, 2, 64:96], s_out0)
            store(t_out["s_bk"][:, :], z_qk[0:NS, 2, 512:1024], s_out0)
            store(t_out["s_bv"][:, :], z_v[0:NS, 2, :], s_out0)
            gp.wait_ge(z_rdy, 8)
            gp.wait_ge(z_cp, 24)
            store(t_out["p_ck"][:, :], z_c[:, 1, 1024:1280], s_out1)
            store(t_out["p_cv"][:, :], z_c[:, 1, 1280:1536], s_out1)
            store(t_out["s_ck"][:, :], z_c[0:NS, 2, 1024:1280], s_out1)
            store(t_out["s_cv"][:, :], z_c[0:NS, 2, 1280:1536], s_out1)
            gp.wait_ge(y_cp, 6)
            store(t_out["y_prompt"].rearrange("(t p) d -> p t d", p=P), htok[:, 0:2, :], s_out)
            store(t_out["y_sample"][:, :], htok[0:NS, 2, :], s_out)
            gp.wait_ge(s_out0, 8 * 16)
            gp.wait_ge(s_out1, 4 * 16)
            gp.wait_ge(s_out, 2 * 16)

        @block.tensor
        def _(pe):
            mm, tp = nc.tensor.matmul, nc.tensor.transpose

            def landed(kind, j):
                n = at[(kind, j)]
                pe.wait_ge(s_in[n % NSLOT], arrived[n])

            def sums(n):
                for k in range(KD):
                    pe.wait_ge(sq_done, 8 * n + k + 1)
                    last = mm(bank(7, NT), ones, sq[:, k, :], start=(k == 0), stop=(k == KD - 1))
                last.then_inc(stat_done, 1)

            def ada(l):
                n0 = at[(f"ada{l}", 0)]
                base = [arrived[n0 + q] for q in range(4)]
                with pe.Fori(0, 3) as i:
                    for q in range(4):
                        sl = (n0 + q) % NSLOT
                        pe.wait_ge(s_in[sl], 16 * i + base[q])
                        w = ring[:, sl, :].rearrange("p (k m) -> p k m", k=KD)
                        for m in range(4):
                            for k in range(KD):
                                last = mm(ps[:, bass.ds(512 * 6 + 144 * i + (36 * q + 9 * m), 9)], w[:, k, 128 * m:128 * m + 128],
                                          csT[:, k, :], start=(k == 0), stop=(k == KD - 1))
                        last.then_inc(ada_done, 1)

            def linear_out(L, kind, per, nk, rhs):
                for k in range(KD):
                    j, m = k // per, k % per
                    if m == 0:
                        landed(kind, j)
                    if L or k >= 2:
                        pe.wait_ge(f_cp, 8 * L + k - 1)
                    w = chunk(kind, j, 0, nk * per * 128).rearrange("p (f m) -> p f m", f=nk)
                    for f in range(nk):
                        last = mm(bank(4 + k % 2, NT), w[:, f, 128 * m:128 * m + 128], rhs[:, f, :],
                                  start=(f == 0), stop=(f == nk - 1))
                    last.then_inc(f_done, 1)

            pe.wait_ge(s_xload, 5 * 16)
            for k in range(KD):
                if k >= 2:
                    pe.wait_ge(x_cp, k - 1)
                for t, (t0, n) in enumerate(TILES):
                    last = tp(bank(k % 2, n, t0), xtok[0:n, t, 128 * k:128 * k + 128], ident[0:n, 0:n])
                last.then_inc(x_tp, 1)
            pe.wait_ge(c_silu, 1)
            for k in range(KD):
                last = tp(bank(2, 9, 9 * k), cstok[:, 128 * k:128 * k + 128], ident[0:9, 0:9])
            pe.wait_ge(s_ldm, 5 * 16)
            tp(bank(3, 96), vecA, ident[0:96, 0:96])
            tp(bank(3, 64, 96), vecB, ident[0:64, 0:64]).then_inc(c_tp, 1)
            sums(0)
            pe.wait_ge(c_cp, 1)
            ada(0)

            nz = 0
            pe.wait_ge(s_ld, 8 * 16)
            pe.wait_ge(h_done, 9)
            for j, w in enumerate((384, 288, 512, 512, 512)):
                landed("in_ab", j)
                wt = chunk("in_ab", j, 0, 8 * w).rearrange("p (k m) -> p k m", k=KD)
                for t, (t0, n) in enumerate(TILES):
                    if nz >= 4:
                        pe.wait_ge(z_cp, nz - 3)
                    for k in range(KD):
                        last = mm(bank(nz % 4, w, 0, n), hT[:, k, t0:t0 + n], wt[:, k, :], start=(k == 0), stop=(k == KD - 1))
                    last.then_inc(z_done, 1)
                    nz += 1
            nt = 0

            def t_bank():
                if nt >= 2:
                    pe.wait_ge(t_cp, nt - 1)
                return 4 + nt % 2

            for hp in range(4):
                b = t_bank()
                for q in range(4):
                    h, c = 2 * hp + q // 2, q % 2
                    last = tp(bank(b, 128, 128 * q, 64), kvb[:, c, 128 * h:128 * h + 64], ident)
                last.then_inc(t_done, 1)
                nt += 1

            def tp_tiles(src, m):
                nonlocal nt
                b = t_bank()
                for t, (t0, n) in enumerate(TILES):
                    last = tp(bank(b, n, t0, m), src(t, n), ident[0:n, 0:n])
                last.then_inc(t_done, 1)
                nt += 1

            pe.wait_ge(z_rdy, 1)
            for k in range(3):
                tp_tiles(lambda t, n: z_qa[0:n, t, 128 * k:128 * k + 128], 128)
            pe.wait_ge(z_rdy, 2)
            for k in range(2):
                tp_tiles(lambda t, n: z_ckv[0:n, t, 128 * k:128 * k + 128], 128)
            tp_tiles(lambda t, n: z_kr[0:n, t, :], 96)
            landed("q_b", 0)
            pe.wait_ge(t_cp, 7)
            wt = chunk("q_b", 0, 0, 2304).rearrange("p (k m) -> p k m", k=3)
            for t, (t0, n) in enumerate(TILES):
                for hh in range(2):
                    i = 2 * t + hh
                    pe.wait_ge(z_cp, 15)
                    if i >= 4:
                        pe.wait_ge(q_cp, i - 3)
                    for k in range(3):
                        last = mm(bank(i % 4, 384, 0, n), qnT[:, k, t0:t0 + n], wt[:, k, 384 * hh:384 * hh + 384],
                                  start=(k == 0), stop=(k == 2))
                    last.then_inc(q_done, 1)
            pe.wait_ge(z_rdy, 5)
            for k in range(8):
                tp_tiles(lambda t, n: z_qk[0:n, t, 128 * k:128 * k + 128], 128)
            pe.wait_ge(q_rope, 3)
            for h in range(HA):
                tp_tiles(lambda t, n: z2[0:n, t, 96 * h:96 * h + 96], 96)
            pe.wait_ge(t_cp, nt)
            for h in range(HA):
                for c in range(2):
                    b = t_bank()
                    mm(bank(b, NT), wukT[0:64, h, 128 * c:128 * c + 128], qhT[0:64, h, :], start=True, stop=True).then_inc(t_done, 1)
                    nt += 1
            pe.wait_ge(t_cp, nt)
            pe.wait_ge(bd_rdy, 1)
            kt_n = [0, 0]

            def cache_tiles(u):
                kind, b = units[u]
                if kind not in ktiles_of:
                    return
                if kind == "As":
                    landed("mla", b)
                elif kind == "Bs":
                    landed("bk", b)
                elif b == 0:
                    landed("c_cache", 0)
                for i in range(ktiles_of[kind]):
                    par = i % 2
                    bk = 7 - par
                    if kt_n[par]:
                        pe.wait_ge(kt_cp[par], kt_n[par])
                    if kind == "As":
                        for c in range(2):
                            tp(bank(bk, 128, 128 * c), chunk("mla", b, 256 * i + 128 * c, 128), ident)
                        last = tp(bank(bk, 128, 256, 96), chunk("mla", b, 2048 + 96 * i, 96), ident)
                    elif kind == "Bs":
                        for j in range(4):
                            last = tp(bank(bk, 128, 128 * j), chunk("bk", b, 512 * i + 128 * j, 128), ident)
                    else:
                        for j in range(2):
                            last = tp(bank(bk, 128, 128 * j), chunk("c_cache", 0, 256 * b + 128 * j, 128), ident)
                    last.then_inc(kt_tp[par], 1)
                    kt_n[par] += 1
                for par in range(2):
                    if kt_n[par]:
                        pe.wait_ge(kt_cp[par], kt_n[par])

            def unit_scores(u):
                kind, i = units[u]
                if u:
                    pe.wait_ge(sc_cp, u)
                if kind in ("Ap", "Bp", "Cp"):
                    for qt, (c0, nk) in enumerate(((0, 128), (128, 256))):
                        q0 = 128 * qt
                        out = bank(0, nk, c0)
                        if kind == "Ap":
                            mm(out, qlT[:, 0, i, q0:q0 + 128], ckvT[:, 0, 0:nk], start=True, stop=False)
                            mm(out, qlT[:, 1, i, q0:q0 + 128], ckvT[:, 1, 0:nk], start=False, stop=False)
                            last = mm(out, qhT[64:96, i, q0:q0 + 128], krT[64:96, 0:nk], start=False, stop=True)
                        elif kind == "Bp":
                            r = 64 * (i % 2)
                            last = mm(out, qT0[r:r + 64, i // 2, q0:q0 + 128], kT0[r:r + 64, i // 2, 0:nk], start=True, stop=True)
                        else:
                            g = i // 4
                            r = 64 * (g % 2)
                            last = mm(out, qT1[r:r + 64, 4 * (g // 2) + i % 4, q0:q0 + 128], kT1[r:r + 64, g // 2, 0:nk],
                                      start=True, stop=True)
                elif kind == "As":
                    keys = kcT[:, 0:2048].rearrange("p (c n) -> p c n", c=2)
                    kr = kcT[64:96, 2048:3072]
                    parts = [(0, 512, keys, kr, 0), (1, 512, keys, kr, 512), (2, 32, ckvT, krT[64:96, :], NTP)]
                    for b, n, kk, rr, k0 in parts:
                        for c in range(2):
                            mm(bank(b, n, 0, 32), qls[:, c, i, :], kk[:, c, k0:k0 + n], start=(c == 0), stop=False)
                        last = mm(bank(b, n, 0, 32), qhs[64:96, i, :], rr[:, k0:k0 + n], start=False, stop=True)
                elif kind == "Bs":
                    keys = kcT[:, 0:2560].rearrange("p (j n) -> p j n", j=4)
                    for b, c0, n, kk, k0 in ((0, 0, 512, keys, 0), (1, 0, 128, keys, 512), (1, 128, 32, kT0, NTP)):
                        for j in range(4):
                            last = mm(bank(b, n, c0, 32), qbd0[:, i, j, :], kk[:, j, k0:k0 + n], start=(j == 0), stop=(j == 3))
                else:
                    keys = kcT_c
                    for c0, n, kk, k0 in ((0, 128, keys, 0), (128, 32, kT1, NTP)):
                        for j in range(2):
                            last = mm(bank(0, n, c0, 64), qbd1[:, i, j, :], kk[:, j, k0:k0 + n], start=(j == 0), stop=(j == 1))
                last.then_inc(sc_done, 1)

            def unit_transposes(u):
                kind, i = units[u]
                n = rows_of[kind]
                pe.wait_ge(pr_done, u + 1)
                if u >= 2:
                    pe.wait_ge(pt_cp, u - 1)
                b = 3 + u % 2
                sc = scores[:, u % 2, :]
                if n == 128:
                    for q in range(3):
                        last = tp(bank(b, 128, 128 * (q if q == 0 else 1 + (q - 1))), sc[:, 128 * q:128 * q + 128], ident)
                else:
                    nk = ktiles_of[kind]
                    for q in range(nk):
                        last = tp(bank(b, n, n * q), sc[0:n, 128 * q:128 * q + 128], ident[0:n, 0:n])
                    last = tp(bank(b, n, n * nk, 32), sc[0:n, 128 * nk:128 * nk + 32], ident[0:n, 0:n])
                last.then_inc(pt_tp, 1)

            def unit_pv(u):
                kind, i = units[u]
                pe.wait_ge(pt_cp, u + 1)
                if u:
                    pe.wait_ge(pv_cp, u)
                pT = probsT[:, u % 2, :]
                if kind == "Ap":
                    for c in range(2):
                        v0, v1 = z_ckv[:, 0, 128 * c:128 * c + 128], z_ckv[:, 1, 128 * c:128 * c + 128]
                        mm(bank(5, 128, 256 * c), v0, pT[:, 0:128], start=True, stop=True)
                        mm(bank(5, 128, 256 * c + 128), v0, pT[:, 128:256], start=True, stop=False)
                        last = mm(bank(5, 128, 256 * c + 128), v1, pT[:, 256:384], start=False, stop=True)
                elif kind in ("Bp", "Cp"):
                    if kind == "Bp":
                        r, v0, vv = 64 * (i % 2), 64 * i, z_v
                    else:
                        r, v0, vv = 64 * (i // 4 % 2), 1280 + 64 * (i // 4), z_c
                    out = ps[r:r + 64, 5 * 512:5 * 512 + 256]
                    mm(out[:, 0:128], vv[:, 0, v0:v0 + 64], pT[:, 0:128], start=True, stop=True)
                    mm(out[:, 128:256], vv[:, 0, v0:v0 + 64], pT[:, 128:256], start=True, stop=False)
                    last = mm(out[:, 128:256], vv[:, 1, v0:v0 + 64], pT[:, 256:384], start=False, stop=True)
                elif kind == "As":
                    for c in range(2):
                        for q in range(NPG):
                            mm(bank(5, 32, 32 * c), chunk("mla", i, 256 * q + 128 * c, 128), pT[:, 32 * q:32 * q + 32],
                               start=(q == 0), stop=False)
                        last = mm(bank(5, 32, 32 * c), z_ckv[0:32, 2, 128 * c:128 * c + 128], pT[0:32, 256:288], start=False, stop=True)
                elif kind == "Bs":
                    landed("bv", i)
                    for j in range(4):
                        for q in range(5):
                            mm(bank(5, 32, 32 * j), chunk("bv", i, 512 * q + 128 * j, 128), pT[:, 32 * q:32 * q + 32],
                               start=(q == 0), stop=False)
                        last = mm(bank(5, 32, 32 * j), z_v[0:32, 2, 128 * j:128 * j + 128], pT[0:32, 160:192], start=False, stop=True)
                else:
                    for j in range(2):
                        mm(bank(5, 64, 64 * j), chunk("c_cache", 0, 2048 + 256 * i + 128 * j, 128), pT[:, 0:64], start=True, stop=False)
                        last = mm(bank(5, 64, 64 * j), z_c[0:32, 2, 1280 + 128 * j:1408 + 128 * j], pT[0:32, 64:128],
                                  start=False, stop=True)
                last.then_inc(pv_done, 1)

            def attention(u0, u1):
                cache_tiles(u0)
                unit_scores(u0)
                for u in range(u0, u1):
                    if u + 1 < u1:
                        cache_tiles(u + 1)
                        unit_scores(u + 1)
                    unit_transposes(u)
                    unit_pv(u)

            attention(0, NU0)
            pe.wait_ge(pv_cp, NU0)
            for h in range(HA):
                if h >= 2:
                    pe.wait_ge(oa_cp, h - 1)
                r = 64 * (h % 2)
                for c in range(2):
                    last = mm(ps[r:r + 64, 512 * (h % 2):512 * (h % 2) + NT], kvb[:, c, 128 * h + 64:128 * h + 128],
                              qlT[:, c, h, :], start=(c == 0), stop=(c == 1))
                last.then_inc(oa_done, 1)
            pe.wait_ge(oa_cp, 8)
            linear_out(0, "out_ab", 4, KD, oT)
            sums(1)
            sums(2)
            pe.wait_ge(h_done, 18)
            for j in range(11):
                landed("ffd_in", j)
                w = chunk("ffd_in", j, 0, 4096).rearrange("p (g k m) -> p g k m", g=2, k=KD)
                for fb in range(2):
                    f = 2 * j + fb
                    if f >= 2:
                        pe.wait_ge(act_done, f - 1)
                    for g in range(2):
                        for k in range(KD):
                            last = mm(bank(2 * (f % 2) + g, NT), w[:, g, k, 128 * fb:128 * fb + 128], hT[:, k, :],
                                      start=(k == 0), stop=(k == KD - 1))
                    last.then_inc(gu_done, 1)
            pe.wait_ge(act_done, 22)
            linear_out(1, "ffd_out", 1, 22, actd)
            sums(3)
            sums(4)
            ada(1)
            pe.wait_ge(h_done, 27)
            for j in range(3):
                landed("qkv_c", j)
                wt = chunk("qkv_c", j, 0, 4096).rearrange("p (k m) -> p k m", k=KD)
                for t, (t0, n) in enumerate(TILES):
                    if nz >= 19:
                        pe.wait_ge(z_cp, nz - 3)
                    for k in range(KD):
                        last = mm(bank(nz % 4, 512, 0, n), hT[:, k, t0:t0 + n], wt[:, k, :], start=(k == 0), stop=(k == KD - 1))
                    last.then_inc(z_done, 1)
                    nz += 1
            mm(bank(7, 4), ident, ones[:, 0:4], start=True, stop=True).then_inc(e_gu, 1)
            pe.wait_ge(z_rdy, 8)
            for k in range(8):
                tp_tiles(lambda t, n: z_c[0:n, t, 128 * k:128 * k + 128], 128)
            for k in range(2):
                tp_tiles(lambda t, n: z_c[0:n, t, 1024 + 128 * k:1152 + 128 * k], 128)
            pe.wait_ge(t_cp, nt)
            pe.wait_ge(bd_rdy, 2)
            attention(NU0, NU)
            pe.wait_ge(pv_cp, NU)
            mm(bank(3, 4), ident, ones[:, 0:4], start=True, stop=True).then_inc(e_used, 4)
            mm(bank(3, 4), ident, ones[:, 0:4], start=True, stop=True).then_inc(e_gu, 1)
            linear_out(2, "out_c", 4, KD, oT)
            mm(bank(3, 4), ident, ones[:, 0:4], start=True, stop=True).then_inc(e_gu, 2)
            sums(5)
            sums(6)

            pe.wait_ge(h_done, 36)
            for t, (t0, n) in enumerate(TILES):
                for k in range(KD):
                    last = mm(bank(0, 8, 8 * t, n), hT[:, k, t0:t0 + n], wrout[:, k, :], start=(k == 0), stop=(k == KD - 1))
            last.then_inc(lg_done, 1)
            for t, (t0, n) in enumerate(TILES):
                for kk in range(2):
                    i = 2 * t + kk
                    if i >= 2:
                        pe.wait_ge(htok_cp, i - 1)
                    for k in range(4):
                        last = tp(bank(4 + i % 2, 128, 128 * k, n), hT[:, 4 * kk + k, t0:t0 + n], ident)
                    last.then_inc(htok_tp, 1)
            pe.wait_ge(msk_done, 1)
            for t in range(3):
                for tt in range(t + 1):
                    last = mm(bank(1, 8, 8 * t), cst[:, C_UP:C_UP + 128] if tt == t else ones, mask[:, tt, :],
                              start=(tt == 0), stop=(tt == t))
            for tt in range(3):
                last = mm(bank(1, 8, 24), ones, mask[:, tt, :], start=(tt == 0), stop=(tt == 2))
            last.then_inc(pos_done, 1)

            def gather(idx_pick, idx_free):
                pe.wait_ge(e_pick, idx_pick)
                if idx_free is not None:
                    pe.wait_ge(e_add, idx_free)
                for kk in range(2):
                    for k in range(4):
                        for t, (t0, n) in enumerate(TILES):
                            last = mm(bank(6 + kk, CAP, CAP * k), htok[0:n, t, 128 * (4 * kk + k):128 * (4 * kk + k) + 128],
                                      pick[0:n, t, :], start=(t == 0), stop=(t == 2))
                last.then_inc(e_gat, 1)

            def put_transposes(idx):
                pe.wait_ge(e_gcpA, idx)
                for t, (t0, n) in enumerate(TILES):
                    last = tp(bank(6, n, t0, CAP), pickg[0:n, t, :], ident[0:n, 0:n])
                last.then_inc(e_ptp, 1)

            def out_transposes(ready, first_free):
                pe.wait_ge(e_ocp, ready)
                pe.wait_ge(e_pcp, first_free)
                for kk in range(2):
                    for k in range(4):
                        last = tp(bank(6 + kk, 128, 128 * k, CAP), oeT[:, 4 * kk + k, :], ident)
                last.then_inc(e_tp, 1)

            def combine(k, par, done_before, tok):
                pe.wait_ge(e_tcp, tok)
                pe.wait_ge(e_add, done_before)
                mm(bank(6 + k % 2, NT), otok[:, 128 * k:128 * k + 128], putT[:, par, :], start=True, stop=True).then_inc(e_cb, 1)

            def expert(it, p_, half):
                for j in range(14):
                    c = 14 * half + j
                    sl = (NPLAN + c) % NSLOT
                    times = sum(1 for q in range(c + 1) if q % NSLOT == c % NSLOT)
                    pe.wait_ge(s_in[sl], 224 * it + (ring_total[sl] + 32 * times))
                    pe.wait_ge(e_act, 28 * it + (c + 1))
                    if j == 0:
                        pe.wait_ge(e_gcpA, 2 * it + p_ + (half + 1))
                        pe.wait_ge(e_gcpV, 2 * it + p_ + (half + 1))
                    w = ring[:, sl, :].rearrange("p (g k m) -> p g k m", g=2, k=KD)
                    for fb in range(2):
                        for g in range(2):
                            for k in range(KD):
                                last = mm(bank(j % 2, CAP, CAP * (2 * fb + g)), w[:, g, k, 128 * fb:128 * fb + 128], hsel[:, k, :],
                                          start=(k == 0), stop=(k == KD - 1))
                    last.then_inc(e_gu, 1)
                    if j == 0:
                        out_transposes(8 * it + 4 * half, 2 * it + p_ + (half + 1))
                    if 1 <= j <= 4:
                        for k in (2 * j - 2, 2 * j - 1):
                            combine(k, 1 - half, 16 * it + (8 * half + k + 1), 4 * it + (2 * half + 2))
                gather(2 * it + p_ + (half + 2), 16 * it + (8 * half + 10))
                for q in range(8):
                    pr, f2 = q // 2, q % 2
                    pe.wait_ge(e_in[q % 4], 64 * it + (32 * half + 16 * (q // 4) + 16))
                    pe.wait_ge(e_act, 28 * it + (14 * half + 7 * f2 + 7 + 2))
                    if f2 == 0:
                        if pr >= 2:
                            pe.wait_ge(e_ocp, 8 * it + (4 * half + pr - 1))
                    w = oring[:, q % 4, :].rearrange("p (f m) -> p f m", f=14)
                    for m in range(2):
                        for f in range(14):
                            last = mm(bank(2 + 2 * (pr % 2) + m, CAP), w[:, f, 128 * m:128 * m + 128], acte[:, 14 * f2 + f, :],
                                      start=(f2 == 0 and f == 0), stop=(f2 == 1 and f == 13))
                    last.then_inc(e_used, 1)
                    if q == 1:
                        put_transposes(2 * it + p_ + (half + 2))

            def pass_body(it0, p_):
                with pe.Fori(0, NE // 2) as i:
                    for half in range(2):
                        expert(it0 + i, p_, half)

            gather(1, None)
            put_transposes(1)
            pass_body(0, 0)
            pe.wait_ge(pass_rdy, 1)
            npass = pe.value_load(passes_i[0:1, :], min_val=1, max_val=MAXPASS)
            with pe.If(npass > 1):
                with pe.Fori(1, npass) as p_:
                    pe.wait_ge(e_pcp, 9 * p_)
                    gather(9 * p_ + 1, 64 * p_ + 2)
                    put_transposes(9 * p_ + 1)
                    pass_body(4 * p_, p_)
            pe.wait_ge(e_gcpV, 9 * npass)
            out_transposes(32 * npass, 9 * npass)
            for k in range(KD):
                combine(k, 1, 64 * npass + (k + 1), 16 * npass + 2)
            pe.wait_ge(e_add, 64 * npass + 10)
            sums(7)
            pe.wait_ge(x_upd, 32)
            for t, (t0, n) in enumerate(TILES):
                for kk in range(2):
                    i = 2 * t + kk
                    if i >= 2:
                        pe.wait_ge(y_cp, i - 1)
                    for k in range(4):
                        last = tp(bank(i % 2, 128, 128 * k, n), xT[:, 4 * kk + k, t0:t0 + n], ident)
                    last.then_inc(y_tp, 1)

        @block.scalar
        def _(act):
            na = [0]

            def link(ins):
                na[0] += 1
                ins.then_inc(chain_a, 1)
                act.wait_ge(chain_a, na[0])

            def fn(out, in_, f, **kw):
                return nc.scalar.activation(out, in_, f, **kw)

            def std(n):
                act.wait_ge(stat_done, n + 1)
                fn(rstd[:, :], bank(7, NT), ACT.Sqrt, scale=1.0 / D, bias=cst[:, C_EPS:C_EPS + 1]).then_inc(std_done, 1)

            def f_out(L, n):
                for k in range(KD):
                    act.wait_ge(f_done, 8 * L + k + 1)
                    fn(sq[:, k, :], bank(4 + k % 2, NT), ACT.Square).then_inc(sq_done, 1)
                    fn(fT[:, k, :], bank(4 + k % 2, NT), ACT.Copy).then_inc(f_cp, 1)
                std(n)

            def x_squares(m):
                for k in range(KD):
                    act.wait_ge(x_upd, 8 * m + k + 1)
                    fn(sq[:, k, :], xT[:, k, :], ACT.Square).then_inc(sq_done, 1)
                std(2 * m + 2)

            act.wait_ge(s_xload, 5 * 16)
            fn(cstok, ctok, ACT.Silu).then_inc(c_silu, 1)
            for k in range(KD):
                act.wait_ge(x_tp, k + 1)
                fn(sq[:, k, :], bank(k % 2, NT), ACT.Square).then_inc(sq_done, 1)
                fn(xT[:, k, :], bank(k % 2, NT), ACT.Copy).then_inc(x_cp, 1)
            std(0)

            nz = 0
            for j, w in enumerate((384, 288, 512, 512, 512)):
                for t, (t0, n) in enumerate(TILES):
                    act.wait_ge(z_done, nz + 1)
                    b = nz % 4
                    if j == 0:
                        fn(z_qa[0:n, t, :], bank(b, 384, 0, n), ACT.Copy)
                        fn(bank(b, 384, 0, n), bank(b, 384, 0, n), ACT.Square, accum_out=ss[0:n, t, 0:1]).then_inc(z_cp, 1)
                    elif j == 1:
                        fn(z_ckv[0:n, t, :], bank(b, 256, 0, n), ACT.Copy)
                        fn(z_kr[0:n, t, 64:96], bank(b, 32, 256, n), ACT.Copy)
                        fn(bank(b, 256, 0, n), bank(b, 256, 0, n), ACT.Square, accum_out=ss[0:n, t, 1:2]).then_inc(z_cp, 1)
                    elif j < 4:
                        fn(z_qk[0:n, t, 512 * (j - 2):512 * (j - 1)], bank(b, 512, 0, n), ACT.Copy).then_inc(z_cp, 1)
                    else:
                        fn(z_v[0:n, t, :], bank(b, 512, 0, n), ACT.Copy).then_inc(z_cp, 1)
                    nz += 1
                if j < 2:
                    act.wait_ge(z_cp, nz)
                    for t, (t0, n) in enumerate(TILES):
                        last = fn(ss[0:n, t, 2 + j:3 + j], ss[0:n, t, j:j + 1], ACT.Sqrt, scale=1.0 / (QL, KV)[j],
                                  bias=cst[0:n, C_EPS:C_EPS + 1])
                    last.then_inc(qn_rdy, 1)
            for t, (t0, n) in enumerate(TILES):
                for hh in range(2):
                    act.wait_ge(q_done, 2 * t + hh + 1)
                    fn(z2[0:n, t, 384 * hh:384 * hh + 384], bank((2 * t + hh) % 4, 384, 0, n), ACT.Copy).then_inc(q_cp, 1)

            kt_n = [0, 0]

            def cache_tiles(u):
                kind, b = units[u]
                for i in range(ktiles_of.get(kind, 0)):
                    par = i % 2
                    kt_n[par] += 1
                    if par:
                        continue
                    act.wait_ge(kt_tp[0], kt_n[0])
                    copy_keys(fn_copy, kind, i, 7).then_inc(kt_cp[0], 1)

            def fn_copy(out, in_):
                return fn(out, in_, ACT.Copy)

            def unit_exp(u):
                kind, i = units[u]
                n = rows_of[kind]
                sc = scores[:, u % 2, :]
                act.wait_ge(mx_done, u + 1)
                if n == 128:
                    fn(sc[:, 0:128], sc[:, 0:128], ACT.Exp, bias=nmax[:, u % 2, 0:1], accum_out=lsum[:, u % 2, 0:1])
                    last = fn(sc[:, 128:384], sc[:, 128:384], ACT.Exp, bias=nmax[:, u % 2, 1:2], accum_out=lsum[:, u % 2, 1:2])
                    if kind == "Cp":
                        for q in range(2):
                            last = fn(lsum[:, u % 2, 2 + q:3 + q], sinks[:, i:i + 1], ACT.Exp, bias=nmax[:, u % 2, q:q + 1])
                else:
                    w = 128 * ktiles_of[kind] + 32
                    last = fn(sc[0:n, 0:w], sc[0:n, 0:w], ACT.Exp, bias=nmax[0:n, u % 2, 0:1], accum_out=lsum[0:n, u % 2, 0:1])
                    if kind == "Cs":
                        last = fn(lsum[0:n, u % 2, 2:3], sinkr[:, :], ACT.Exp, bias=nmax[0:n, u % 2, 0:1])
                last.then_inc(ex_done, 1)

            def unit_copies(u):
                kind, i = units[u]
                n = rows_of[kind]
                act.wait_ge(pt_tp, u + 1)
                b = 3 + u % 2
                pT = probsT[:, u % 2, :]
                if n == 128:
                    fn(pT[:, 0:384], bank(b, 384), ACT.Copy).then_inc(pt_cp, 1)
                else:
                    w = n * ktiles_of[kind]
                    fn(pT[:, 0:w], bank(b, w), ACT.Copy)
                    fn(pT[0:32, w:w + n], bank(b, n, w, 32), ACT.Copy).then_inc(pt_cp, 1)
                act.wait_ge(pv_done, u + 1)
                tok = NTP + TS * i
                if kind == "Ap":
                    last = fn(qlT[:, :, i, 0:256], bank(5).rearrange("p (c n) -> p c n", c=2), ACT.Copy)
                elif kind == "Bp":
                    r = 64 * (i % 2)
                    last = fn(oT[r:r + 64, 4 + i // 2, 0:256], ps[r:r + 64, 2560:2816], ACT.Copy)
                elif kind == "Cp":
                    g = i // 4
                    r = 64 * (g % 2)
                    last = fn(oT[r:r + 64, 4 * (g // 2) + i % 4, 0:256], ps[r:r + 64, 2560:2816], ACT.Copy)
                elif kind == "As":
                    for c in range(2):
                        last = fn(qlT[:, c, :, tok:tok + TS], bank(5, 32, 32 * c).rearrange("p (h t) -> p h t", t=TS), ACT.Copy)
                elif kind == "Bs":
                    for r in range(2):
                        for j in range(4):
                            c0 = 2560 + 32 * j + 4 * (2 * j + r)
                            last = fn(oT[64 * r:64 * r + 64, 4 + j, tok:tok + TS], ps[64 * r:64 * r + 64, c0:c0 + 4], ACT.Copy)
                else:
                    for r in range(2):
                        for j in range(2):
                            c0 = 2560 + 64 * j + 16 * (2 * j + r)
                            last = fn(oT[64 * r:64 * r + 64, 4 * j:4 * j + 4, tok:tok + TS],
                                      ps[64 * r:64 * r + 64, c0:c0 + 16].rearrange("p (r t) -> p r t", t=TS), ACT.Copy)
                last.then_inc(pv_cp, 1)

            def attention(u0, u1):
                cache_tiles(u0)
                unit_exp(u0)
                for u in range(u0, u1):
                    if u + 1 < u1:
                        cache_tiles(u + 1)
                        unit_exp(u + 1)
                    unit_copies(u)

            act.wait_ge(s_out0, 8 * 16)
            attention(0, NU0)
            for h in range(HA):
                act.wait_ge(oa_done, h + 1)
                r = 64 * (h % 2)
                fn(oT[r:r + 64, h // 2, :], ps[r:r + 64, 512 * (h % 2):512 * (h % 2) + NT], ACT.Copy).then_inc(oa_cp, 1)
            f_out(0, 1)
            x_squares(0)
            for f in range(22):
                act.wait_ge(gu_done, f + 1)
                if f:
                    act.wait_ge(act_done, f)
                fn(silu_d, bank(2 * (f % 2), NT), ACT.Silu).then_inc(si_done, 1)
            f_out(1, 3)
            x_squares(1)
            for j in range(3):
                for t, (t0, n) in enumerate(TILES):
                    act.wait_ge(z_done, nz + 1)
                    out, src = z_c[0:n, t, 512 * j:512 * j + 512], bank(nz % 4, 512, 0, n)
                    if j < 2:
                        out = out.rearrange("p (r a d) -> p a r d", a=2, r=4)
                        src = src.rearrange("p (a r d) -> p a r d", a=2, r=4)
                    fn(out, src, ACT.Copy).then_inc(z_cp, 1)
                    nz += 1
            attention(NU0, NU)
            f_out(2, 5)
            x_squares(2)

            act.wait_ge(s_out1, 4 * 16)
            for t, (t0, n) in enumerate(TILES):
                for kk in range(2):
                    i = 2 * t + kk
                    act.wait_ge(htok_tp, i + 1)
                    fn(htok[0:n, t, 512 * kk:512 * kk + 512], bank(4 + i % 2, 512, 0, n), ACT.Copy).then_inc(htok_cp, 1)
            act.wait_ge(lg_cp, 1)
            fn(gate[:, :, 1:2], gate[:, :, 0:1], ACT.Exp).then_inc(ge_done, 1)

            def gather_copy(idx):
                act.wait_ge(e_gat, idx)
                fn(hsel[:, 0:4, :], bank(6, 4 * CAP).rearrange("p (k n) -> p k n", k=4), ACT.Copy).then_inc(e_gcpA, 1)

            def put_copy(idx, par):
                act.wait_ge(e_ptp, idx)
                fn(putT[:, par, :], bank(6, NT, 0, CAP), ACT.Copy).then_inc(e_pcp, 1)

            def out_tok(idx):
                act.wait_ge(e_tp, idx)
                for kk in range(2):
                    fn(otok[:, 512 * kk:512 * kk + 512], bank(6 + kk, 512, 0, CAP), ACT.Copy).then_inc(e_tcp, 1)

            def expert(it, p_, half):
                for j in range(14):
                    c = 14 * half + j
                    act.wait_ge(e_gu, 28 * it + (c + 5))
                    act.wait_ge(e_act, 28 * it + (c + 1))
                    fn(sil[:, j % 2, :, :], bank(j % 2, 4 * CAP).rearrange("p (f g n) -> p f g n", f=2, g=2)[:, :, 0, :],
                       ACT.Silu).then_inc(e_si, 1)
                    if j == 0:
                        out_tok(2 * it + (half + 1))
                gather_copy(2 * it + p_ + (half + 2))
                for pr in range(4):
                    act.wait_ge(e_used, 16 * it + (8 * half + 2 * pr + 6))
                    b = 2 + 2 * (pr % 2)
                    fn(oeT[:, 2 * pr, :], bank(b, CAP), ACT.Copy)
                    fn(oeT[:, 2 * pr + 1, :], bank(b + 1, CAP), ACT.Copy).then_inc(e_ocp, 1)
                    if pr == 0:
                        put_copy(2 * it + p_ + (half + 2), 1 - half)

            def pass_body(it0, p_):
                with act.Fori(0, NE // 2) as i:
                    for half in range(2):
                        expert(it0 + i, p_, half)

            gather_copy(1)
            put_copy(1, 0)
            pass_body(0, 0)
            act.wait_ge(pass_rdy, 1)
            npass = act.value_load(passes_i[0:1, :], min_val=1, max_val=MAXPASS)
            with act.If(npass > 1):
                with act.Fori(1, npass) as p_:
                    gather_copy(9 * p_ + 1)
                    put_copy(9 * p_ + 1, 0)
                    pass_body(4 * p_, p_)
            out_tok(8 * npass + 1)
            act.wait_ge(e_cb, 64 * npass + KD)
            for k in range(KD):
                act.wait_ge(e_add, 64 * npass + (k + 3))
                fn(sq[:, k, :], fT[:, k, :], ACT.Square).then_inc(sq_done, 1)
            std(7)
            for i in range(6):
                t, kk = i // 2, i % 2
                n = TILES[t][1]
                act.wait_ge(y_tp, i + 1)
                fn(htok[0:n, t, 512 * kk:512 * kk + 512], bank(i % 2, 512, 0, n), ACT.Copy).then_inc(y_cp, 1)

        @block.vector
        def _(dve):
            V = nc.vector
            nv = [0]

            def link(ins):
                nv[0] += 1
                ins.then_inc(chain_v, 1)
                dve.wait_ge(chain_v, nv[0])

            def sample(t, k0=0, k1=KD):
                return t[:, k0:k1, NTP:NT].rearrange("p k (b t) -> p k b t", t=TS)

            def per_batch(t):
                return t[:, :, 1:9].unsqueeze(3).broadcast_to([P, KD, NB, TS])

            def pre_norm(n, l, w):
                sh = mod[:, l, 24 * w:24 * w + 8, :]
                dve.wait_ge(std_done, n + 1)
                link(V.reciprocal(rinv[:, :], rstd[:, :]))
                link(V.tensor_tensor(hT, xT[:, :, :], rinv[:, :].unsqueeze(1).broadcast_to([P, KD, NT]), ALU.mult))
                for k in range(KD):
                    V.tensor_scalar(hT[:, k, 0:NTP], hT[:, k, 0:NTP], coef[:, 2 * w, k, 0:1], sh[:, k, 0:1],
                                    ALU.mult, ALU.add).then_inc(h_done, 1)
                link(V.tensor_tensor(sample(hT), sample(hT), per_batch(coef[:, 2 * w, :, :]), ALU.mult))
                V.tensor_tensor(sample(hT), sample(hT), per_batch(sh), ALU.add).then_inc(h_done, 1)

            def post_norm(n, m, w):
                g = coef[:, 2 * w + 1, :, :]
                dve.wait_ge(std_done, n + 1)
                link(V.reciprocal(rinv[:, :], rstd[:, :]))
                link(V.tensor_tensor(fT, fT, rinv[:, :].unsqueeze(1).broadcast_to([P, KD, NT]), ALU.mult))
                link(V.tensor_tensor(sample(fT), sample(fT), per_batch(g), ALU.mult))
                link(V.tensor_tensor(sample(xT), sample(xT), sample(fT), ALU.add))
                for k in range(KD):
                    V.scalar_tensor_tensor(out=xT[:, k, 0:NTP], in0=fT[:, k, 0:NTP], scalar=g[:, k, 0:1],
                                           in1=xT[:, k, 0:NTP], op0=ALU.mult, op1=ALU.add).then_inc(x_upd, 1)

            def coefficients(l):
                dve.wait_ge(ada_done, 12 * (l + 1))
                bias = vecT[:, 48 * l:48 * l + 48].unsqueeze(2).broadcast_to([P, 48, 9])
                link(V.tensor_tensor(mod[:, l, :, :], bank(6, 432).rearrange("p (m c) -> p m c", c=9), bias, ALU.add))
                for w in range(2):
                    for i, (name, blk) in enumerate((("pre", 8), ("post", 16))):
                        g = vecT[:, 96 + 32 * w + 16 * i + 8 * l:96 + 32 * w + 16 * i + 8 * l + 8].unsqueeze(2).broadcast_to([P, 8, 9])
                        src = mod[:, l, 24 * w + blk:24 * w + blk + 8, :]
                        if name == "pre":
                            V.scalar_tensor_tensor(out=coef[:, 2 * w, :, :], in0=src, scalar=1.0, in1=g, op0=ALU.add, op1=ALU.mult)
                        else:
                            last = V.tensor_tensor(coef[:, 2 * w + 1, :, :], src, g, ALU.mult)
                link(last)

            def rope(x, n, heads, half, tab, ta, tb, done=None, value=0):
                c = tab[0:n, 0:2 * half].unsqueeze(1).broadcast_to([n, heads, 2 * half])
                s1 = tab[0:n, 2 * half:3 * half].unsqueeze(1).broadcast_to([n, heads, half])
                s2 = tab[0:n, 3 * half:4 * half].unsqueeze(1).broadcast_to([n, heads, half])
                V.tensor_tensor(ta, x[:, :, 0:2 * half], c, ALU.mult)
                V.tensor_tensor(tb[:, :, 0:half], x[:, :, half:2 * half], s1, ALU.mult)
                link(V.tensor_tensor(tb[:, :, half:2 * half], x[:, :, 0:half], s2, ALU.mult))
                last = V.tensor_tensor(x[:, :, 0:2 * half], ta, tb, ALU.add)
                if done is None:
                    link(last)
                else:
                    last.then_inc(done, 1)
                    dve.wait_ge(done, value)

            def rope_tmp(region, n, heads, w):
                a = region[0:n, 0:heads * w].rearrange("p (h w) -> p h w", h=heads)
                b = region[0:n, heads * w:2 * heads * w].rearrange("p (h w) -> p h w", h=heads)
                return a, b

            dve.wait_ge(c_tp, 1)
            V.tensor_copy(csT[:, :, :], bank(2, 72).rearrange("p (k c) -> p k c", c=9))
            link(V.tensor_copy(vecT[:, :], bank(3, 160)))
            dve.wait_ge(s_xload, 5 * 16)
            dve.wait_ge(s_ld, 8 * 16)
            V.tensor_scalar(nsinks[:, :], sinks[:, :], -1.0, None, ALU.mult)
            link(V.tensor_scalar(nsinkr[:, :], sinkr[:, :], -1.0, None, ALU.mult))
            V.memset(z_kr[:, :, 0:64], 0.0)
            V.memset(qbd, 0.0).then_inc(c_cp, 1)
            coefficients(0)
            pre_norm(0, 0, 0)

            for j, (zz, width, g0) in enumerate(((z_qa, QL, 0), (z_ckv, KV, QL))):
                dve.wait_ge(qn_rdy, j + 1)
                for t, (t0, n) in enumerate(TILES):
                    last = V.reciprocal(ss[0:n, t, 4 + j:5 + j], ss[0:n, t, 2 + j:3 + j])
                link(last)
                if j == 1:
                    for t, (t0, n) in enumerate(TILES):
                        kr = z_kr[0:n, t:t + 1, 64:96]
                        ta, tb = rope_tmp(rtmp2[:, 640:960], n, 1, 32)
                        rope(kr, n, 1, 16, cst[:, C_RA + 64 * t:C_RA + 64 * t + 64], ta, tb)
                for t, (t0, n) in enumerate(TILES):
                    last = V.scalar_tensor_tensor(out=zz[0:n, t, :], in0=zz[0:n, t, :], scalar=ss[0:n, t, 4 + j:5 + j],
                                                  in1=gqkv[0:n, g0:g0 + width], op0=ALU.mult, op1=ALU.mult)
                last.then_inc(z_rdy, 1)
            tcount = [0]

            def t_next():
                dve.wait_ge(t_done, tcount[0] + 1)
                tcount[0] += 1
                return 4 + (tcount[0] - 1) % 2

            for hp in range(4):
                b = t_next()
                V.tensor_copy(wukT[0:64, 2 * hp:2 * hp + 2, :], bank(b, 512, 0, 64).rearrange("p (h c) -> p h c", h=2)).then_inc(t_cp, 1)
            for k in range(3):
                V.tensor_copy(qnT[:, k, :], bank(t_next(), NT)).then_inc(t_cp, 1)
            for k in range(2):
                V.tensor_copy(ckvT[:, k, :], bank(t_next(), NT)).then_inc(t_cp, 1)
            V.tensor_copy(krT[64:96, :], ps[64:96, 512 * t_next():][:, 0:NT]).then_inc(t_cp, 1)
            dve.wait_ge(z_cp, 12)
            for t, (t0, n) in enumerate(TILES):
                ta, tb = rope_tmp(rtmp2, n, 16, 16)
                rope(z_qk[0:n, t, :].rearrange("p (h d) -> p h d", h=16), n, 16, 8, cst[:, C_RB + 32 * t:C_RB + 32 * t + 32], ta, tb, z_rdy, 3 + t)
            for t, (t0, n) in enumerate(TILES):
                dve.wait_ge(q_cp, 2 * t + 2)
                ta, tb = rope_tmp(rtmp2, n, 8, 32)
                rope(z2[0:n, t, :].rearrange("p (h d) -> p h d", h=8)[:, :, 64:96], n, 8, 16,
                     cst[:, C_RA + 64 * t:C_RA + 64 * t + 64], ta, tb, q_rope, t + 1)
            for k in range(4):
                V.tensor_copy(qT0[:, k, :], bank(t_next(), NT)).then_inc(t_cp, 1)
            for k in range(4):
                V.tensor_copy(kT0[:, k, :], bank(t_next(), NT)).then_inc(t_cp, 1)
            for h in range(HA):
                V.tensor_copy(qhT[:, h, :], bank(t_next(), NT, 0, 96)).then_inc(t_cp, 1)
            for h in range(HA):
                for c in range(2):
                    V.tensor_copy(qlT[:, c, h, :], bank(t_next(), NT)).then_inc(t_cp, 1)
            dve.wait_ge(t_cp, tcount[0])
            for c in range(2):
                V.tensor_copy(qls[:, c, :, :].rearrange("p b (h t) -> p h b t", t=TS),
                              qlT[:, c, :, NTP:NT].rearrange("p h (b t) -> p h b t", t=TS))
            V.tensor_copy(qhs[64:96, :, :].rearrange("p b (h t) -> p h b t", t=TS),
                          qhT[64:96, :, NTP:NT].rearrange("p h (b t) -> p h b t", t=TS))
            for j in range(4):
                for r in range(2):
                    h = 2 * j + r
                    last = V.tensor_copy(qbd0[64 * r:64 * r + 64, :, j, 4 * h:4 * h + 4],
                                         qT0[64 * r:64 * r + 64, j, NTP:NT].rearrange("p (b t) -> p b t", t=TS))
            last.then_inc(bd_rdy, 1)
            dve.wait_ge(s_out0, 8 * 16)

            kt_n = [0, 0]

            def cache_tiles(u):
                kind, b = units[u]
                for i in range(ktiles_of.get(kind, 0)):
                    par = i % 2
                    kt_n[par] += 1
                    if not par:
                        continue
                    dve.wait_ge(kt_tp[1], kt_n[1])
                    copy_keys(V.tensor_copy, kind, i, 6).then_inc(kt_cp[1], 1)

            def unit_max(u):
                kind, i = units[u]
                n = rows_of[kind]
                sc = scores[:, u % 2, :]
                dve.wait_ge(sc_done, u + 1)
                if u >= 2:
                    dve.wait_ge(pt_tp, u - 1)
                scale = MLA_SCALE if kind[0] == "A" else HD_SCALE

                def masked(out, src, m):
                    return V.scalar_tensor_tensor(out=out, in0=src, scalar=scale, in1=m, op0=ALU.mult, op1=ALU.add)

                if n == 128:
                    m0 = {"A": M_A, "B": M_B, "C": M_C}[kind[0]]
                    last = masked(sc[:, 0:384], bank(0, 384), msk[:, m0:m0 + 384])
                    w = 384
                elif kind == "As":
                    V.tensor_scalar(sc[0:32, 0:1024], ps[0:32, 0:1024], scale, None, ALU.mult)
                    last = masked(sc[0:32, 1024:1056], bank(2, 32, 0, 32), msk[0:32, M_NA + 32 * i:M_NA + 32 * i + 32])
                    w = 1056
                elif kind == "Bs":
                    masked(sc[0:32, 0:640], ps[0:32, 0:640], msk[0:32, M_SB:M_SB + 640])
                    last = masked(sc[0:32, 640:672], ps[0:32, 640:672], msk[0:32, M_NB + 32 * i:M_NB + 32 * i + 32])
                    w = 672
                else:
                    masked(sc[0:64, 0:128], ps[0:64, 0:128], cst[0:64, C_CM:C_CM + 128])
                    last = masked(sc[0:64, 128:160], ps[0:64, 128:160], msk[0:64, M_NA + 32 * i:M_NA + 32 * i + 32])
                    w = 160
                last.then_inc(sc_cp, 1)
                dve.wait_ge(sc_cp, u + 1)
                nm = nmax[:, u % 2, :]
                if n == 128:
                    V.tensor_reduce(nm[:, 0:1], sc[:, 0:128], AX_X, ALU.max, negate=True)
                    last = V.tensor_reduce(nm[:, 1:2], sc[:, 128:384], AX_X, ALU.max, negate=True)
                    if kind == "Cp":
                        link(last)
                        last = V.tensor_scalar(nm[:, 0:2], nm[:, 0:2], nsinks[:, i:i + 1], None, ALU.min)
                else:
                    last = V.tensor_reduce(nm[0:n, 0:1], sc[0:n, 0:w], AX_X, ALU.max, negate=True)
                    if kind == "Cs":
                        link(last)
                        last = V.tensor_scalar(nm[0:n, 0:1], nm[0:n, 0:1], nsinkr[:, :], None, ALU.min)
                last.then_inc(mx_done, 1)

            def unit_probs(u):
                kind, i = units[u]
                n = rows_of[kind]
                sc = scores[:, u % 2, :]
                ls, r = lsum[:, u % 2, :], rl[:, u % 2, :]
                dve.wait_ge(ex_done, u + 1)
                nh = 2 if n == 128 else 1
                if kind[0] == "C":
                    link(V.tensor_tensor(ls[0:n, 0:nh], ls[0:n, 0:nh], ls[0:n, 2:2 + nh], ALU.add))
                link(V.reciprocal(r[0:n, 0:nh], ls[0:n, 0:nh]))
                if nh == 2:
                    V.tensor_scalar(sc[:, 0:128], sc[:, 0:128], r[:, 0:1], None, ALU.mult)
                    V.tensor_scalar(sc[:, 128:384], sc[:, 128:384], r[:, 1:2], None, ALU.mult).then_inc(pr_done, 1)
                else:
                    w = 128 * ktiles_of[kind] + 32
                    V.tensor_scalar(sc[0:n, 0:w], sc[0:n, 0:w], r[0:n, 0:1], None, ALU.mult).then_inc(pr_done, 1)

            def attention(u0, u1):
                cache_tiles(u0)
                unit_max(u0)
                for u in range(u0, u1):
                    unit_probs(u)
                    if u + 1 < u1:
                        cache_tiles(u + 1)
                        unit_max(u + 1)

            attention(0, NU0)
            post_norm(1, 0, 0)
            pre_norm(2, 0, 1)
            for f in range(22):
                dve.wait_ge(si_done, f + 1)
                V.tensor_tensor(actd[:, f, :], bank(2 * (f % 2) + 1, NT), silu_d, ALU.mult).then_inc(act_done, 1)
            post_norm(3, 1, 1)
            link(V.memset(qbd, 0.0))
            coefficients(1)
            pre_norm(4, 1, 0)
            dve.wait_ge(z_cp, 24)
            for t, (t0, n) in enumerate(TILES):
                ta, tb = rope_tmp(rtmp2, n, 20, 16)
                rope(z_c[0:n, t, 0:1280].rearrange("p (h d) -> p h d", h=20), n, 20, 8, cst[:, C_RB + 32 * t:C_RB + 32 * t + 32], ta, tb, z_rdy, 6 + t)
            for k in range(8):
                V.tensor_copy(qT1[:, k, :], bank(t_next(), NT)).then_inc(t_cp, 1)
            for k in range(2):
                V.tensor_copy(kT1[:, k, :], bank(t_next(), NT)).then_inc(t_cp, 1)
            dve.wait_ge(t_cp, tcount[0])
            for j in range(2):
                for r in range(2):
                    g = 2 * j + r
                    for b in range(NB):
                        last = V.tensor_copy(qbd1[64 * r:64 * r + 64, b, j, 16 * g:16 * g + 16].rearrange("p (r t) -> p r t", t=TS),
                                             qT1[64 * r:64 * r + 64, 4 * j:4 * j + 4, NTP + TS * b:NTP + TS * b + TS])
            last.then_inc(bd_rdy, 1)
            attention(NU0, NU)
            post_norm(5, 2, 0)
            pre_norm(6, 1, 1)

            V.memset(oh, 0.0)
            V.memset(gate, 0.0)
            V.memset(gates, 0.0)
            V.memset(posm, -1.0)
            V.memset(topf, 0.0)
            V.memset(oeT, 0.0).then_inc(e_add, 2)
            V.memset(putT, 0.0).then_inc(e_act, 2)
            link(V.memset(fT, 0.0))
            dve.wait_ge(lg_done, 1)
            for t, (t0, n) in enumerate(TILES):
                last = V.tensor_tensor(logit[0:n, t, :], bank(0, 8, 8 * t, n), brout[0:n, :], ALU.add)
            link(last)
            for t, (t0, n) in enumerate(TILES):
                last = V.max(top[0:n, t, :], logit[0:n, t, :])
            link(last)
            for t, (t0, n) in enumerate(TILES):
                V.max_index(topi[0:n, t, :], top[0:n, t, :], logit[0:n, t, :])
                last = V.tensor_tensor(gate[0:n, t, 0:1], top[0:n, t, 1:2], top[0:n, t, 0:1], ALU.subtract)
            last.then_inc(lg_cp, 1)
            dve.wait_ge(lg_cp, 1)
            for t, (t0, n) in enumerate(TILES):
                last = V.tensor_copy(topf[0:n, t, :], topi[0:n, t, 0:2])
            link(last)
            for t, (t0, n) in enumerate(TILES):
                for w in range(2):
                    last = V.tensor_scalar(oh[0:n, w, t, :], cst[0:n, C_I8:C_I8 + 8], topf[0:n, t, w:w + 1], None, ALU.is_equal)
            link(last)
            V.tensor_tensor(mask, oh[:, 0, :, :], oh[:, 1, :, :], ALU.add).then_inc(msk_done, 1)
            dve.wait_ge(ge_done, 1)
            link(V.tensor_scalar(gate[:, :, 2:3], gate[:, :, 1:2], 1.0, None, ALU.add))
            link(V.reciprocal(gate[:, :, 2:3], gate[:, :, 2:3]))
            link(V.tensor_tensor(gate[:, :, 3:4], gate[:, :, 2:3], gate[:, :, 1:2], ALU.mult))
            for w in range(2):
                last = V.tensor_tensor(oh[:, w, :, :], oh[:, w, :, :], gate[:, :, 2 + w:3 + w].broadcast_to([P, 3, NE]), ALU.mult)
            link(last)
            link(V.tensor_tensor(gates[:, 0:NE, :].rearrange("p n t -> p t n"), oh[:, 0, :, :], oh[:, 1, :, :], ALU.add))
            dve.wait_ge(msk_done, 1)
            dve.wait_ge(pos_done, 1)
            link(V.scalar_tensor_tensor(out=pm_t, in0=bank(1, 24).rearrange("p (t n) -> p t n", t=3), scalar=1.0, in1=mask,
                                        op0=ALU.add, op1=ALU.mult))
            link(V.tensor_scalar(posm[:, 0:NE, :].rearrange("p n t -> p t n"), pm_t, -1.0, None, ALU.add))
            link(V.tensor_reduce(passes, bank(1, 8, 24), AX_X, ALU.max))
            for q in range(1, MAXPASS):
                V.tensor_scalar(cnt[:, q:q + 1], passes, float(CAP * q), None, ALU.is_gt)
            V.memset(cnt[:, MAXPASS:MAXPASS + 1], 1.0)
            link(V.memset(cnt[:, 0:1], 0.0))
            link(V.tensor_reduce(passes, cnt[:, 1:MAXPASS + 1], AX_X, ALU.add))
            V.tensor_copy(passes_i, passes).then_inc(pass_rdy, 1)

            ne = [0]

            def elink(ins, base):
                ne[0] += 1
                ins.then_inc(chain_e, 1)
                dve.wait_ge(chain_e, base + ne[0])

            def choose(e, gathered, turned, base):
                if gathered is not None:
                    dve.wait_ge(e_gat, gathered)
                    dve.wait_ge(e_ptp, turned)
                V.tensor_copy(cur[:, 0:1, :], posm[:, bass.ds(e, 1), :])
                elink(V.tensor_copy(cur[:, 1:2, :], gates[:, bass.ds(e, 1), :]), base)
                for t in range(3):
                    V.tensor_scalar(pick[:, t, :], cst[:, C_IC:C_IC + CAP], cur[:, 0, t:t + 1], None, ALU.is_equal)
                    last = V.tensor_scalar(pickg[:, t, :], cst[:, C_IC:C_IC + CAP], cur[:, 0, t:t + 1], cur[:, 1, t:t + 1],
                                           ALU.is_equal, ALU.mult)
                last.then_inc(e_pick, 1)

            def gather_copy(idx):
                dve.wait_ge(e_gat, idx)
                V.tensor_copy(hsel[:, 4:8, :], bank(7, 4 * CAP).rearrange("p (k n) -> p k n", k=4)).then_inc(e_gcpV, 1)

            def add(k, idx):
                dve.wait_ge(e_cb, idx)
                return V.tensor_tensor(fT[:, k, :], bank(6 + k % 2, NT), fT[:, k, :], ALU.add)

            def expert(it, i, p_, half, base):
                for j in range(14):
                    c = 14 * half + j
                    dve.wait_ge(e_si, 28 * it + (c + 1))
                    V.tensor_tensor(acte[:, 2 * j:2 * j + 2, :],
                                    bank(j % 2, 4 * CAP).rearrange("p (f g n) -> p f g n", f=2, g=2)[:, :, 1, :],
                                    sil[:, j % 2, :, :], ALU.mult).then_inc(e_act, 1)
                    if 1 <= j <= 4:
                        for k in (2 * j - 2, 2 * j - 1):
                            add(k, 16 * it + (8 * half + k + 1)).then_inc(e_add, 1)
                    if j == 6:
                        choose(2 * i + (half + 1), 2 * it + p_ + (half + 1), 2 * it + p_ + (half + 1), base)
                gather_copy(2 * it + p_ + (half + 2))

            def pass_body(it0, p_, base):
                with dve.Fori(0, NE // 2) as i:
                    ne[0] = 0
                    for half in range(2):
                        expert(it0 + i, i, p_, half, base + 2 * i)
                assert ne[0] == 2

            ne[0] = 0
            choose(0, None, None, 0)
            gather_copy(1)
            pass_body(0, 0, 1)
            dve.wait_ge(pass_rdy, 1)
            npass = dve.value_load(passes_i[0:1, :], min_val=1, max_val=MAXPASS)
            with dve.If(npass > 1):
                with dve.Fori(1, npass) as p_:
                    dve.wait_ge(e_pick, 9 * p_)
                    ne[0] = 0
                    base = 10 * p_ - 1
                    elink(V.tensor_scalar(posm[:, :, :], posm[:, :, :], float(-CAP), None, ALU.add), base)
                    choose(0, 9 * p_, 9 * p_, base)
                    gather_copy(9 * p_ + 1)
                    pass_body(4 * p_, p_, 10 * p_ + 1)
            dve.wait_ge(e_add, 64 * npass + 2)
            for k in range(KD):
                add(k, 64 * npass + (k + 1)).then_inc(e_add, 1)
            dve.wait_ge(e_add, 64 * npass + 10)
            post_norm(7, 3, 1)

    return nc


_INS = ["x_prompt", "x_sample", "c_prompt", "c_sample", "cache_mla_ckv", "cache_mla_krope", "cache_b_k", "cache_b_v",
        "cache_c_k", "cache_c_v", "page_table", "w_ada", "b_ada", "g_pre_mix", "g_post_mix", "g_pre_ffn", "g_post_ffn",
        "w_in_ab", "g_q_a", "w_q_b", "g_kv_a", "w_kv_b", "w_out_ab", "w_ffd_in", "w_ffd_out", "w_qkv_c", "sinks_c",
        "w_out_c", "w_router", "b_router", "w_moe_in", "w_moe_out"]
_OUTS = [("y_prompt", (NTP, D), (1, NTP, D)), ("y_sample", (NS, D), (NB, TS, D)),
         ("p_ckv", (NTP, KV), (1, 1, NTP, KV)), ("p_kr", (NTP, RA), (1, 1, NTP, RA)),
         ("p_bk", (NTP, 512), (1, 1, NTP, 8, HD)), ("p_bv", (NTP, 512), (1, 1, NTP, 8, HD)),
         ("p_ck", (128, 256), (1, 1, 128, GC, HD)), ("p_cv", (128, 256), (1, 1, 128, GC, HD)),
         ("s_ckv", (NS, KV), (1, NB, TS, KV)), ("s_kr", (NS, RA), (1, NB, TS, RA)),
         ("s_bk", (NS, 512), (1, NB, TS, 8, HD)), ("s_bv", (NS, 512), (1, NB, TS, 8, HD)),
         ("s_ck", (NS, 256), (1, NB, TS, GC, HD)), ("s_cv", (NS, 256), (1, NB, TS, GC, HD))]


def kernel(**inputs):
    import concourse.bacc as bacc
    from concourse.bass_utils import run_bass_kernel_spmd as run

    nc = bacc.Bacc("TRN2", target_bir_lowering=False, num_devices=1)
    arrays, t_in, t_out = {}, {}, {}
    cst, msk = shape_constants()
    for name, a in [(n, inputs[n]) for n in _INS] + [("cst", cst), ("msk", msk)]:
        a = np.ascontiguousarray(a)
        arrays[f"in_{name}"] = a
        t_in[name] = nc.dram_tensor(f"in_{name}", a.shape, mybir.dt.from_np(a.dtype), kind="ExternalInput").ap()
    for name, shape, _ in _OUTS:
        t_out[name] = nc.dram_tensor(f"out_{name}", shape, F32, kind="ExternalOutput").ap()
    build(nc, t_in, t_out)
    r = run(nc, [arrays], core_ids=[0])
    return tuple(r.results[0][f"out_{name}"].reshape(shape) for name, _, shape in _OUTS)
```

```python
from contextlib import ExitStack

import numpy as np
import concourse.bass as bass
from concourse import mybir

F32 = mybir.dt.float32
I32 = mybir.dt.int32
U32 = mybir.dt.uint32
ALU = mybir.AluOpType
ACT = mybir.ActivationFunctionType
AX_X = mybir.AxisListType.X

D, P, KD = 1024, 128, 8
NTP, NB, TS = 256, 8, 4
NS = NB * TS
NT = NTP + NS
TILES = [(0, 128), (128, 128), (256, 32)]
PAST, PAGE = 1024, 128
NPG = PAST // PAGE
QL, KV, NOPE, RA, HA, HD = 384, 256, 64, 32, 8, 64
HC, GC = 16, 4
FD, NE, FE = 2816, 8, 3584
MLA_SCALE = float(NOPE + RA) ** -0.5
HD_SCALE = float(HD) ** -0.5
EPS, NEG = 1e-6, -1e30
THETA = 500000.0
CAP = 144
MAXPASS = -(-NT // CAP)
CX = CAP - P

SLOT = 4096
NSLOT = 4
OSLOT = 14 * 256
BCOLS = 5 * 128

C_ID, C_ONE, C_UP, C_IC, C_I8 = 0, 128, 256, 384, 384 + CAP
C_RA = C_I8 + 8
C_RB = C_RA + 3 * 64
C_CM = C_RB + 3 * 32
C_EPS = C_CM + 128
NCST = C_EPS + 1
M_A, M_B, M_C, M_SB, M_NA, M_NB = 0, 384, 768, 1152, 1152 + BCOLS, 1152 + BCOLS + 256
NMSK = M_NB + 256


def shape_constants():
    f = np.float32
    c = np.zeros((P, NCST), f)
    c[:, C_ID:C_ID + 128] = np.eye(P)
    c[:, C_ONE:C_ONE + 128] = 1
    c[:, C_UP:C_UP + 128] = np.triu(np.ones((P, P)), 1)
    c[:, C_IC:C_IC + CAP] = np.arange(CAP)
    c[:, C_I8:C_I8 + 8] = np.arange(8)
    c[:, C_EPS] = EPS
    pos = [np.arange(128), 128 + np.arange(128), PAST + np.arange(128) % TS]
    for half, at in ((RA // 2, C_RA), (HD // 8, C_RB)):
        inv = f(THETA) ** (-np.arange(half, dtype=f) / f(half))
        for t in range(3):
            ang = pos[t].astype(f)[:, None] * inv.astype(f)[None, :]
            cos, sin = np.cos(ang).astype(f), np.sin(ang).astype(f)
            c[:, at + t * 4 * half:at + (t + 1) * 4 * half] = np.concatenate([cos, cos, -sin, sin], 1)
    r = np.arange(64) % TS
    c[:64, C_CM:C_CM + 128] = np.where(np.arange(128)[None] > r[:, None], 0, NEG)

    def count(dist):
        n = np.zeros(dist.shape)
        for w, d in ((128, 1), (512, 4), (2048, 16)):
            n += (dist >= 0) & (dist <= w) & (dist % d == 0)
        return np.where(n > 0, np.log(np.maximum(n, 1)), NEG)

    m = np.zeros((P, NMSK), f)
    q, k = np.arange(128)[:, None], np.arange(128)[None]
    dist = np.concatenate([q - k, q + 128 - k, q - k], 1)
    m[:, M_A:M_A + 384] = np.where(dist >= 0, 0, NEG)
    m[:, M_B:M_B + 384] = count(dist)
    m[:, M_C:M_C + 384] = np.where((dist >= 0) & (dist < 128), 0, NEG)
    p = np.arange(128)
    keys = np.concatenate([p // 4 * 16 + p % 4] + [512 + 4 * p + i for i in range(4)])
    t = (np.arange(32) % TS)[:, None]
    m[:32, M_SB:M_SB + BCOLS] = count(PAST + t - keys[None])
    kb, kt = np.arange(NS)[None] // TS, np.arange(NS)[None] % TS
    for b in range(NB):
        m[:64, M_NA + 32 * b:M_NA + 32 * b + 32] = np.where((kb == b) & (kt <= r[:, None]), 0, NEG)
        m[:32, M_NB + 32 * b:M_NB + 32 * b + 32] = np.where(kb == b, count(t - kt), NEG)
    return c, m


def ring_plan():
    plan = [("ada0", j, 1) for j in range(12)]
    plan += [("in_ab", j, 1) for j in range(5)]
    plan += [("q_b", 0, 1)]
    u0 = units_of_layer0()
    ada1 = ada1_steps()
    for u in range(-1, len(u0)):
        if u + 1 < len(u0) and u0[u + 1][0] == "Bs":
            plan += [("bk", u0[u + 1][1], 2)]
        elif u + 1 < len(u0) and u0[u + 1][0] == "As":
            plan += [("mla", u0[u + 1][1], 2 * NPG)]
        if u in ada1:
            plan += [("ada1", ada1[u], 1)]
        if u >= 0 and u0[u][0] == "Bs":
            plan += [("bv", u0[u][1], 2)]
    plan += [("out_ab", j, 1) for j in range(2)]
    plan += [("ffd_in", j, 2) for j in range(11)]
    plan += [("ffd_out", j, 1) for j in range(8)]
    plan += [("qkv_c", j, 1) for j in range(3)]
    plan += [("c_cache", 0, 2)]
    plan += [("out_c", j, 4) for j in range(2)]
    at, arrived, total = {}, {}, [0] * NSLOT
    for n, (kind, j, dmas) in enumerate(plan):
        total[n % NSLOT] += 16 * dmas
        at[(kind, j)] = n
        arrived[n] = total[n % NSLOT]
    return plan, at, arrived, total


def units_of_layer0():
    out = []
    for i in range(8):
        out += [("Bs", i), ("Bp", i), ("As", i), ("Ap", i)]
    return out


def ada1_steps():
    u0 = units_of_layer0()
    free = [u for u in range(len(u0) - 1) if u0[u + 1][0] != "As"]
    return {u: j for j, u in enumerate(free[::2][:12])}


def units_of_layer1():
    out = []
    for i in range(8):
        out += [("Cs", i), ("Cp", 2 * i), ("Cp", 2 * i + 1)]
    return out


def build(nc, t_in, t_out):
    plan, at, arrived, ring_total = ring_plan()
    NPLAN = len(plan)
    ada1 = ada1_steps()
    units = units_of_layer0() + units_of_layer1()
    NU0 = len(units_of_layer0())
    NU = len(units)
    rows_of = {"Ap": 128, "Bp": 128, "Cp": 128, "As": 32, "Bs": 32, "Cs": 64}
    ktiles_of = {"As": NPG, "Bs": 5, "Cs": 1}

    ctx = ExitStack()
    with ctx:
        def sb(name, shape, dt=F32):
            return ctx.enter_context(nc.sbuf_tensor(name, shape, dt))

        def sem(name):
            return ctx.enter_context(nc.semaphore(name))

        ring = sb("ring", [P, NSLOT, SLOT])
        mix = sb("mix", [P, 4 * OSLOT])
        xT = sb("xT", [P, KD, NT])
        work = sb("work", [P, 3 * KD * NT])
        z = sb("z", [P, 6624])
        o_or_q = sb("o_or_q", [P, KD * NT])
        rinv_rstd = sb("rinv_rstd", [P, 2 * NT])
        rinv, rstd = rinv_rstd[:, 0:NT], rinv_rstd[:, NT:2 * NT]
        mod = sb("mod", [P, 2, 48, 9])
        coef = sb("coef", [P, 4, KD, 9])
        cst = sb("cst", [P, NCST])
        gqkv = sb("gqkv", [P, QL + KV])
        vecT = sb("vecT", [P, 160])
        csT = sb("csT", [P, KD, 9])
        sinks = sb("sinks", [P, HC])
        nsinks = sb("nsinks", [P, HC])
        sinkr = sb("sinkr", [64, 1])
        nsinkr = sb("nsinkr", [64, 1])
        brout = sb("brout", [P, NE])
        wrout = sb("wrout", [P, KD, NE])
        ptab = sb("ptab", [1, NB * NPG], I32)
        nmax = sb("nmax", [P, 2, 2])
        lsum = sb("lsum", [P, 2, 4])
        rl = sb("rl", [P, 2, 2])
        ss = sb("ss", [P, 3, 6])

        hT = work[:, 0:2304].rearrange("p (k n) -> p k n", k=KD)
        fT = work[:, 2304:4608].rearrange("p (k n) -> p k n", k=KD)
        sq = work[:, 4608:6912].rearrange("p (k n) -> p k n", k=KD)
        qhT = work[0:96, 0:2304].rearrange("p (h n) -> p h n", h=HA)
        qlT = work[:, 2304:6912].rearrange("p (c h n) -> p c h n", c=2, h=HA)
        xtok = z[:, 0:3072].rearrange("p (t n) -> p t n", t=3)
        ctok = z[0:9, 3072:4096]
        cstok = z[0:9, 4096:5120]
        vecA = z[0:96, 5120:5248]
        vecB = z[0:64, 5248:5376]
        z_qk = z[:, 0:3072].rearrange("p (t n) -> p t n", t=3)
        z_v = z[:, 3072:4608].rearrange("p (t n) -> p t n", t=3)
        z_ckv = z[:, 4608:5376].rearrange("p (t n) -> p t n", t=3)
        z_kr = z[:, 5376:5472 + 192].rearrange("p (t n) -> p t n", t=3)
        z_qa = o_or_q[:, 0:1152].rearrange("p (t n) -> p t n", t=3)
        rtmp = o_or_q[:, 1152:2304]
        rtmp2 = z[:, 5664:6624]
        qls = z[:, 5664:6176].rearrange("p (c b n) -> p c b n", c=2, b=NB)
        qhs = z[:, 6176:6432].rearrange("p (b n) -> p b n", b=NB)
        z2 = o_or_q[:, :].rearrange("p (t n) -> p t n", t=3)
        z_c = z[:, 0:4608].rearrange("p (t n) -> p t n", t=3)
        oT = o_or_q[:, :].rearrange("p (k n) -> p k n", k=KD)
        kcT = z[:, 0:3072]
        kcT_c = z[:, 5120:5376].rearrange("p (j n) -> p j n", j=2)
        actd = z[:, 0:22 * NT].rearrange("p (f n) -> p f n", f=22)

        m_at = [0]

        def mixview(n):
            m_at[0] += n
            return mix[:, m_at[0] - n:m_at[0]]

        msk = mixview(NMSK)
        qkT = mixview(4032)
        qT0 = qkT[:, 0:1152].rearrange("p (k n) -> p k n", k=4)
        kT0 = qkT[:, 1152:2304].rearrange("p (k n) -> p k n", k=4)
        ckvT = qkT[:, 2304:2880].rearrange("p (k n) -> p k n", k=2)
        qnT = qkT[:, 2880:3744].rearrange("p (k n) -> p k n", k=3)
        krT = qkT[:, 3744:4032]
        qT1 = qkT[:, 0:2304].rearrange("p (k n) -> p k n", k=8)
        kT1 = qkT[:, 2304:2880].rearrange("p (k n) -> p k n", k=2)
        wukT = mixview(2048).rearrange("p (h c) -> p h c", h=HA)
        kvb = mixview(2048).rearrange("p (c n) -> p c n", c=2)
        scores = mixview(2112).rearrange("p (b n) -> p b n", b=2)
        mrow = [[scores[0:9, 0, 0:512], scores[0:9, 1, 0:512]], [gqkv[0:9, 0:512], rinv_rstd[0:9, 0:512]]]
        probsT = mixview(768).rearrange("p (b n) -> p b n", b=2)
        qbd = mixview(1024)
        qbd0 = qbd.rearrange("p (b j n) -> p b j n", b=NB, j=4)
        qbd1 = qbd.rearrange("p (b j n) -> p b j n", b=NB, j=2)
        oring = mix[:, 0:4 * OSLOT].rearrange("p (s n) -> p s n", s=4)

        acte = z[:, 0:28 * CAP].rearrange("p (f n) -> p f n", f=28)
        hsel = z[:, 28 * CAP:36 * CAP].rearrange("p (k n) -> p k n", k=KD)
        oeT = z[:, 36 * CAP:44 * CAP].rearrange("p (k n) -> p k n", k=KD)
        sil = z[:, 44 * CAP:46 * CAP].rearrange("p (b n) -> p b n", b=2)
        otok = [work[:, 0:D], work[0:CX, D:2 * D]]
        gpl = work[:, 2 * D:2 * D + 2]
        cnt_i = work[0:1, 2 * D + 8:2 * D + 16].bitcast(I32)
        htok = [work[:, 4608:4608 + D], work[:, 4608 + D:4608 + 2 * D], o_or_q[:, 0:D]]
        pick = o_or_q[:, D:D + 3 * CAP].rearrange("p (t n) -> p t n", t=3)
        putT = [o_or_q[:, D + 3 * CAP:D + 3 * CAP + NT], o_or_q[0:CX, D + 3 * CAP + NT:D + 3 * CAP + 2 * NT]]
        rt = o_or_q[:, D + 3 * CAP + 2 * NT:2304]
        logit = rt[:, 0:24].rearrange("p (t n) -> p t n", t=3)
        top = rt[:, 24:48].rearrange("p (t n) -> p t n", t=3)
        topi = rt[:, 48:72].bitcast(U32).rearrange("p (t n) -> p t n", t=3)
        topf = rt[:, 72:78].rearrange("p (t n) -> p t n", t=3)
        gate = rt[:, 84:96].rearrange("p (t n) -> p t n", t=3)
        oh = rt[:, 96:144].rearrange("p (w t n) -> p w t n", w=2, t=3)
        mask = rt[:, 144:168].rearrange("p (t n) -> p t n", t=3)
        gates = rt[:, 168:195].rearrange("p (n t) -> p n t", t=3)
        posm = rt[:, 195:222].rearrange("p (n t) -> p n t", t=3)
        cur = rt[:, 222:228].rearrange("p (w t) -> p w t", w=2)
        pm_t = rt[:, 232:256].rearrange("p (t n) -> p t n", t=3)
        cnt = rt[:, 256:264]
        passes = rt[:, 265:266]
        passes_i = rt[:, 267:268].bitcast(I32)
        silu_d = z[:, 22 * NT:23 * NT]

        ps = ctx.enter_context(nc.psum_tensor("ps", [P, 8 * 512], F32))

        def bank(i, n=512, at_=0, rows=P):
            return ps[0:rows, 512 * i + at_:512 * i + at_ + n]

        ident = cst[:, C_ID:C_ID + 128]
        ones = cst[:, C_ONE:C_ONE + 128]
        iota_c = cst[:, C_IC:C_IC + CAP]

        s_in = [sem(f"ring_in{i}") for i in range(NSLOT)]
        s_ld, s_ldm = sem("loaded"), sem("loaded_vectors")
        s_xload = sem("x_loaded")
        s_pt = sem("page_table_loaded")
        x_tp, x_cp = sem("x_transposed"), sem("x_copied")
        c_silu, c_tp, c_cp = sem("c_silu"), sem("c_transposed"), sem("c_copied")
        sq_done, stat_done, std_done = sem("squares_done"), sem("sums_done"), sem("std_done")
        h_done, x_upd = sem("h_done"), sem("x_updated")
        ada_done, ada_row, ada_tp, ada_add = sem("ada_done"), sem("ada_rows_copied"), sem("ada_transposed"), sem("ada_added")
        z_done, z_cp, z_rdy = sem("z_done"), sem("z_copied"), sem("z_ready")
        t_done, t_cp = sem("mixer_transposes_done"), sem("mixer_transposes_copied")
        q_done, q_cp, q_rope = sem("q_done"), sem("q_copied"), sem("q_roped")
        qn_rdy = sem("qn_ready")
        bd_rdy = sem("block_diagonal_ready")
        kt_tp = [sem("cache_transposed_even"), sem("cache_transposed_odd")]
        kt_cp = [sem("cache_copied_even"), sem("cache_copied_odd")]
        sc_done, sc_cp, mx_done, ex_done, pr_done = (sem("scores_done"), sem("scores_copied"), sem("max_done"),
                                                     sem("exp_done"), sem("probs_done"))
        pt_tp, pt_cp, pv_done, pv_cp = (sem("probs_transposed"), sem("probsT_copied"), sem("pv_done"),
                                        sem("pv_copied"))
        oa_done, oa_cp = sem("oa_done"), sem("oa_copied")
        f_done, f_cp = sem("f_done"), sem("f_copied")
        gu_done, si_done, act_done = sem("gate_up_done"), sem("silu_done"), sem("act_done")
        y_tp, y_cp, s_out = sem("y_transposed"), sem("y_copied"), sem("stored")
        s_out0 = sem("stored_layer0")
        s_out1 = sem("stored_layer1")
        chain_v, chain_a = sem("vector_chain"), sem("scalar_chain")
        htok_tp, htok_cp, lg_done, lg_cp = sem("htok_transposed"), sem("htok_copied"), sem("logits_done"), sem("logits_copied")
        ge_done, msk_done, pos_done, pass_rdy = sem("gate_exp_done"), sem("route_masks_done"), sem("positions_done"), sem("passes_ready")
        e_gu, e_si, e_act = sem("e_gate_up_done"), sem("e_silu_done"), sem("e_act_done")
        e_in, e_used = [sem(f"oring_in{i}") for i in range(4)], sem("oring_used")
        e_half, e_ocp = sem("e_out_first_half_done"), sem("e_out_copied")
        e_tp, e_tcpA, e_tcpV = sem("e_out_transposed"), sem("e_out_tok_copied_act"), sem("e_out_tok_copied_vec")
        e_cb, e_add = sem("combine_done"), sem("combine_added")
        e_pick, e_gat, e_gcpA, e_gcpV = sem("pick_ready"), sem("gathered"), sem("gather_copied_act"), sem("gather_copied_vec")
        e_ptp, e_pcp = sem("put_transposed"), sem("put_copied")
        chain_e = sem("vector_chain_experts")

        def copy_keys(copy, kind, i, b):
            if kind == "As":
                copy(kcT[:, 0:2048].rearrange("p (c n) -> p c n", c=2)[:, :, 128 * i:128 * i + 128],
                     bank(b, 256).rearrange("p (c n) -> p c n", c=2))
                return copy(kcT[64:96, 2048 + 128 * i:2176 + 128 * i], ps[64:96, 512 * b + 256:512 * b + 384])
            if kind == "Bs":
                return copy(kcT[:, 0:2560].rearrange("p (j n) -> p j n", j=4)[:, :, 128 * i:128 * i + 128],
                            bank(b).rearrange("p (j n) -> p j n", j=4))
            return copy(kcT_c, bank(b, 256).rearrange("p (j n) -> p j n", j=2))

        block = ctx.enter_context(nc.Block())

        unit_at = {unit: u for u, unit in enumerate(units)}
        used = []
        for kind, j, _n in plan:
            used.append({
                "ada0": (ada_done, j + 1), "ada1": (ada_done, 13 + j), "in_ab": (z_done, 3 * (j + 1)), "q_b": (q_done, 6),
                "bk": (sc_done, unit_at.get(("Bs", j), 0) + 1),
                "bv": (pv_done, unit_at.get(("Bs", j), 0) + 1),
                "mla": (pv_done, unit_at.get(("As", j), 0) + 1),
                "out_ab": (f_done, 4 * (j + 1)), "ffd_in": (gu_done, 2 * (j + 1)), "ffd_out": (f_done, 9 + j),
                "qkv_c": (z_done, 18 + 3 * j), "c_cache": (pv_done, unit_at["Cs", NB - 1] + 1), "out_c": (f_done, 20 + 4 * j),
            }[kind])

        def slot_of(kind, j):
            return at[(kind, j)] % NSLOT

        def chunk(kind, j, off, n):
            return ring[:, slot_of(kind, j), off:off + n]

        @block.sync
        def _(sp):
            sp.dma_start(xtok[:, 0:2, :], t_in["x_prompt"][0].rearrange("(t p) d -> p t d", p=P)).then_inc(s_xload, 16)
            sp.dma_start(cst[:, :], t_in["cst"][:, :]).then_inc(s_xload, 16)
            sp.dma_start(xtok[0:NS, 2, :], t_in["x_sample"].rearrange("b t d -> (b t) d")).then_inc(s_xload, 16)
            sp.dma_start(ctok[0:1, :], t_in["c_prompt"]).then_inc(s_xload, 16)
            sp.dma_start(ctok[1:9, :], t_in["c_sample"]).then_inc(s_xload, 16)
            sp.dma_start(vecA, t_in["b_ada"].rearrange("l (m p) -> (l m) p", p=P)).then_inc(s_ldm, 16)
            for i, name in enumerate(("g_pre_mix", "g_post_mix", "g_pre_ffn", "g_post_ffn")):
                sp.dma_start(vecB[16 * i:16 * i + 16, :], t_in[name].rearrange("l (m p) -> (l m) p", p=P)).then_inc(s_ldm, 16)

            def free(n):
                if n >= NSLOT:
                    sp.wait_ge(*used[n - NSLOT])

            def ada0():
                w = t_in["w_ada"][0].rearrange("(k p) m -> p k m", p=P)
                for j in range(4):
                    sp.dma_start(chunk("ada0", j, 0, 4096).rearrange("p (k m) -> p k m", k=KD),
                                 w[:, :, 512 * j:512 * j + 512]).then_inc(s_in[j], 16)
                with sp.Fori(1, 3) as i:
                    for q in range(4):
                        sp.wait_ge(ada_done, 4 * i + (q - 3))
                        sp.dma_start(ring[:, q, :].rearrange("p (k m) -> p k m", k=KD),
                                     w[:, :, bass.ds(2048 * i + 512 * q, 512)]).then_inc(s_in[q], 16)

            def put(kind, j):
                n = at[(kind, j)]
                free(n)
                s = s_in[n % NSLOT]
                if kind == "in_ab":
                    c0, w = ((0, 384), (384, 288), (672, 512), (1184, 512), (1696, 512))[j]
                    sp.dma_start(chunk(kind, j, 0, 8 * w).rearrange("p (k m) -> p k m", k=KD),
                                 t_in["w_in_ab"][0].rearrange("(k p) m -> p k m", p=P)[:, :, c0:c0 + w]).then_inc(s, 16)
                elif kind == "ada1":
                    sp.dma_start(chunk(kind, j, 0, 4096).rearrange("p (k m) -> p k m", k=KD),
                                 t_in["w_ada"][1].rearrange("(k p) m -> p k m", p=P)[:, :, 512 * j:512 * j + 512]).then_inc(s, 16)
                elif kind == "q_b":
                    sp.dma_start(chunk(kind, j, 0, 2304).rearrange("p (k m) -> p k m", k=3),
                                 t_in["w_q_b"][0].rearrange("(k p) m -> p k m", p=P)).then_inc(s, 16)
                elif kind in ("bk", "bv"):
                    src = t_in["cache_b_k" if kind == "bk" else "cache_b_v"][0, j].rearrange("s h d -> s (h d)")
                    sp.dma_start(chunk(kind, j, 0, 512),
                                 src[0:512, :].rearrange("(g r) n -> g r n", r=16)[:, 0:4, :]).then_inc(s, 16)
                    sp.dma_start(chunk(kind, j, 512, 2048), src[512:1024, :].rearrange("(p i) n -> p (i n)", i=4)).then_inc(s, 16)
                elif kind == "mla":
                    ck, kr = t_in["cache_mla_ckv"][0], t_in["cache_mla_krope"][0]
                    with sp.Fori(0, NPG) as i:
                        page = sp.value_load(ptab[0:1, bass.ds(NPG * j + i, 1)], min_val=0, max_val=ck.shape[0] - 1)
                        sp.dma_start(ring[:, n % NSLOT, bass.ds(256 * i, 256)],
                                     ck[bass.ds(page, 1), :, :].rearrange("a s c -> (a s) c")).then_inc(s, 16)
                        sp.dma_start(ring[:, n % NSLOT, bass.ds(2048 + 64 + 96 * i, 32)],
                                     kr[bass.ds(page, 1), :, :].rearrange("a s c -> (a s) c")).then_inc(s, 16)
                elif kind == "out_ab":
                    sp.dma_start(chunk(kind, j, 0, 4096).rearrange("p (k m) -> p k m", k=KD),
                                 t_in["w_out_ab"][0].rearrange("(k p) m -> p k m", p=P)[:, :, 512 * j:512 * j + 512]).then_inc(s, 16)
                elif kind == "ffd_in":
                    w = t_in["w_ffd_in"][0].rearrange("(k p) (g m) -> p k g m", p=P, g=2)
                    for g in range(2):
                        sp.dma_start(chunk(kind, j, 2048 * g, 2048).rearrange("p (k m) -> p k m", k=KD),
                                     w[:, :, g, 256 * j:256 * j + 256]).then_inc(s, 16)
                elif kind == "ffd_out":
                    sp.dma_start(chunk(kind, j, 0, 2816).rearrange("p (f m) -> p f m", f=22),
                                 t_in["w_ffd_out"][0].rearrange("(f p) m -> p f m", p=P)[:, :, 128 * j:128 * j + 128]).then_inc(s, 16)
                elif kind == "qkv_c":
                    sp.dma_start(chunk(kind, j, 0, 4096).rearrange("p (k m) -> p k m", k=KD),
                                 t_in["w_qkv_c"][0].rearrange("(k p) m -> p k m", p=P)[:, :, 512 * j:512 * j + 512]).then_inc(s, 16)
                elif kind == "c_cache":
                    for w, name in enumerate(("cache_c_k", "cache_c_v")):
                        sp.dma_start(chunk(kind, j, 2048 * w, 2048).rearrange("p (b n) -> p b n", b=NB),
                                     t_in[name][0].rearrange("b s h d -> s b (h d)")).then_inc(s, 16)
                elif kind == "out_c":
                    w = t_in["w_out_c"][0].rearrange("(b r d) m -> b d r m", r=4, d=64)
                    for a in range(2):
                        for jj in range(2):
                            sp.dma_start(ring[64 * a:64 * a + 64, n % NSLOT, 2048 * jj:2048 * jj + 2048].rearrange("p (r m) -> p r m", r=4),
                                         w[2 * jj + a, :, :, 512 * j:512 * j + 512]).then_inc(s, 16)

            ada0()
            sp.wait_ge(s_pt, 16)
            for kind, j, _n in plan[12:]:
                put(kind, j)

            wi = t_in["w_moe_in"][0].rearrange("e (k p) m -> p e k m", p=P)
            wo = t_in["w_moe_out"][0].rearrange("e (f p) m -> p e f m", p=P)

            def expert_loads(it, i, half):
                e = 2 * i + half

                def put_in(j):
                    c = 14 * half + j
                    sl = (NPLAN + c) % NSLOT
                    sp.wait_ge(e_gu, 56 * it + (2 * c + 2))
                    for g in range(2):
                        src = wi[:, bass.ds(e, 1), :, g * FE + 256 * j:g * FE + 256 * j + 256].rearrange("p a k m -> p (a k) m")
                        sp.dma_start(ring[:, sl, 2048 * g:2048 * g + 2048].rearrange("p (k m) -> p k m", k=KD),
                                     src).then_inc(s_in[sl], 16)

                def put_out(q):
                    sp.wait_ge(e_used, 16 * it + (8 * half + q + 1))
                    src = wo[:, bass.ds(e, 1), 14 * (q % 2):14 * (q % 2) + 14, 256 * (q // 2):256 * (q // 2) + 256]
                    sp.dma_start(oring[:, q % 4, :].rearrange("p (f m) -> p f m", f=14),
                                 src.rearrange("p a f m -> p (a f) m")).then_inc(e_in[q % 4], 16)

                for j in range(4):
                    put_in(j)
                for q in range(4):
                    put_out(q)
                for j in range(4, 14):
                    put_in(j)
                for q in range(4, 8):
                    put_out(q)

            def pass_body(it0):
                with sp.Fori(0, NE // 2) as i:
                    for half in range(2):
                        expert_loads(it0 + i, i, half)

            pass_body(0)
            sp.wait_ge(pass_rdy, 1)
            npass = sp.value_load(passes_i[0:1, :], min_val=1, max_val=MAXPASS)
            with sp.If(npass > 1):
                with sp.Fori(1, npass) as p_:
                    pass_body(4 * p_)

        @block.gpsimd
        def _(gp):
            gp.dma_start(ptab[:, :], t_in["page_table"].rearrange("b g -> (b g)").rearrange("(a n) -> a n", a=1)).then_inc(s_pt, 16)
            gp.dma_start(gqkv[:, 0:QL], t_in["g_q_a"].broadcast_to([P, QL])).then_inc(s_ld, 16)
            gp.dma_start(gqkv[:, QL:QL + KV], t_in["g_kv_a"].broadcast_to([P, KV])).then_inc(s_ld, 16)
            gp.dma_start(sinks[:, :], t_in["sinks_c"].broadcast_to([P, HC])).then_inc(s_ld, 16)
            gp.dma_start(brout[:, :], t_in["b_router"].broadcast_to([P, NE])).then_inc(s_ld, 16)
            with nc.allow_non_contiguous_dma(reason="64 single values"):
                gp.dma_start(sinkr[:, :], t_in["sinks_c"].rearrange("a (h o) -> h a o", o=1).broadcast_to([HC, TS, 1])).then_inc(s_ld, 16)
            gp.dma_start(wrout[:, :, :], t_in["w_router"][0].rearrange("(k p) e -> p k e", p=P)).then_inc(s_ld, 16)
            gp.dma_start(kvb[:, :, :], t_in["w_kv_b"][0].rearrange("(c p) h n -> p c (h n)", p=P)).then_inc(s_ld, 16)
            gp.dma_start(msk, t_in["msk"][:, :]).then_inc(s_ld, 16)

            def store(dst, src, s):
                gp.dma_start(dst, src).then_inc(s, 16)

            gp.wait_ge(z_rdy, 5)
            gp.wait_ge(z_cp, 15)
            store(t_out["p_ckv"].rearrange("(t p) c -> p t c", p=P), z_ckv[:, 0:2, :], s_out0)
            store(t_out["p_kr"].rearrange("(t p) c -> p t c", p=P), z_kr[:, 0:2, 64:96], s_out0)
            store(t_out["p_bk"].rearrange("(t p) c -> p t c", p=P), z_qk[:, 0:2, 512:1024], s_out0)
            store(t_out["p_bv"].rearrange("(t p) c -> p t c", p=P), z_v[:, 0:2, :], s_out0)
            store(t_out["s_ckv"][:, :], z_ckv[0:NS, 2, :], s_out0)
            store(t_out["s_kr"][:, :], z_kr[0:NS, 2, 64:96], s_out0)
            store(t_out["s_bk"][:, :], z_qk[0:NS, 2, 512:1024], s_out0)
            store(t_out["s_bv"][:, :], z_v[0:NS, 2, :], s_out0)
            gp.wait_ge(z_rdy, 8)
            gp.wait_ge(z_cp, 24)
            store(t_out["p_ck"][:, :], z_c[:, 1, 1024:1280], s_out1)
            store(t_out["p_cv"][:, :], z_c[:, 1, 1280:1536], s_out1)
            store(t_out["s_ck"][:, :], z_c[0:NS, 2, 1024:1280], s_out1)
            store(t_out["s_cv"][:, :], z_c[0:NS, 2, 1280:1536], s_out1)
            gp.wait_ge(y_cp, 6)
            for t in range(2):
                store(t_out["y_prompt"][128 * t:128 * t + 128, :], htok[t], s_out)
            store(t_out["y_sample"][:, :], htok[2][0:NS, :], s_out)
            gp.wait_ge(s_out0, 8 * 16)
            gp.wait_ge(s_out1, 4 * 16)
            gp.wait_ge(s_out, 3 * 16)

        @block.tensor
        def _(pe):
            mm, tp = nc.tensor.matmul, nc.tensor.transpose

            def landed(kind, j):
                n = at[(kind, j)]
                pe.wait_ge(s_in[n % NSLOT], arrived[n])

            def sums(n):
                for k in range(KD):
                    pe.wait_ge(sq_done, 8 * n + k + 1)
                    last = mm(bank(7, NT), ones, sq[:, k, :], start=(k == 0), stop=(k == KD - 1))
                last.then_inc(stat_done, 1)

            def ada_rows(w, b, before_last=None):
                for k in range(KD):
                    if k == KD - 1 and before_last:
                        before_last()
                    last = mm(bank(b, 512, 0, 9), csT[:, k, :], w[:, k, :], start=(k == 0), stop=(k == KD - 1))
                last.then_inc(ada_done, 1)

            def ada0():
                def can_turn(i, q, first):
                    pe.wait_ge(ada_row, 4 * i + (q + 1))
                    if q >= 2 or not first:
                        pe.wait_ge(ada_add, 4 * i + (q - 1))

                def turn(q):
                    for m in range(4):
                        last = tp(bank(6 + q % 2, 9, 9 * m), mrow[0][q % 2][:, 128 * m:128 * m + 128], ident[0:9, 0:9])
                    last.then_inc(ada_tp, 1)

                def round_(i, first):
                    for q in range(4):
                        pe.wait_ge(s_in[q], 16 * i + 16)
                        if q >= 2 or not first:
                            pe.wait_ge(ada_row, 4 * i + (q - 1))
                        w = ring[:, q, :].rearrange("p (k m) -> p k m", k=KD)
                        if first and q == 0:
                            ada_rows(w, 4)
                            continue
                        before = (i, q - 1, first) if q else (i - 1, 3, False)
                        ada_rows(w, 4 + q % 2, lambda: can_turn(*before))
                        turn((q - 1) % 4)

                round_(0, True)
                with pe.Fori(1, 3) as i:
                    round_(i, False)
                can_turn(2, 3, False)
                turn(3)

            def linear_out(L, kind, per, nk, rhs):
                for k in range(KD):
                    j, m = k // per, k % per
                    if m == 0:
                        landed(kind, j)
                    if L or k >= 2:
                        pe.wait_ge(f_cp, 8 * L + k - 1)
                    w = chunk(kind, j, 0, nk * per * 128).rearrange("p (f m) -> p f m", f=nk)
                    for f in range(nk):
                        last = mm(bank(4 + k % 2, NT), w[:, f, 128 * m:128 * m + 128], rhs[:, f, :],
                                  start=(f == 0), stop=(f == nk - 1))
                    last.then_inc(f_done, 1)

            pe.wait_ge(s_xload, 5 * 16)
            for k in range(KD):
                if k >= 2:
                    pe.wait_ge(x_cp, k - 1)
                for t, (t0, n) in enumerate(TILES):
                    last = tp(bank(k % 2, n, t0), xtok[0:n, t, 128 * k:128 * k + 128], ident[0:n, 0:n])
                last.then_inc(x_tp, 1)
            pe.wait_ge(c_silu, 1)
            for k in range(KD):
                last = tp(bank(2, 9, 9 * k), cstok[:, 128 * k:128 * k + 128], ident[0:9, 0:9])
            pe.wait_ge(s_ldm, 5 * 16)
            tp(bank(3, 96), vecA, ident[0:96, 0:96])
            tp(bank(3, 64, 96), vecB, ident[0:64, 0:64]).then_inc(c_tp, 1)
            sums(0)
            pe.wait_ge(c_cp, 1)
            ada0()

            nz = 0
            pe.wait_ge(s_ld, 8 * 16)
            pe.wait_ge(h_done, 9)
            for j, w in enumerate((384, 288, 512, 512, 512)):
                landed("in_ab", j)
                wt = chunk("in_ab", j, 0, 8 * w).rearrange("p (k m) -> p k m", k=KD)
                for t, (t0, n) in enumerate(TILES):
                    if nz >= 4:
                        pe.wait_ge(z_cp, nz - 3)
                    for k in range(KD):
                        last = mm(bank(nz % 4, w, 0, n), hT[:, k, t0:t0 + n], wt[:, k, :], start=(k == 0), stop=(k == KD - 1))
                    last.then_inc(z_done, 1)
                    nz += 1
            nt = 0

            def t_bank():
                if nt >= 2:
                    pe.wait_ge(t_cp, nt - 1)
                return 4 + nt % 2

            for hp in range(4):
                b = t_bank()
                for q in range(4):
                    h, c = 2 * hp + q // 2, q % 2
                    last = tp(bank(b, 128, 128 * q, 64), kvb[:, c, 128 * h:128 * h + 64], ident)
                last.then_inc(t_done, 1)
                nt += 1

            def tp_tiles(src, m):
                nonlocal nt
                b = t_bank()
                for t, (t0, n) in enumerate(TILES):
                    last = tp(bank(b, n, t0, m), src(t, n), ident[0:n, 0:n])
                last.then_inc(t_done, 1)
                nt += 1

            pe.wait_ge(z_rdy, 1)
            for k in range(3):
                tp_tiles(lambda t, n: z_qa[0:n, t, 128 * k:128 * k + 128], 128)
            pe.wait_ge(z_rdy, 2)
            for k in range(2):
                tp_tiles(lambda t, n: z_ckv[0:n, t, 128 * k:128 * k + 128], 128)
            tp_tiles(lambda t, n: z_kr[0:n, t, :], 96)
            landed("q_b", 0)
            pe.wait_ge(t_cp, 7)
            wt = chunk("q_b", 0, 0, 2304).rearrange("p (k m) -> p k m", k=3)
            for t, (t0, n) in enumerate(TILES):
                for hh in range(2):
                    i = 2 * t + hh
                    pe.wait_ge(z_cp, 15)
                    if i >= 4:
                        pe.wait_ge(q_cp, i - 3)
                    for k in range(3):
                        last = mm(bank(i % 4, 384, 0, n), qnT[:, k, t0:t0 + n], wt[:, k, 384 * hh:384 * hh + 384],
                                  start=(k == 0), stop=(k == 2))
                    last.then_inc(q_done, 1)
            pe.wait_ge(z_rdy, 5)
            for k in range(8):
                tp_tiles(lambda t, n: z_qk[0:n, t, 128 * k:128 * k + 128], 128)
            pe.wait_ge(q_rope, 3)
            for h in range(HA):
                tp_tiles(lambda t, n: z2[0:n, t, 96 * h:96 * h + 96], 96)
            pe.wait_ge(t_cp, nt)
            for h in range(HA):
                for c in range(2):
                    b = t_bank()
                    mm(bank(b, NT), wukT[0:64, h, 128 * c:128 * c + 128], qhT[0:64, h, :], start=True, stop=True).then_inc(t_done, 1)
                    nt += 1
            pe.wait_ge(t_cp, nt)
            pe.wait_ge(bd_rdy, 1)
            kt_n = [0, 0]

            def cache_tiles(u):
                kind, b = units[u]
                if kind not in ktiles_of:
                    return
                if kind == "As":
                    landed("mla", b)
                elif kind == "Bs":
                    landed("bk", b)
                elif b == 0:
                    landed("c_cache", 0)
                for i in range(ktiles_of[kind]):
                    par = i % 2
                    bk = 7 - par
                    if kt_n[par]:
                        pe.wait_ge(kt_cp[par], kt_n[par])
                    if kind == "As":
                        for c in range(2):
                            tp(bank(bk, 128, 128 * c), chunk("mla", b, 256 * i + 128 * c, 128), ident)
                        last = tp(bank(bk, 128, 256, 96), chunk("mla", b, 2048 + 96 * i, 96), ident)
                    elif kind == "Bs":
                        for j in range(4):
                            last = tp(bank(bk, 128, 128 * j), chunk("bk", b, 512 * i + 128 * j, 128), ident)
                    else:
                        for j in range(2):
                            last = tp(bank(bk, 128, 128 * j), chunk("c_cache", 0, 256 * b + 128 * j, 128), ident)
                    last.then_inc(kt_tp[par], 1)
                    kt_n[par] += 1
                for par in range(2):
                    if kt_n[par]:
                        pe.wait_ge(kt_cp[par], kt_n[par])

            def unit_scores(u):
                kind, i = units[u]
                if u:
                    pe.wait_ge(sc_cp, u)
                if kind in ("Ap", "Bp", "Cp"):
                    for qt, (c0, nk) in enumerate(((0, 128), (128, 256))):
                        q0 = 128 * qt
                        out = bank(0, nk, c0)
                        if kind == "Ap":
                            mm(out, qlT[:, 0, i, q0:q0 + 128], ckvT[:, 0, 0:nk], start=True, stop=False)
                            mm(out, qlT[:, 1, i, q0:q0 + 128], ckvT[:, 1, 0:nk], start=False, stop=False)
                            last = mm(out, qhT[64:96, i, q0:q0 + 128], krT[64:96, 0:nk], start=False, stop=True)
                        elif kind == "Bp":
                            r = 64 * (i % 2)
                            last = mm(out, qT0[r:r + 64, i // 2, q0:q0 + 128], kT0[r:r + 64, i // 2, 0:nk], start=True, stop=True)
                        else:
                            g = i // 4
                            r = 64 * (g % 2)
                            last = mm(out, qT1[r:r + 64, 4 * (g // 2) + i % 4, q0:q0 + 128], kT1[r:r + 64, g // 2, 0:nk],
                                      start=True, stop=True)
                elif kind == "As":
                    keys = kcT[:, 0:2048].rearrange("p (c n) -> p c n", c=2)
                    kr = kcT[64:96, 2048:3072]
                    parts = [(0, 512, keys, kr, 0), (1, 512, keys, kr, 512), (2, 32, ckvT, krT[64:96, :], NTP)]
                    for b, n, kk, rr, k0 in parts:
                        for c in range(2):
                            mm(bank(b, n, 0, 32), qls[:, c, i, :], kk[:, c, k0:k0 + n], start=(c == 0), stop=False)
                        last = mm(bank(b, n, 0, 32), qhs[64:96, i, :], rr[:, k0:k0 + n], start=False, stop=True)
                elif kind == "Bs":
                    keys = kcT[:, 0:2560].rearrange("p (j n) -> p j n", j=4)
                    for b, c0, n, kk, k0 in ((0, 0, 512, keys, 0), (1, 0, 128, keys, 512), (1, 128, 32, kT0, NTP)):
                        for j in range(4):
                            last = mm(bank(b, n, c0, 32), qbd0[:, i, j, :], kk[:, j, k0:k0 + n], start=(j == 0), stop=(j == 3))
                else:
                    keys = kcT_c
                    for c0, n, kk, k0 in ((0, 128, keys, 0), (128, 32, kT1, NTP)):
                        for j in range(2):
                            last = mm(bank(0, n, c0, 64), qbd1[:, i, j, :], kk[:, j, k0:k0 + n], start=(j == 0), stop=(j == 1))
                last.then_inc(sc_done, 1)

            def unit_transposes(u):
                kind, i = units[u]
                n = rows_of[kind]
                pe.wait_ge(pr_done, u + 1)
                if u >= 2:
                    pe.wait_ge(pt_cp, u - 1)
                b = 3 + u % 2
                sc = scores[:, u % 2, :]
                if n == 128:
                    for q in range(3):
                        last = tp(bank(b, 128, 128 * (q if q == 0 else 1 + (q - 1))), sc[:, 128 * q:128 * q + 128], ident)
                else:
                    nk = ktiles_of[kind]
                    for q in range(nk):
                        last = tp(bank(b, n, n * q), sc[0:n, 128 * q:128 * q + 128], ident[0:n, 0:n])
                    last = tp(bank(b, n, n * nk, 32), sc[0:n, 128 * nk:128 * nk + 32], ident[0:n, 0:n])
                last.then_inc(pt_tp, 1)

            def unit_pv(u):
                kind, i = units[u]
                pe.wait_ge(pt_cp, u + 1)
                if u:
                    pe.wait_ge(pv_cp, u)
                pT = probsT[:, u % 2, :]
                if kind == "Ap":
                    for c in range(2):
                        v0, v1 = z_ckv[:, 0, 128 * c:128 * c + 128], z_ckv[:, 1, 128 * c:128 * c + 128]
                        mm(bank(5, 128, 256 * c), v0, pT[:, 0:128], start=True, stop=True)
                        mm(bank(5, 128, 256 * c + 128), v0, pT[:, 128:256], start=True, stop=False)
                        last = mm(bank(5, 128, 256 * c + 128), v1, pT[:, 256:384], start=False, stop=True)
                elif kind in ("Bp", "Cp"):
                    if kind == "Bp":
                        r, v0, vv = 64 * (i % 2), 64 * i, z_v
                    else:
                        r, v0, vv = 64 * (i // 4 % 2), 1280 + 64 * (i // 4), z_c
                    out = ps[r:r + 64, 5 * 512:5 * 512 + 256]
                    mm(out[:, 0:128], vv[:, 0, v0:v0 + 64], pT[:, 0:128], start=True, stop=True)
                    mm(out[:, 128:256], vv[:, 0, v0:v0 + 64], pT[:, 128:256], start=True, stop=False)
                    last = mm(out[:, 128:256], vv[:, 1, v0:v0 + 64], pT[:, 256:384], start=False, stop=True)
                elif kind == "As":
                    for c in range(2):
                        for q in range(NPG):
                            mm(bank(5, 32, 32 * c), chunk("mla", i, 256 * q + 128 * c, 128), pT[:, 32 * q:32 * q + 32],
                               start=(q == 0), stop=False)
                        last = mm(bank(5, 32, 32 * c), z_ckv[0:32, 2, 128 * c:128 * c + 128], pT[0:32, 256:288], start=False, stop=True)
                elif kind == "Bs":
                    landed("bv", i)
                    for j in range(4):
                        for q in range(5):
                            mm(bank(5, 32, 32 * j), chunk("bv", i, 512 * q + 128 * j, 128), pT[:, 32 * q:32 * q + 32],
                               start=(q == 0), stop=False)
                        last = mm(bank(5, 32, 32 * j), z_v[0:32, 2, 128 * j:128 * j + 128], pT[0:32, 160:192], start=False, stop=True)
                else:
                    for j in range(2):
                        mm(bank(5, 64, 64 * j), chunk("c_cache", 0, 2048 + 256 * i + 128 * j, 128), pT[:, 0:64], start=True, stop=False)
                        last = mm(bank(5, 64, 64 * j), z_c[0:32, 2, 1280 + 128 * j:1408 + 128 * j], pT[0:32, 64:128],
                                  start=False, stop=True)
                last.then_inc(pv_done, 1)

            def ada1_rows(j):
                landed("ada1", j)
                if j:
                    pe.wait_ge(ada_add, 12 + j)
                ada_rows(chunk("ada1", j, 0, 4096).rearrange("p (k m) -> p k m", k=KD), 2)

            def ada1_turn(j):
                pe.wait_ge(ada_row, 13 + j)
                for m in range(4):
                    last = tp(bank(2, 9, 9 * m), mrow[1][j % 2][:, 128 * m:128 * m + 128], ident[0:9, 0:9])
                last.then_inc(ada_tp, 1)

            def attention(u0, u1):
                cache_tiles(u0)
                unit_scores(u0)
                for u in range(u0, u1):
                    if u + 1 < u1:
                        cache_tiles(u + 1)
                        unit_scores(u + 1)
                    if u in ada1:
                        pe.wait_ge(sc_cp, u + 1)
                        ada1_rows(ada1[u])
                    unit_transposes(u)
                    unit_pv(u)
                    if u in ada1:
                        ada1_turn(ada1[u])

            attention(0, NU0)
            pe.wait_ge(pv_cp, NU0)
            for h in range(HA):
                if h >= 2:
                    pe.wait_ge(oa_cp, h - 1)
                r = 64 * (h % 2)
                for c in range(2):
                    last = mm(ps[r:r + 64, 512 * (h % 2):512 * (h % 2) + NT], kvb[:, c, 128 * h + 64:128 * h + 128],
                              qlT[:, c, h, :], start=(c == 0), stop=(c == 1))
                last.then_inc(oa_done, 1)
            pe.wait_ge(oa_cp, 8)
            linear_out(0, "out_ab", 4, KD, oT)
            sums(1)
            sums(2)
            pe.wait_ge(h_done, 18)
            for j in range(11):
                landed("ffd_in", j)
                w = chunk("ffd_in", j, 0, 4096).rearrange("p (g k m) -> p g k m", g=2, k=KD)
                for fb in range(2):
                    f = 2 * j + fb
                    if f >= 2:
                        pe.wait_ge(act_done, f - 1)
                    for g in range(2):
                        for k in range(KD):
                            last = mm(bank(2 * (f % 2) + g, NT), w[:, g, k, 128 * fb:128 * fb + 128], hT[:, k, :],
                                      start=(k == 0), stop=(k == KD - 1))
                    last.then_inc(gu_done, 1)
            pe.wait_ge(act_done, 22)
            linear_out(1, "ffd_out", 1, 22, actd)
            sums(3)
            sums(4)
            pe.wait_ge(h_done, 27)
            for j in range(3):
                landed("qkv_c", j)
                wt = chunk("qkv_c", j, 0, 4096).rearrange("p (k m) -> p k m", k=KD)
                for t, (t0, n) in enumerate(TILES):
                    if nz >= 19:
                        pe.wait_ge(z_cp, nz - 3)
                    for k in range(KD):
                        last = mm(bank(nz % 4, 512, 0, n), hT[:, k, t0:t0 + n], wt[:, k, :], start=(k == 0), stop=(k == KD - 1))
                    last.then_inc(z_done, 1)
                    nz += 1
            mm(bank(7, 4), ident, ones[:, 0:4], start=True, stop=True).then_inc(e_gu, 2)
            pe.wait_ge(z_rdy, 8)
            for k in range(8):
                tp_tiles(lambda t, n: z_c[0:n, t, 128 * k:128 * k + 128], 128)
            for k in range(2):
                tp_tiles(lambda t, n: z_c[0:n, t, 1024 + 128 * k:1152 + 128 * k], 128)
            pe.wait_ge(t_cp, nt)
            pe.wait_ge(bd_rdy, 2)
            attention(NU0, NU)
            pe.wait_ge(pv_cp, NU)
            mm(bank(3, 4), ident, ones[:, 0:4], start=True, stop=True).then_inc(e_used, 4)
            mm(bank(3, 4), ident, ones[:, 0:4], start=True, stop=True).then_inc(e_gu, 2)
            linear_out(2, "out_c", 4, KD, oT)
            mm(bank(3, 4), ident, ones[:, 0:4], start=True, stop=True).then_inc(e_gu, 4)
            sums(5)
            sums(6)

            pe.wait_ge(h_done, 36)
            for t, (t0, n) in enumerate(TILES):
                for k in range(KD):
                    last = mm(bank(0, 8, 8 * t, n), hT[:, k, t0:t0 + n], wrout[:, k, :], start=(k == 0), stop=(k == KD - 1))
            last.then_inc(lg_done, 1)
            for t, (t0, n) in enumerate(TILES):
                for kk in range(2):
                    i = 2 * t + kk
                    if i >= 2:
                        pe.wait_ge(htok_cp, i - 1)
                    for k in range(4):
                        last = tp(bank(4 + i % 2, 128, 128 * k, n), hT[:, 4 * kk + k, t0:t0 + n], ident)
                    last.then_inc(htok_tp, 1)
            pe.wait_ge(msk_done, 1)
            for t in range(3):
                for tt in range(t + 1):
                    last = mm(bank(1, 8, 8 * t), cst[:, C_UP:C_UP + 128] if tt == t else ones, mask[:, tt, :],
                              start=(tt == 0), stop=(tt == t))
            for tt in range(3):
                last = mm(bank(1, 8, 24), ones, mask[:, tt, :], start=(tt == 0), stop=(tt == 2))
            last.then_inc(pos_done, 1)

            def gather(idx):
                pe.wait_ge(e_pick, idx)
                for k in range(KD):
                    for t, (t0, n) in enumerate(TILES):
                        last = mm(bank(k // 3, CAP, CAP * (k % 3)), htok[t][0:n, 128 * k:128 * k + 128], pick[0:n, t, :],
                                  start=(t == 0), stop=(t == 2))
                last.then_inc(e_gat, 1)

            def turn_choice(adds):
                pe.wait_ge(e_add, adds)
                for w, (c0, c) in enumerate(((0, P), (P, CX))):
                    for t, (t0, n) in enumerate(TILES):
                        tp(bank(6 + w, n, t0, c), pick[0:n, t, c0:c0 + c], ident[0:n, 0:n])
                    for t, (t0, n) in enumerate(TILES):
                        last = mm(bank(6 + w, 1, 300, c), pick[0:n, t, c0:c0 + c], cur[0:n, 1, t:t + 1], start=(t == 0), stop=(t == 2))
                last.then_inc(e_ptp, 1)

            def ffn_in(it, half, rows):
                for j in range(14):
                    c = 14 * half + j
                    sl = (NPLAN + c) % NSLOT
                    times = sum(1 for q in range(c + 1) if q % NSLOT == c % NSLOT)
                    pe.wait_ge(s_in[sl], 224 * it + (ring_total[sl] + 32 * times))
                    w = ring[:, sl, :].rearrange("p (g k m) -> p g k m", g=2, k=KD)
                    for fb in range(2):
                        f = 2 * j + fb
                        pe.wait_ge(e_act, 56 * it + (28 * half + f + 1))
                        for g in range(2):
                            for k in range(KD):
                                last = mm(bank(f % 4, rows, CAP * g), w[:, g, k, 128 * fb:128 * fb + 128], hsel[:, k, 0:rows],
                                          start=(k == 0), stop=(k == KD - 1))
                        last.then_inc(e_gu, 1)
                    if j == 6:
                        turn_choice(16 * it + (8 * half + 2))

            def ffn_out(it, half, rows):
                for q in range(8):
                    pr, f2 = q // 2, q % 2
                    pe.wait_ge(e_in[q % 4], 64 * it + (32 * half + 16 * (q // 4) + 16))
                    pe.wait_ge(e_act, 56 * it + (28 * half + 14 * f2 + 14 + 4))
                    w = oring[:, q % 4, :].rearrange("p (f m) -> p f m", f=14)
                    for m in range(2):
                        if f2 == 0 and pr:
                            pe.wait_ge(e_ocp, 16 * it + (8 * half + 2 * pr + m - 1))
                        for f in range(14):
                            last = mm(bank(4 + m, rows), w[:, f, 128 * m:128 * m + 128], acte[:, 14 * f2 + f, 0:rows],
                                      start=(f2 == 0 and f == 0), stop=(f2 == 1 and f == 13))
                        if f2 == 1 and m == 0:
                            last.then_inc(e_half, 1)
                    last.then_inc(e_used, 1)

            def out_transposes(it, half):
                pe.wait_ge(e_ocp, 16 * it + (8 * half + 8))
                pe.wait_ge(e_pcp, 2 * it + (half + 1))
                for k in range(KD):
                    tp(bank(6 + k // 4, 128, 128 * (k % 4)), oeT[:, k, 0:P], ident)
                    last = tp(bank(3 + 2 * (k // 4), 128, 128 * (k % 4), CX), oeT[:, k, P:CAP], ident)
                last.then_inc(e_tp, 1)

            def combine(it, half, wide):
                pe.wait_ge(e_tcpA, 4 * it + (2 * half + 2))
                pe.wait_ge(e_tcpV, 4 * it + (2 * half + 2))
                for k in range(KD):
                    pe.wait_ge(e_add, 16 * it + (8 * half + k + 1))
                    last = mm(bank(6 + k % 2, NT), otok[0][:, 128 * k:128 * k + 128], putT[0], start=True, stop=not wide)
                    if wide:
                        last = mm(bank(6 + k % 2, NT), otok[1][:, 128 * k:128 * k + 128], putT[1], start=False, stop=True)
                    last.then_inc(e_cb, 1)

            def expert(it, i, p_, half):
                pe.wait_ge(e_gcpA, 2 * it + p_ + (half + 1))
                pe.wait_ge(e_gcpV, 2 * it + p_ + (half + 1))
                wide = pe.value_load(cnt_i[0:1, bass.ds(2 * i + half, 1)], min_val=0, max_val=NT) > p_ * CAP + P

                def body(rows):
                    ffn_in(it, half, rows)
                    ffn_out(it, half, rows)
                    gather(2 * it + p_ + (half + 2))
                    out_transposes(it, half)
                    combine(it, half, rows > P)

                with pe.If(wide):
                    body(CAP)
                with pe.Else():
                    body(P)

            def pass_body(it0, p_):
                with pe.Fori(0, NE // 2) as i:
                    for half in range(2):
                        expert(it0 + i, i, p_, half)

            pe.wait_ge(pass_rdy, 1)
            gather(1)
            pass_body(0, 0)
            npass = pe.value_load(passes_i[0:1, :], min_val=1, max_val=MAXPASS)
            with pe.If(npass > 1):
                with pe.Fori(1, npass) as p_:
                    gather(9 * p_ + 1)
                    pass_body(4 * p_, p_)
            pe.wait_ge(e_add, 64 * npass + 2)
            sums(7)
            pe.wait_ge(x_upd, 32)
            for t, (t0, n) in enumerate(TILES):
                for kk in range(2):
                    i = 2 * t + kk
                    if i >= 2:
                        pe.wait_ge(y_cp, i - 1)
                    for k in range(4):
                        last = tp(bank(i % 2, 128, 128 * k, n), xT[:, 4 * kk + k, t0:t0 + n], ident)
                    last.then_inc(y_tp, 1)

        @block.scalar
        def _(act):
            na = [0]

            def link(ins):
                na[0] += 1
                ins.then_inc(chain_a, 1)
                act.wait_ge(chain_a, na[0])

            def fn(out, in_, f, **kw):
                return nc.scalar.activation(out, in_, f, **kw)

            def std(n):
                act.wait_ge(stat_done, n + 1)
                fn(rstd[:, :], bank(7, NT), ACT.Sqrt, scale=1.0 / D, bias=cst[:, C_EPS:C_EPS + 1]).then_inc(std_done, 1)

            def f_out(L, n):
                for k in range(KD):
                    act.wait_ge(f_done, 8 * L + k + 1)
                    fn(sq[:, k, :], bank(4 + k % 2, NT), ACT.Square).then_inc(sq_done, 1)
                    fn(fT[:, k, :], bank(4 + k % 2, NT), ACT.Copy).then_inc(f_cp, 1)
                std(n)

            def x_squares(m):
                for k in range(KD):
                    act.wait_ge(x_upd, 8 * m + k + 1)
                    fn(sq[:, k, :], xT[:, k, :], ACT.Square).then_inc(sq_done, 1)
                std(2 * m + 2)

            act.wait_ge(s_xload, 5 * 16)
            fn(cstok, ctok, ACT.Silu).then_inc(c_silu, 1)
            for k in range(KD):
                act.wait_ge(x_tp, k + 1)
                fn(sq[:, k, :], bank(k % 2, NT), ACT.Square).then_inc(sq_done, 1)
                fn(xT[:, k, :], bank(k % 2, NT), ACT.Copy).then_inc(x_cp, 1)
            std(0)
            for j in range(12):
                act.wait_ge(ada_done, j + 1)
                if j >= 2:
                    act.wait_ge(ada_tp, j - 1)
                fn(mrow[0][j % 2], bank(4 + j % 2, 512, 0, 9), ACT.Copy).then_inc(ada_row, 1)

            nz = 0
            for j, w in enumerate((384, 288, 512, 512, 512)):
                for t, (t0, n) in enumerate(TILES):
                    act.wait_ge(z_done, nz + 1)
                    b = nz % 4
                    if j == 0:
                        fn(z_qa[0:n, t, :], bank(b, 384, 0, n), ACT.Copy)
                        fn(bank(b, 384, 0, n), bank(b, 384, 0, n), ACT.Square, accum_out=ss[0:n, t, 0:1]).then_inc(z_cp, 1)
                    elif j == 1:
                        fn(z_ckv[0:n, t, :], bank(b, 256, 0, n), ACT.Copy)
                        fn(z_kr[0:n, t, 64:96], bank(b, 32, 256, n), ACT.Copy)
                        fn(bank(b, 256, 0, n), bank(b, 256, 0, n), ACT.Square, accum_out=ss[0:n, t, 1:2]).then_inc(z_cp, 1)
                    elif j < 4:
                        fn(z_qk[0:n, t, 512 * (j - 2):512 * (j - 1)], bank(b, 512, 0, n), ACT.Copy).then_inc(z_cp, 1)
                    else:
                        fn(z_v[0:n, t, :], bank(b, 512, 0, n), ACT.Copy).then_inc(z_cp, 1)
                    nz += 1
                if j < 2:
                    act.wait_ge(z_cp, nz)
                    for t, (t0, n) in enumerate(TILES):
                        last = fn(ss[0:n, t, 2 + j:3 + j], ss[0:n, t, j:j + 1], ACT.Sqrt, scale=1.0 / (QL, KV)[j],
                                  bias=cst[0:n, C_EPS:C_EPS + 1])
                    last.then_inc(qn_rdy, 1)
            for t, (t0, n) in enumerate(TILES):
                for hh in range(2):
                    act.wait_ge(q_done, 2 * t + hh + 1)
                    fn(z2[0:n, t, 384 * hh:384 * hh + 384], bank((2 * t + hh) % 4, 384, 0, n), ACT.Copy).then_inc(q_cp, 1)

            kt_n = [0, 0]

            def cache_tiles(u):
                kind, b = units[u]
                for i in range(ktiles_of.get(kind, 0)):
                    par = i % 2
                    kt_n[par] += 1
                    if par:
                        continue
                    act.wait_ge(kt_tp[0], kt_n[0])
                    copy_keys(fn_copy, kind, i, 7).then_inc(kt_cp[0], 1)

            def fn_copy(out, in_):
                return fn(out, in_, ACT.Copy)

            def unit_exp(u):
                kind, i = units[u]
                n = rows_of[kind]
                sc = scores[:, u % 2, :]
                act.wait_ge(mx_done, u + 1)
                if n == 128:
                    fn(sc[:, 0:128], sc[:, 0:128], ACT.Exp, bias=nmax[:, u % 2, 0:1], accum_out=lsum[:, u % 2, 0:1])
                    last = fn(sc[:, 128:384], sc[:, 128:384], ACT.Exp, bias=nmax[:, u % 2, 1:2], accum_out=lsum[:, u % 2, 1:2])
                    if kind == "Cp":
                        for q in range(2):
                            last = fn(lsum[:, u % 2, 2 + q:3 + q], sinks[:, i:i + 1], ACT.Exp, bias=nmax[:, u % 2, q:q + 1])
                else:
                    w = 128 * ktiles_of[kind] + 32
                    last = fn(sc[0:n, 0:w], sc[0:n, 0:w], ACT.Exp, bias=nmax[0:n, u % 2, 0:1], accum_out=lsum[0:n, u % 2, 0:1])
                    if kind == "Cs":
                        last = fn(lsum[0:n, u % 2, 2:3], sinkr[:, :], ACT.Exp, bias=nmax[0:n, u % 2, 0:1])
                last.then_inc(ex_done, 1)

            def unit_copies(u):
                kind, i = units[u]
                n = rows_of[kind]
                act.wait_ge(pt_tp, u + 1)
                b = 3 + u % 2
                pT = probsT[:, u % 2, :]
                if n == 128:
                    fn(pT[:, 0:384], bank(b, 384), ACT.Copy).then_inc(pt_cp, 1)
                else:
                    w = n * ktiles_of[kind]
                    fn(pT[:, 0:w], bank(b, w), ACT.Copy)
                    fn(pT[0:32, w:w + n], bank(b, n, w, 32), ACT.Copy).then_inc(pt_cp, 1)
                act.wait_ge(pv_done, u + 1)
                tok = NTP + TS * i
                if kind == "Ap":
                    last = fn(qlT[:, :, i, 0:256], bank(5).rearrange("p (c n) -> p c n", c=2), ACT.Copy)
                elif kind == "Bp":
                    r = 64 * (i % 2)
                    last = fn(oT[r:r + 64, 4 + i // 2, 0:256], ps[r:r + 64, 2560:2816], ACT.Copy)
                elif kind == "Cp":
                    g = i // 4
                    r = 64 * (g % 2)
                    last = fn(oT[r:r + 64, 4 * (g // 2) + i % 4, 0:256], ps[r:r + 64, 2560:2816], ACT.Copy)
                elif kind == "As":
                    for c in range(2):
                        last = fn(qlT[:, c, :, tok:tok + TS], bank(5, 32, 32 * c).rearrange("p (h t) -> p h t", t=TS), ACT.Copy)
                elif kind == "Bs":
                    for r in range(2):
                        for j in range(4):
                            c0 = 2560 + 32 * j + 4 * (2 * j + r)
                            last = fn(oT[64 * r:64 * r + 64, 4 + j, tok:tok + TS], ps[64 * r:64 * r + 64, c0:c0 + 4], ACT.Copy)
                else:
                    for r in range(2):
                        for j in range(2):
                            c0 = 2560 + 64 * j + 16 * (2 * j + r)
                            last = fn(oT[64 * r:64 * r + 64, 4 * j:4 * j + 4, tok:tok + TS],
                                      ps[64 * r:64 * r + 64, c0:c0 + 16].rearrange("p (r t) -> p r t", t=TS), ACT.Copy)
                last.then_inc(pv_cp, 1)

            def attention(u0, u1):
                cache_tiles(u0)
                unit_exp(u0)
                for u in range(u0, u1):
                    if u + 1 < u1:
                        cache_tiles(u + 1)
                        unit_exp(u + 1)
                    if u in ada1:
                        act.wait_ge(ada_done, 13 + ada1[u])
                        act.wait_ge(ada_tp, 11 + ada1[u])
                        fn(mrow[1][ada1[u] % 2], bank(2, 512, 0, 9), ACT.Copy).then_inc(ada_row, 1)
                    unit_copies(u)

            act.wait_ge(s_out0, 8 * 16)
            attention(0, NU0)
            for h in range(HA):
                act.wait_ge(oa_done, h + 1)
                r = 64 * (h % 2)
                fn(oT[r:r + 64, h // 2, :], ps[r:r + 64, 512 * (h % 2):512 * (h % 2) + NT], ACT.Copy).then_inc(oa_cp, 1)
            f_out(0, 1)
            x_squares(0)
            for f in range(22):
                act.wait_ge(gu_done, f + 1)
                if f:
                    act.wait_ge(act_done, f)
                fn(silu_d, bank(2 * (f % 2), NT), ACT.Silu).then_inc(si_done, 1)
            f_out(1, 3)
            x_squares(1)
            for j in range(3):
                for t, (t0, n) in enumerate(TILES):
                    act.wait_ge(z_done, nz + 1)
                    out, src = z_c[0:n, t, 512 * j:512 * j + 512], bank(nz % 4, 512, 0, n)
                    if j < 2:
                        out = out.rearrange("p (r a d) -> p a r d", a=2, r=4)
                        src = src.rearrange("p (a r d) -> p a r d", a=2, r=4)
                    fn(out, src, ACT.Copy).then_inc(z_cp, 1)
                    nz += 1
            attention(NU0, NU)
            f_out(2, 5)
            x_squares(2)

            act.wait_ge(s_out1, 4 * 16)
            for t, (t0, n) in enumerate(TILES):
                for kk in range(2):
                    i = 2 * t + kk
                    act.wait_ge(htok_tp, i + 1)
                    fn(htok[t][0:n, 512 * kk:512 * kk + 512], bank(4 + i % 2, 512, 0, n), ACT.Copy).then_inc(htok_cp, 1)
            act.wait_ge(lg_cp, 1)
            fn(gate[:, :, 1:2], gate[:, :, 0:1], ACT.Exp).then_inc(ge_done, 1)

            def gather_copy(idx):
                act.wait_ge(e_gat, idx)
                fn(hsel[:, 0:3, :], bank(0, 3 * CAP).rearrange("p (k n) -> p k n", k=3), ACT.Copy)
                fn(hsel[:, 6:8, :], bank(2, 2 * CAP).rearrange("p (k n) -> p k n", k=2), ACT.Copy).then_inc(e_gcpA, 1)

            def expert(it, p_, half):
                for f in range(28):
                    act.wait_ge(e_gu, 56 * it + (28 * half + f + 9))
                    act.wait_ge(e_act, 56 * it + (28 * half + f + 3))
                    fn(sil[:, f % 2, :], bank(f % 4, CAP), ACT.Silu).then_inc(e_si, 1)
                    if f == 15:
                        act.wait_ge(e_ptp, 2 * it + (half + 1))
                        for w, c in enumerate((P, CX)):
                            fn(putT[w], bank(6 + w, NT, 0, c), ACT.Copy)
                            last = fn(gpl[0:c, w:w + 1], bank(6 + w, 1, 300, c), ACT.Copy)
                        last.then_inc(e_pcp, 1)
                for pr in range(4):
                    act.wait_ge(e_half, 8 * it + (4 * half + pr + 1))
                    fn(oeT[:, 2 * pr, :], bank(4, CAP), ACT.Copy).then_inc(e_ocp, 1)
                    act.wait_ge(e_used, 16 * it + (8 * half + 2 * pr + 6))
                    fn(oeT[:, 2 * pr + 1, :], bank(5, CAP), ACT.Copy).then_inc(e_ocp, 1)
                gather_copy(2 * it + p_ + (half + 2))
                act.wait_ge(e_pcp, 2 * it + (half + 1))
                act.wait_ge(e_tp, 2 * it + (half + 1))
                for kk in range(2):
                    fn(otok[0][:, 512 * kk:512 * kk + 512], bank(6 + kk), ACT.Copy, scale=gpl[:, 0:1]).then_inc(e_tcpA, 1)

            def pass_body(it0, p_):
                with act.Fori(0, NE // 2) as i:
                    for half in range(2):
                        expert(it0 + i, p_, half)

            gather_copy(1)
            pass_body(0, 0)
            act.wait_ge(pass_rdy, 1)
            npass = act.value_load(passes_i[0:1, :], min_val=1, max_val=MAXPASS)
            with act.If(npass > 1):
                with act.Fori(1, npass) as p_:
                    gather_copy(9 * p_ + 1)
                    pass_body(4 * p_, p_)
            act.wait_ge(e_add, 64 * npass + 2)
            for k in range(KD):
                fn(sq[:, k, :], fT[:, k, :], ACT.Square).then_inc(sq_done, 1)
            std(7)
            for i in range(6):
                t, kk = i // 2, i % 2
                n = TILES[t][1]
                act.wait_ge(y_tp, i + 1)
                fn(htok[t][0:n, 512 * kk:512 * kk + 512], bank(i % 2, 512, 0, n), ACT.Copy).then_inc(y_cp, 1)

        @block.vector
        def _(dve):
            V = nc.vector
            nv = [0]

            def link(ins):
                nv[0] += 1
                ins.then_inc(chain_v, 1)
                dve.wait_ge(chain_v, nv[0])

            def sample(t, k0=0, k1=KD):
                return t[:, k0:k1, NTP:NT].rearrange("p k (b t) -> p k b t", t=TS)

            def per_batch(t):
                return t[:, :, 1:9].unsqueeze(3).broadcast_to([P, KD, NB, TS])

            def pre_norm(n, l, w):
                sh = mod[:, l, 24 * w:24 * w + 8, :]
                dve.wait_ge(std_done, n + 1)
                link(V.reciprocal(rinv[:, :], rstd[:, :]))
                link(V.tensor_tensor(hT, xT[:, :, :], rinv[:, :].unsqueeze(1).broadcast_to([P, KD, NT]), ALU.mult))
                for k in range(KD):
                    V.tensor_scalar(hT[:, k, 0:NTP], hT[:, k, 0:NTP], coef[:, 2 * w, k, 0:1], sh[:, k, 0:1],
                                    ALU.mult, ALU.add).then_inc(h_done, 1)
                link(V.tensor_tensor(sample(hT), sample(hT), per_batch(coef[:, 2 * w, :, :]), ALU.mult))
                V.tensor_tensor(sample(hT), sample(hT), per_batch(sh), ALU.add).then_inc(h_done, 1)

            def post_norm(n, m, w):
                g = coef[:, 2 * w + 1, :, :]
                dve.wait_ge(std_done, n + 1)
                link(V.reciprocal(rinv[:, :], rstd[:, :]))
                link(V.tensor_tensor(fT, fT, rinv[:, :].unsqueeze(1).broadcast_to([P, KD, NT]), ALU.mult))
                link(V.tensor_tensor(sample(fT), sample(fT), per_batch(g), ALU.mult))
                link(V.tensor_tensor(sample(xT), sample(xT), sample(fT), ALU.add))
                for k in range(KD):
                    V.scalar_tensor_tensor(out=xT[:, k, 0:NTP], in0=fT[:, k, 0:NTP], scalar=g[:, k, 0:1],
                                           in1=xT[:, k, 0:NTP], op0=ALU.mult, op1=ALU.add).then_inc(x_upd, 1)

            def ada_bias(l, m0, m):
                return vecT[:, 48 * l + m0:48 * l + m0 + m].unsqueeze(2).broadcast_to([P, m, 9])

            def coefficients(l):
                for w in range(2):
                    for i, (name, blk) in enumerate((("pre", 8), ("post", 16))):
                        g = vecT[:, 96 + 32 * w + 16 * i + 8 * l:96 + 32 * w + 16 * i + 8 * l + 8].unsqueeze(2).broadcast_to([P, 8, 9])
                        src = mod[:, l, 24 * w + blk:24 * w + blk + 8, :]
                        if name == "pre":
                            V.scalar_tensor_tensor(out=coef[:, 2 * w, :, :], in0=src, scalar=1.0, in1=g, op0=ALU.add, op1=ALU.mult)
                        else:
                            last = V.tensor_tensor(coef[:, 2 * w + 1, :, :], src, g, ALU.mult)
                link(last)

            def rope(x, n, heads, half, tab, ta, tb, done=None, value=0):
                c = tab[0:n, 0:2 * half].unsqueeze(1).broadcast_to([n, heads, 2 * half])
                s1 = tab[0:n, 2 * half:3 * half].unsqueeze(1).broadcast_to([n, heads, half])
                s2 = tab[0:n, 3 * half:4 * half].unsqueeze(1).broadcast_to([n, heads, half])
                V.tensor_tensor(ta, x[:, :, 0:2 * half], c, ALU.mult)
                V.tensor_tensor(tb[:, :, 0:half], x[:, :, half:2 * half], s1, ALU.mult)
                link(V.tensor_tensor(tb[:, :, half:2 * half], x[:, :, 0:half], s2, ALU.mult))
                last = V.tensor_tensor(x[:, :, 0:2 * half], ta, tb, ALU.add)
                if done is None:
                    link(last)
                else:
                    last.then_inc(done, 1)
                    dve.wait_ge(done, value)

            def rope_tmp(region, n, heads, w):
                a = region[0:n, 0:heads * w].rearrange("p (h w) -> p h w", h=heads)
                b = region[0:n, heads * w:2 * heads * w].rearrange("p (h w) -> p h w", h=heads)
                return a, b

            dve.wait_ge(c_tp, 1)
            V.tensor_copy(csT[:, :, :], bank(2, 72).rearrange("p (k c) -> p k c", c=9))
            link(V.tensor_copy(vecT[:, :], bank(3, 160)))
            dve.wait_ge(s_xload, 5 * 16)
            dve.wait_ge(s_ld, 8 * 16)
            V.tensor_scalar(nsinks[:, :], sinks[:, :], -1.0, None, ALU.mult)
            link(V.tensor_scalar(nsinkr[:, :], sinkr[:, :], -1.0, None, ALU.mult))
            V.memset(z_kr[:, :, 0:64], 0.0)
            V.memset(qbd, 0.0).then_inc(c_cp, 1)
            with dve.Fori(0, 3) as i:
                for q in range(4):
                    dve.wait_ge(ada_tp, 4 * i + (q + 1))
                    V.tensor_tensor(mod[:, 0, bass.ds(16 * i + 4 * q, 4), :], bank(6 + q % 2, 36).rearrange("p (m c) -> p m c", c=9),
                                    vecT[:, bass.ds(16 * i + 4 * q, 4)].unsqueeze(2).broadcast_to([P, 4, 9]), ALU.add).then_inc(ada_add, 1)
            dve.wait_ge(ada_add, 12)
            coefficients(0)
            pre_norm(0, 0, 0)

            for j, (zz, width, g0) in enumerate(((z_qa, QL, 0), (z_ckv, KV, QL))):
                dve.wait_ge(qn_rdy, j + 1)
                for t, (t0, n) in enumerate(TILES):
                    last = V.reciprocal(ss[0:n, t, 4 + j:5 + j], ss[0:n, t, 2 + j:3 + j])
                link(last)
                if j == 1:
                    for t, (t0, n) in enumerate(TILES):
                        kr = z_kr[0:n, t:t + 1, 64:96]
                        ta, tb = rope_tmp(rtmp2[:, 640:960], n, 1, 32)
                        rope(kr, n, 1, 16, cst[:, C_RA + 64 * t:C_RA + 64 * t + 64], ta, tb)
                for t, (t0, n) in enumerate(TILES):
                    last = V.scalar_tensor_tensor(out=zz[0:n, t, :], in0=zz[0:n, t, :], scalar=ss[0:n, t, 4 + j:5 + j],
                                                  in1=gqkv[0:n, g0:g0 + width], op0=ALU.mult, op1=ALU.mult)
                last.then_inc(z_rdy, 1)
            tcount = [0]

            def t_next():
                dve.wait_ge(t_done, tcount[0] + 1)
                tcount[0] += 1
                return 4 + (tcount[0] - 1) % 2

            for hp in range(4):
                b = t_next()
                V.tensor_copy(wukT[0:64, 2 * hp:2 * hp + 2, :], bank(b, 512, 0, 64).rearrange("p (h c) -> p h c", h=2)).then_inc(t_cp, 1)
            for k in range(3):
                V.tensor_copy(qnT[:, k, :], bank(t_next(), NT)).then_inc(t_cp, 1)
            for k in range(2):
                V.tensor_copy(ckvT[:, k, :], bank(t_next(), NT)).then_inc(t_cp, 1)
            V.tensor_copy(krT[64:96, :], ps[64:96, 512 * t_next():][:, 0:NT]).then_inc(t_cp, 1)
            dve.wait_ge(z_cp, 12)
            for t, (t0, n) in enumerate(TILES):
                ta, tb = rope_tmp(rtmp2, n, 16, 16)
                rope(z_qk[0:n, t, :].rearrange("p (h d) -> p h d", h=16), n, 16, 8, cst[:, C_RB + 32 * t:C_RB + 32 * t + 32], ta, tb, z_rdy, 3 + t)
            for t, (t0, n) in enumerate(TILES):
                dve.wait_ge(q_cp, 2 * t + 2)
                ta, tb = rope_tmp(rtmp2, n, 8, 32)
                rope(z2[0:n, t, :].rearrange("p (h d) -> p h d", h=8)[:, :, 64:96], n, 8, 16,
                     cst[:, C_RA + 64 * t:C_RA + 64 * t + 64], ta, tb, q_rope, t + 1)
            for k in range(4):
                V.tensor_copy(qT0[:, k, :], bank(t_next(), NT)).then_inc(t_cp, 1)
            for k in range(4):
                V.tensor_copy(kT0[:, k, :], bank(t_next(), NT)).then_inc(t_cp, 1)
            for h in range(HA):
                V.tensor_copy(qhT[:, h, :], bank(t_next(), NT, 0, 96)).then_inc(t_cp, 1)
            for h in range(HA):
                for c in range(2):
                    V.tensor_copy(qlT[:, c, h, :], bank(t_next(), NT)).then_inc(t_cp, 1)
            dve.wait_ge(t_cp, tcount[0])
            for c in range(2):
                V.tensor_copy(qls[:, c, :, :].rearrange("p b (h t) -> p h b t", t=TS),
                              qlT[:, c, :, NTP:NT].rearrange("p h (b t) -> p h b t", t=TS))
            V.tensor_copy(qhs[64:96, :, :].rearrange("p b (h t) -> p h b t", t=TS),
                          qhT[64:96, :, NTP:NT].rearrange("p h (b t) -> p h b t", t=TS))
            for j in range(4):
                for r in range(2):
                    h = 2 * j + r
                    last = V.tensor_copy(qbd0[64 * r:64 * r + 64, :, j, 4 * h:4 * h + 4],
                                         qT0[64 * r:64 * r + 64, j, NTP:NT].rearrange("p (b t) -> p b t", t=TS))
            last.then_inc(bd_rdy, 1)
            dve.wait_ge(s_out0, 8 * 16)

            kt_n = [0, 0]

            def cache_tiles(u):
                kind, b = units[u]
                for i in range(ktiles_of.get(kind, 0)):
                    par = i % 2
                    kt_n[par] += 1
                    if not par:
                        continue
                    dve.wait_ge(kt_tp[1], kt_n[1])
                    copy_keys(V.tensor_copy, kind, i, 6).then_inc(kt_cp[1], 1)

            def unit_max(u):
                kind, i = units[u]
                n = rows_of[kind]
                sc = scores[:, u % 2, :]
                dve.wait_ge(sc_done, u + 1)
                if u >= 2:
                    dve.wait_ge(pt_tp, u - 1)
                scale = MLA_SCALE if kind[0] == "A" else HD_SCALE

                def masked(out, src, m):
                    return V.scalar_tensor_tensor(out=out, in0=src, scalar=scale, in1=m, op0=ALU.mult, op1=ALU.add)

                if n == 128:
                    m0 = {"A": M_A, "B": M_B, "C": M_C}[kind[0]]
                    last = masked(sc[:, 0:384], bank(0, 384), msk[:, m0:m0 + 384])
                    w = 384
                elif kind == "As":
                    V.tensor_scalar(sc[0:32, 0:1024], ps[0:32, 0:1024], scale, None, ALU.mult)
                    last = masked(sc[0:32, 1024:1056], bank(2, 32, 0, 32), msk[0:32, M_NA + 32 * i:M_NA + 32 * i + 32])
                    w = 1056
                elif kind == "Bs":
                    masked(sc[0:32, 0:640], ps[0:32, 0:640], msk[0:32, M_SB:M_SB + 640])
                    last = masked(sc[0:32, 640:672], ps[0:32, 640:672], msk[0:32, M_NB + 32 * i:M_NB + 32 * i + 32])
                    w = 672
                else:
                    masked(sc[0:64, 0:128], ps[0:64, 0:128], cst[0:64, C_CM:C_CM + 128])
                    last = masked(sc[0:64, 128:160], ps[0:64, 128:160], msk[0:64, M_NA + 32 * i:M_NA + 32 * i + 32])
                    w = 160
                last.then_inc(sc_cp, 1)
                dve.wait_ge(sc_cp, u + 1)
                nm = nmax[:, u % 2, :]
                if n == 128:
                    V.tensor_reduce(nm[:, 0:1], sc[:, 0:128], AX_X, ALU.max, negate=True)
                    last = V.tensor_reduce(nm[:, 1:2], sc[:, 128:384], AX_X, ALU.max, negate=True)
                    if kind == "Cp":
                        link(last)
                        last = V.tensor_scalar(nm[:, 0:2], nm[:, 0:2], nsinks[:, i:i + 1], None, ALU.min)
                else:
                    last = V.tensor_reduce(nm[0:n, 0:1], sc[0:n, 0:w], AX_X, ALU.max, negate=True)
                    if kind == "Cs":
                        link(last)
                        last = V.tensor_scalar(nm[0:n, 0:1], nm[0:n, 0:1], nsinkr[:, :], None, ALU.min)
                last.then_inc(mx_done, 1)

            def unit_probs(u):
                kind, i = units[u]
                n = rows_of[kind]
                sc = scores[:, u % 2, :]
                ls, r = lsum[:, u % 2, :], rl[:, u % 2, :]
                dve.wait_ge(ex_done, u + 1)
                nh = 2 if n == 128 else 1
                if kind[0] == "C":
                    link(V.tensor_tensor(ls[0:n, 0:nh], ls[0:n, 0:nh], ls[0:n, 2:2 + nh], ALU.add))
                link(V.reciprocal(r[0:n, 0:nh], ls[0:n, 0:nh]))
                if nh == 2:
                    V.tensor_scalar(sc[:, 0:128], sc[:, 0:128], r[:, 0:1], None, ALU.mult)
                    V.tensor_scalar(sc[:, 128:384], sc[:, 128:384], r[:, 1:2], None, ALU.mult).then_inc(pr_done, 1)
                else:
                    w = 128 * ktiles_of[kind] + 32
                    V.tensor_scalar(sc[0:n, 0:w], sc[0:n, 0:w], r[0:n, 0:1], None, ALU.mult).then_inc(pr_done, 1)

            def attention(u0, u1):
                cache_tiles(u0)
                unit_max(u0)
                for u in range(u0, u1):
                    unit_probs(u)
                    if u - 1 in ada1:
                        j = ada1[u - 1]
                        dve.wait_ge(ada_tp, 13 + j)
                        V.tensor_tensor(mod[:, 1, 4 * j:4 * j + 4, :], bank(2, 36).rearrange("p (m c) -> p m c", c=9),
                                        ada_bias(1, 4 * j, 4), ALU.add).then_inc(ada_add, 1)
                    if u + 1 < u1:
                        cache_tiles(u + 1)
                        unit_max(u + 1)

            attention(0, NU0)
            post_norm(1, 0, 0)
            pre_norm(2, 0, 1)
            for f in range(22):
                dve.wait_ge(si_done, f + 1)
                V.tensor_tensor(actd[:, f, :], bank(2 * (f % 2) + 1, NT), silu_d, ALU.mult).then_inc(act_done, 1)
            post_norm(3, 1, 1)
            link(V.memset(qbd, 0.0))
            dve.wait_ge(ada_add, 24)
            coefficients(1)
            pre_norm(4, 1, 0)
            dve.wait_ge(z_cp, 24)
            for t, (t0, n) in enumerate(TILES):
                ta, tb = rope_tmp(rtmp2, n, 20, 16)
                rope(z_c[0:n, t, 0:1280].rearrange("p (h d) -> p h d", h=20), n, 20, 8, cst[:, C_RB + 32 * t:C_RB + 32 * t + 32], ta, tb, z_rdy, 6 + t)
            for k in range(8):
                V.tensor_copy(qT1[:, k, :], bank(t_next(), NT)).then_inc(t_cp, 1)
            for k in range(2):
                V.tensor_copy(kT1[:, k, :], bank(t_next(), NT)).then_inc(t_cp, 1)
            dve.wait_ge(t_cp, tcount[0])
            for j in range(2):
                for r in range(2):
                    g = 2 * j + r
                    for b in range(NB):
                        last = V.tensor_copy(qbd1[64 * r:64 * r + 64, b, j, 16 * g:16 * g + 16].rearrange("p (r t) -> p r t", t=TS),
                                             qT1[64 * r:64 * r + 64, 4 * j:4 * j + 4, NTP + TS * b:NTP + TS * b + TS])
            last.then_inc(bd_rdy, 1)
            attention(NU0, NU)
            post_norm(5, 2, 0)
            pre_norm(6, 1, 1)

            V.memset(oh, 0.0)
            V.memset(gate, 0.0)
            V.memset(posm, -1.0)
            V.memset(topf, 0.0)
            V.memset(gates, 0.0).then_inc(e_add, 2)
            V.memset(cnt, 0.0).then_inc(e_act, 4)
            link(V.memset(fT, 0.0))
            dve.wait_ge(lg_done, 1)
            for t, (t0, n) in enumerate(TILES):
                last = V.tensor_tensor(logit[0:n, t, :], bank(0, 8, 8 * t, n), brout[0:n, :], ALU.add)
            link(last)
            for t, (t0, n) in enumerate(TILES):
                last = V.max(top[0:n, t, :], logit[0:n, t, :])
            link(last)
            for t, (t0, n) in enumerate(TILES):
                V.max_index(topi[0:n, t, :], top[0:n, t, :], logit[0:n, t, :])
                last = V.tensor_tensor(gate[0:n, t, 0:1], top[0:n, t, 1:2], top[0:n, t, 0:1], ALU.subtract)
            last.then_inc(lg_cp, 1)
            dve.wait_ge(lg_cp, 1)
            for t, (t0, n) in enumerate(TILES):
                last = V.tensor_copy(topf[0:n, t, :], topi[0:n, t, 0:2])
            link(last)
            for t, (t0, n) in enumerate(TILES):
                for w in range(2):
                    last = V.tensor_scalar(oh[0:n, w, t, :], cst[0:n, C_I8:C_I8 + 8], topf[0:n, t, w:w + 1], None, ALU.is_equal)
            link(last)
            V.tensor_tensor(mask, oh[:, 0, :, :], oh[:, 1, :, :], ALU.add).then_inc(msk_done, 1)
            dve.wait_ge(ge_done, 1)
            link(V.tensor_scalar(gate[:, :, 2:3], gate[:, :, 1:2], 1.0, None, ALU.add))
            link(V.reciprocal(gate[:, :, 2:3], gate[:, :, 2:3]))
            link(V.tensor_tensor(gate[:, :, 3:4], gate[:, :, 2:3], gate[:, :, 1:2], ALU.mult))
            for w in range(2):
                last = V.tensor_tensor(oh[:, w, :, :], oh[:, w, :, :], gate[:, :, 2 + w:3 + w].broadcast_to([P, 3, NE]), ALU.mult)
            link(last)
            link(V.tensor_tensor(gates[:, 0:NE, :].rearrange("p n t -> p t n"), oh[:, 0, :, :], oh[:, 1, :, :], ALU.add))
            dve.wait_ge(msk_done, 1)
            dve.wait_ge(pos_done, 1)
            link(V.scalar_tensor_tensor(out=pm_t, in0=bank(1, 24).rearrange("p (t n) -> p t n", t=3), scalar=1.0, in1=mask,
                                        op0=ALU.add, op1=ALU.mult))
            link(V.tensor_scalar(posm[:, 0:NE, :].rearrange("p n t -> p t n"), pm_t, -1.0, None, ALU.add))
            link(V.tensor_reduce(passes, bank(1, 8, 24), AX_X, ALU.max))
            for q in range(1, MAXPASS):
                V.tensor_scalar(cnt[:, q:q + 1], passes, float(CAP * q), None, ALU.is_gt)
            V.memset(cnt[:, MAXPASS:MAXPASS + 1], 1.0)
            link(V.memset(cnt[:, 0:1], 0.0))
            link(V.tensor_reduce(passes, cnt[:, 1:MAXPASS + 1], AX_X, ALU.add))
            V.tensor_copy(cnt_i, bank(1, 8, 24, 1))
            V.tensor_copy(passes_i, passes).then_inc(pass_rdy, 1)

            ne = [0]

            def elink(ins, base):
                ne[0] += 1
                ins.then_inc(chain_e, 1)
                dve.wait_ge(chain_e, base + ne[0])

            def choose(e, gathered, turned, base):
                if gathered is not None:
                    dve.wait_ge(e_gat, gathered)
                    dve.wait_ge(e_ptp, turned)
                V.tensor_copy(cur[:, 0:1, :], posm[:, bass.ds(e, 1), :])
                elink(V.tensor_copy(cur[:, 1:2, :], gates[:, bass.ds(e, 1), :]), base)
                for t in range(3):
                    last = V.tensor_scalar(pick[:, t, :], iota_c, cur[:, 0, t:t + 1], None, ALU.is_equal)
                last.then_inc(e_pick, 1)

            def gather_copy(idx):
                dve.wait_ge(e_gat, idx)
                V.tensor_copy(hsel[:, 3:6, :], bank(1, 3 * CAP).rearrange("p (k n) -> p k n", k=3)).then_inc(e_gcpV, 1)

            def expert(it, i, p_, half, base):
                for f in range(28):
                    dve.wait_ge(e_si, 56 * it + (28 * half + f + 1))
                    V.tensor_tensor(acte[:, f, :], bank(f % 4, CAP, CAP), sil[:, f % 2, :], ALU.mult).then_inc(e_act, 1)
                    if f == 17:
                        choose(2 * i + (half + 1), 2 * it + p_ + (half + 1), 2 * it + (half + 1), base)
                gather_copy(2 * it + p_ + (half + 2))
                dve.wait_ge(e_pcp, 2 * it + (half + 1))
                dve.wait_ge(e_tp, 2 * it + (half + 1))
                for kk in range(2):
                    V.tensor_scalar(otok[1][:, 512 * kk:512 * kk + 512], bank(3 + 2 * kk, 512, 0, CX), gpl[0:CX, 1:2], None,
                                    ALU.mult).then_inc(e_tcpV, 1)
                for k in range(KD):
                    dve.wait_ge(e_cb, 16 * it + (8 * half + k + 1))
                    V.tensor_tensor(fT[:, k, :], bank(6 + k % 2, NT), fT[:, k, :], ALU.add).then_inc(e_add, 1)

            def pass_body(it0, p_, base):
                with dve.Fori(0, NE // 2) as i:
                    ne[0] = 0
                    for half in range(2):
                        expert(it0 + i, i, p_, half, base + 2 * i)
                assert ne[0] == 2

            ne[0] = 0
            choose(0, None, None, 0)
            gather_copy(1)
            pass_body(0, 0, 1)
            dve.wait_ge(pass_rdy, 1)
            npass = dve.value_load(passes_i[0:1, :], min_val=1, max_val=MAXPASS)
            with dve.If(npass > 1):
                with dve.Fori(1, npass) as p_:
                    dve.wait_ge(e_pick, 9 * p_)
                    ne[0] = 0
                    base = 10 * p_ - 1
                    elink(V.tensor_scalar(posm[:, :, :], posm[:, :, :], float(-CAP), None, ALU.add), base)
                    choose(0, 9 * p_, 8 * p_, base)
                    gather_copy(9 * p_ + 1)
                    pass_body(4 * p_, p_, 10 * p_ + 1)
            dve.wait_ge(e_add, 64 * npass + 2)
            post_norm(7, 3, 1)

    return nc


_INS = ["x_prompt", "x_sample", "c_prompt", "c_sample", "cache_mla_ckv", "cache_mla_krope", "cache_b_k", "cache_b_v",
        "cache_c_k", "cache_c_v", "page_table", "w_ada", "b_ada", "g_pre_mix", "g_post_mix", "g_pre_ffn", "g_post_ffn",
        "w_in_ab", "g_q_a", "w_q_b", "g_kv_a", "w_kv_b", "w_out_ab", "w_ffd_in", "w_ffd_out", "w_qkv_c", "sinks_c",
        "w_out_c", "w_router", "b_router", "w_moe_in", "w_moe_out"]
_OUTS = [("y_prompt", (NTP, D), (1, NTP, D)), ("y_sample", (NS, D), (NB, TS, D)),
         ("p_ckv", (NTP, KV), (1, 1, NTP, KV)), ("p_kr", (NTP, RA), (1, 1, NTP, RA)),
         ("p_bk", (NTP, 512), (1, 1, NTP, 8, HD)), ("p_bv", (NTP, 512), (1, 1, NTP, 8, HD)),
         ("p_ck", (128, 256), (1, 1, 128, GC, HD)), ("p_cv", (128, 256), (1, 1, 128, GC, HD)),
         ("s_ckv", (NS, KV), (1, NB, TS, KV)), ("s_kr", (NS, RA), (1, NB, TS, RA)),
         ("s_bk", (NS, 512), (1, NB, TS, 8, HD)), ("s_bv", (NS, 512), (1, NB, TS, 8, HD)),
         ("s_ck", (NS, 256), (1, NB, TS, GC, HD)), ("s_cv", (NS, 256), (1, NB, TS, GC, HD))]


def kernel(**inputs):
    import concourse.bacc as bacc
    from concourse.bass_utils import run_bass_kernel_spmd as run

    nc = bacc.Bacc("TRN2", target_bir_lowering=False, num_devices=1)
    arrays, t_in, t_out = {}, {}, {}
    cst, msk = shape_constants()
    for name, a in [(n, inputs[n]) for n in _INS] + [("cst", cst), ("msk", msk)]:
        a = np.ascontiguousarray(a)
        arrays[f"in_{name}"] = a
        t_in[name] = nc.dram_tensor(f"in_{name}", a.shape, mybir.dt.from_np(a.dtype), kind="ExternalInput").ap()
    for name, shape, _ in _OUTS:
        t_out[name] = nc.dram_tensor(f"out_{name}", shape, F32, kind="ExternalOutput").ap()
    build(nc, t_in, t_out)
    r = run(nc, [arrays], core_ids=[0])
    return tuple(r.results[0][f"out_{name}"].reshape(shape) for name, _, shape in _OUTS)
```

```python
from contextlib import ExitStack

import numpy as np
import concourse.bass as bass
from concourse import mybir

F32 = mybir.dt.float32
I32 = mybir.dt.int32
U32 = mybir.dt.uint32
ALU = mybir.AluOpType
ACT = mybir.ActivationFunctionType
AX_X = mybir.AxisListType.X

D, P, KD = 1024, 128, 8
NTP, NB, TS = 256, 8, 4
NS = NB * TS
NT = NTP + NS
TILES = [(0, 128), (128, 128), (256, 32)]
PAST, PAGE = 1024, 128
NPG = PAST // PAGE
QL, KV, NOPE, RA, HA, HD = 384, 256, 64, 32, 8, 64
HC, GC = 16, 4
FD, NE, FE = 2816, 8, 3584
NFD, NFE = FD // P, FE // P
NA1 = 16
A1 = 6 * D // NA1
MLA_SCALE = float(NOPE + RA) ** -0.5
HD_SCALE = float(HD) ** -0.5
EPS, NEG = 1e-6, -1e30
THETA = 500000.0
CAP = 144
MAXPASS = -(-NT // CAP)
CX = CAP - P

SLOT = 4096
NSLOT = 4
OSLOT = 14 * 256
BCOLS = 5 * 128

C_ID, C_ONE, C_UP, C_IC, C_I8 = 0, 128, 256, 384, 384 + CAP
C_RA = C_I8 + 8
C_RB = C_RA + 3 * 64
C_CM = C_RB + 3 * 32
C_EPS = C_CM + 128
NCST = C_EPS + 1
M_A, M_B, M_C, M_SB, M_NA, M_NB = 0, 384, 768, 1152, 1152 + BCOLS, 1152 + BCOLS + 256
NMSK = M_NB + 256


def shape_constants():
    f = np.float32
    c = np.zeros((P, NCST), f)
    c[:, C_ID:C_ID + 128] = np.eye(P)
    c[:, C_ONE:C_ONE + 128] = 1
    c[:, C_UP:C_UP + 128] = np.triu(np.ones((P, P)), 1)
    c[:, C_IC:C_IC + CAP] = np.arange(CAP)
    c[:, C_I8:C_I8 + 8] = np.arange(8)
    c[:, C_EPS] = EPS
    pos = [np.arange(128), 128 + np.arange(128), PAST + np.arange(128) % TS]
    for half, at in ((RA // 2, C_RA), (HD // 8, C_RB)):
        inv = f(THETA) ** (-np.arange(half, dtype=f) / f(half))
        for t in range(3):
            ang = pos[t].astype(f)[:, None] * inv.astype(f)[None, :]
            cos, sin = np.cos(ang).astype(f), np.sin(ang).astype(f)
            c[:, at + t * 4 * half:at + (t + 1) * 4 * half] = np.concatenate([cos, cos, -sin, sin], 1)
    r = np.arange(64) % TS
    c[:64, C_CM:C_CM + 128] = np.where(np.arange(128)[None] > r[:, None], 0, NEG)

    def count(dist):
        n = np.zeros(dist.shape)
        for w, d in ((128, 1), (512, 4), (2048, 16)):
            n += (dist >= 0) & (dist <= w) & (dist % d == 0)
        return np.where(n > 0, np.log(np.maximum(n, 1)), NEG)

    m = np.zeros((P, NMSK), f)
    q, k = np.arange(128)[:, None], np.arange(128)[None]
    dist = np.concatenate([q - k, q + 128 - k, q - k], 1)
    m[:, M_A:M_A + 384] = np.where(dist >= 0, 0, NEG)
    m[:, M_B:M_B + 384] = count(dist)
    m[:, M_C:M_C + 384] = np.where((dist >= 0) & (dist < 128), 0, NEG)
    p = np.arange(128)
    keys = np.concatenate([p // 4 * 16 + p % 4] + [512 + 4 * p + i for i in range(4)])
    t = (np.arange(32) % TS)[:, None]
    m[:32, M_SB:M_SB + BCOLS] = count(PAST + t - keys[None])
    kb, kt = np.arange(NS)[None] // TS, np.arange(NS)[None] % TS
    for b in range(NB):
        m[:64, M_NA + 32 * b:M_NA + 32 * b + 32] = np.where((kb == b) & (kt <= r[:, None]), 0, NEG)
        m[:32, M_NB + 32 * b:M_NB + 32 * b + 32] = np.where(kb == b, count(t - kt), NEG)
    return c, m


def ring_plan():
    plan = [("ada0", j, 1) for j in range(12)]
    plan += [("in_ab", j, 1) for j in range(5)]
    plan += [("q_b", 0, 1)]
    u0 = units_of_layer0()
    ada1 = ada1_steps()
    for u in range(-2, len(u0)):
        if u >= 0 and u0[u][0] == "Bs":
            plan += [("bv", u0[u][1], 2)]
        if u in ada1:
            plan += [("ada1", ada1[u], 1)]
        if u + 2 < len(u0) and u0[u + 2][0] == "Bs":
            plan += [("bk", u0[u + 2][1], 2)]
        elif u + 2 < len(u0) and u0[u + 2][0] == "As":
            plan += [("mla", u0[u + 2][1], 2 * NPG)]
    plan += [("out_ab", j, 1) for j in range(2)]
    plan += [("ffd_in", j, 2) for j in range(11)]
    plan += [("ffd_out", j, 1) for j in range(8)]
    plan += [("qkv_c", j, 1) for j in range(3)]
    plan += [("c_cache", 0, 2)]
    plan += [("out_c", j, 4) for j in range(2)]
    at, arrived, total = {}, {}, [0] * NSLOT
    for n, (kind, j, dmas) in enumerate(plan):
        total[n % NSLOT] += 16 * dmas
        at[(kind, j)] = n
        arrived[n] = total[n % NSLOT]
    return plan, at, arrived, total


def units_of_layer0():
    out = []
    for i in range(8):
        out += [("Bs", i), ("Bp", i), ("As", i), ("Ap", i)]
    return out


def ada1_steps():
    u0 = units_of_layer0()
    return {u: j for j, u in enumerate(u for u in range(-1, len(u0) - 1) if u0[u + 1][0] in ("As", "Bs"))}


def units_of_layer1():
    out = []
    for i in range(8):
        out += [("Cs", i), ("Cp", 2 * i), ("Cp", 2 * i + 1)]
    return out


def build(nc, t_in, t_out):
    plan, at, arrived, ring_total = ring_plan()
    NPLAN = len(plan)
    ada1 = ada1_steps()
    units = units_of_layer0() + units_of_layer1()
    NU0 = len(units_of_layer0())
    NU = len(units)
    rows_of = {"Ap": 128, "Bp": 128, "Cp": 128, "As": 32, "Bs": 32, "Cs": 64}
    ktiles_of = {"As": NPG, "Bs": 5, "Cs": 1}

    ctx = ExitStack()
    with ctx:
        def sb(name, shape, dt=F32):
            return ctx.enter_context(nc.sbuf_tensor(name, shape, dt))

        def sem(name):
            return ctx.enter_context(nc.semaphore(name))

        ring = sb("ring", [P, NSLOT, SLOT])
        mix = sb("mix", [P, 4 * OSLOT])
        xT = sb("xT", [P, KD, NT])
        work = sb("work", [P, 3 * KD * NT])
        z = sb("z", [P, 6624])
        o_or_q = sb("o_or_q", [P, KD * NT])
        rinv_rstd = sb("rinv_rstd", [P, 2 * NT])
        rinv, rstd = rinv_rstd[:, 0:NT], rinv_rstd[:, NT:2 * NT]
        mod = sb("mod", [P, 2, 48, 9])
        coef = sb("coef", [P, 4, KD, 9])
        cst = sb("cst", [P, NCST])
        gqkv = sb("gqkv", [P, QL + KV])
        vecT = sb("vecT", [P, 160])
        csT = sb("csT", [P, KD, 9])
        sinks = sb("sinks", [P, HC])
        nsinks = sb("nsinks", [P, HC])
        sinkr = sb("sinkr", [64, 1])
        nsinkr = sb("nsinkr", [64, 1])
        brout = sb("brout", [P, NE])
        wrout = sb("wrout", [P, KD, NE])
        ptab = sb("ptab", [1, NB * NPG], I32)
        nmax = sb("nmax", [P, 4, 2])
        lsum = sb("lsum", [P, 4, 4])
        rl = sb("rl", [P, 4, 2])
        ss = sb("ss", [P, 3, 6])

        hT = work[:, 0:2304].rearrange("p (k n) -> p k n", k=KD)
        fT = work[:, 2304:4608].rearrange("p (k n) -> p k n", k=KD)
        sq = work[:, 4608:6912].rearrange("p (k n) -> p k n", k=KD)
        qhT = work[0:96, 0:2304].rearrange("p (h n) -> p h n", h=HA)
        qlT = work[:, 2304:6912].rearrange("p (c h n) -> p c h n", c=2, h=HA)
        xtok = z[:, 0:3072].rearrange("p (t n) -> p t n", t=3)
        ctok = z[0:9, 3072:4096]
        cstok = z[0:9, 4096:5120]
        vecA = z[0:96, 5120:5248]
        vecB = z[0:64, 5248:5376]
        z_qk = z[:, 0:3072].rearrange("p (t n) -> p t n", t=3)
        z_v = z[:, 3072:4608].rearrange("p (t n) -> p t n", t=3)
        z_ckv = z[:, 4608:5376].rearrange("p (t n) -> p t n", t=3)
        z_kr = z[:, 5376:5472 + 192].rearrange("p (t n) -> p t n", t=3)
        z_qa = o_or_q[:, 0:1152].rearrange("p (t n) -> p t n", t=3)
        rtmp2 = z[:, 5664:6624]
        qls = z[:, 5664:6176].rearrange("p (c b n) -> p c b n", c=2, b=NB)
        qhs = z[:, 6176:6432].rearrange("p (b n) -> p b n", b=NB)
        z2 = o_or_q[:, :].rearrange("p (t n) -> p t n", t=3)
        z_c = z[:, 0:4608].rearrange("p (t n) -> p t n", t=3)
        oT = o_or_q[:, :].rearrange("p (k n) -> p k n", k=KD)
        kcT = z[:, 0:3072]
        actd = z[:, 0:NFD * NT].rearrange("p (f n) -> p f n", f=NFD)

        m_at = [0]

        def mixview(n):
            m_at[0] += n
            return mix[:, m_at[0] - n:m_at[0]]

        msk = mixview(NMSK)
        qkT = mixview(4032)
        qT0 = qkT[:, 0:1152].rearrange("p (k n) -> p k n", k=4)
        kT0 = qkT[:, 1152:2304].rearrange("p (k n) -> p k n", k=4)
        ckvT = qkT[:, 2304:2880].rearrange("p (k n) -> p k n", k=2)
        qnT = qkT[:, 2880:3744].rearrange("p (k n) -> p k n", k=3)
        krT = qkT[:, 3744:4032]
        qT1 = qkT[:, 0:2304].rearrange("p (k n) -> p k n", k=8)
        kT1 = qkT[:, 2304:2880].rearrange("p (k n) -> p k n", k=2)
        wukT = mixview(2048).rearrange("p (h c) -> p h c", h=HA)
        kcT_c = wukT.rearrange("p h c -> p (h c)").rearrange("p (b j n) -> p b j n", b=NB, j=2)
        kvb = mixview(2048).rearrange("p (c n) -> p c n", c=2)
        scores = mixview(2112).rearrange("p (b n) -> p b n", b=2)
        mrow = [[scores[0:9, 0, 0:512], scores[0:9, 1, 0:512]], [gqkv[0:9, 0:512], rinv_rstd[0:9, 0:512]]]
        probsT = mixview(768).rearrange("p (b n) -> p b n", b=2)
        qbd = mixview(1024)
        qbd0 = qbd.rearrange("p (b j n) -> p b j n", b=NB, j=4)
        qbd1 = qbd.rearrange("p (b j n) -> p b j n", b=NB, j=2)
        oring = mix[:, 0:4 * OSLOT].rearrange("p (s n) -> p s n", s=4)

        acte = z[:, 0:28 * CAP].rearrange("p (f n) -> p f n", f=28)
        hsel = z[:, 28 * CAP:36 * CAP].rearrange("p (k n) -> p k n", k=KD)
        oeT = z[:, 36 * CAP:44 * CAP].rearrange("p (k n) -> p k n", k=KD)
        sil = z[:, 44 * CAP:46 * CAP].rearrange("p (b n) -> p b n", b=2)
        otok = [work[:, 0:D], work[0:CX, D:2 * D]]
        gpl = work[:, 2 * D:2 * D + 2]
        cnt_i = work[0:1, 2 * D + 8:2 * D + 16].bitcast(I32)
        htok = [work[:, 4608:4608 + D], work[:, 4608 + D:4608 + 2 * D], o_or_q[:, 0:D]]
        pick = o_or_q[:, D:D + 3 * CAP].rearrange("p (t n) -> p t n", t=3)
        putT = [o_or_q[:, D + 3 * CAP:D + 3 * CAP + NT], o_or_q[0:CX, D + 3 * CAP + NT:D + 3 * CAP + 2 * NT]]
        rt = o_or_q[:, D + 3 * CAP + 2 * NT:2304]
        logit = rt[:, 0:24].rearrange("p (t n) -> p t n", t=3)
        top = rt[:, 24:48].rearrange("p (t n) -> p t n", t=3)
        topi = rt[:, 48:72].bitcast(U32).rearrange("p (t n) -> p t n", t=3)
        topf = rt[:, 72:78].rearrange("p (t n) -> p t n", t=3)
        gate = rt[:, 84:96].rearrange("p (t n) -> p t n", t=3)
        oh = rt[:, 96:144].rearrange("p (w t n) -> p w t n", w=2, t=3)
        mask = rt[:, 144:168].rearrange("p (t n) -> p t n", t=3)
        gates = rt[:, 168:195].rearrange("p (n t) -> p n t", t=3)
        posm = rt[:, 195:222].rearrange("p (n t) -> p n t", t=3)
        cur = rt[:, 222:228].rearrange("p (w t) -> p w t", w=2)
        pm_t = rt[:, 232:256].rearrange("p (t n) -> p t n", t=3)
        cnt = rt[:, 256:264]
        passes = rt[:, 265:266]
        passes_i = rt[:, 267:268].bitcast(I32)
        silu_d = z[:, 22 * NT:23 * NT]

        ps = ctx.enter_context(nc.psum_tensor("ps", [P, 8 * 512], F32))

        def bank(i, n=512, at_=0, rows=P):
            return ps[0:rows, 512 * i + at_:512 * i + at_ + n]

        ident = cst[:, C_ID:C_ID + 128]
        ones = cst[:, C_ONE:C_ONE + 128]
        iota_c = cst[:, C_IC:C_IC + CAP]

        s_in = [sem(f"ring_in{i}") for i in range(NSLOT)]
        s_ld, s_ldm = sem("loaded"), sem("loaded_vectors")
        s_xload = sem("x_loaded")
        s_pt = sem("page_table_loaded")
        x_tp, x_cp = sem("x_transposed"), sem("x_copied")
        c_silu, c_tp, c_cp = sem("c_silu"), sem("c_transposed"), sem("c_copied")
        sq_done, sq_added, stat_done, std_done = sem("squares_done"), sem("squares_added"), sem("sums_done"), sem("std_done")
        h_part, h_done, x_upd = sem("h_before_shift"), sem("h_done"), sem("x_updated")
        ada_done, ada_row, ada_tp, ada_add = sem("ada_done"), sem("ada_rows_copied"), sem("ada_transposed"), sem("ada_added")
        z_done, z_cp, z_rdy = sem("z_done"), sem("z_copied"), sem("z_ready")
        t_done, t_cpA, t_cpV = (sem("mixer_transposes_done"), sem("mixer_transposes_copied_act"),
                               sem("mixer_transposes_copied_vec"))
        q_done, q_cp, q_rope = sem("q_done"), sem("q_copied"), sem("q_roped")
        qn_rdy = sem("qn_ready")
        bd_rdy = sem("block_diagonal_ready")
        kt_tp = [sem("cache_transposed_even"), sem("cache_transposed_odd")]
        kt_cp = [sem("cache_copied_even"), sem("cache_copied_odd")]
        sc_done, sc_cp, mx_done, ex_done, pr_done = (sem("scores_done"), sem("scores_copied"), sem("max_done"),
                                                     sem("exp_done"), sem("probs_done"))
        pt_tp, pt_cp, pv_done, pv_cp = (sem("probs_transposed"), sem("probsT_copied"), sem("pv_done"),
                                        sem("pv_copied"))
        ob_done, ob_cp = sem("b_rows_done"), sem("b_rows_copied")
        oa_done, oa_cp = sem("oa_done"), [sem("oa_copied_act"), sem("oa_copied_vec")]
        f_done, f_cp = sem("f_done"), sem("f_copied")
        gu_done, si_done, act_done = sem("gate_up_done"), sem("silu_done"), sem("act_done")
        y_tp, y_cp, s_out = sem("y_transposed"), sem("y_copied"), sem("stored")
        s_out0 = sem("stored_layer0")
        s_out1 = sem("stored_layer1")
        chain_v = sem("vector_chain")
        htok_tp, htok_cp, lg_done, lg_cp = sem("htok_transposed"), sem("htok_copied"), sem("logits_done"), sem("logits_copied")
        ge_done, msk_done, pos_done, pass_rdy = sem("gate_exp_done"), sem("route_masks_done"), sem("positions_done"), sem("passes_ready")
        e_gu, e_si, e_act = sem("e_gate_up_done"), sem("e_silu_done"), sem("e_act_done")
        e_in, e_used = [sem(f"oring_in{i}") for i in range(4)], sem("oring_used")
        e_half, e_ocp = sem("e_out_first_half_done"), sem("e_out_copied")
        e_tp, e_tcpA, e_tcpV = sem("e_out_transposed"), sem("e_out_tok_copied_act"), sem("e_out_tok_copied_vec")
        e_cb, e_add = sem("combine_done"), sem("combine_added")
        e_pick, e_gat, e_gcpA, e_gcpV = sem("pick_ready"), sem("gathered"), sem("gather_copied_act"), sem("gather_copied_vec")
        e_ptp, e_pcp = sem("put_transposed"), sem("put_copied")
        chain_e = sem("vector_chain_experts")

        KT_BANKS = (7, 6, 2)

        def place(u):
            return u % 2 if u < NU0 else (u - NU0) % 4

        def scores_of(u):
            return scores[:, u % 2, :] if u < NU0 else scores.rearrange("p b n -> p (b n)")[:, 384 * place(u):384 * place(u) + 384]

        def by_act(t):
            return t < 4 or (t >= 10 and t % 2 == 1)

        def copied(engine, t):
            a = sum(by_act(i) for i in range(t + 1))
            if a:
                engine.wait_ge(t_cpA, a)
            if t + 1 > a:
                engine.wait_ge(t_cpV, t + 1 - a)

        T_QN, T_CKV, T_QK, T_1 = 4, 7, 10, 42
        t_dst = [(wukT[0:64, 2 * i:2 * i + 2, :].rearrange("p h c -> p (h c)"), 0, 64, 512) for i in range(4)]
        t_dst += [(qnT[:, k, :], 0, 128, NT) for k in range(3)]
        t_dst += [(ckvT[:, k, :], 0, 128, NT) for k in range(2)]
        t_dst += [(krT[64:96, :], 64, 96, NT)]
        t_dst += [(qT0[:, k, :], 0, 128, NT) for k in range(4)] + [(kT0[:, k, :], 0, 128, NT) for k in range(4)]
        t_dst += [(qhT[:, h, :], 0, 96, NT) for h in range(HA)]
        t_dst += [(qlT[:, c, h, :], 0, 128, NT) for h in range(HA) for c in range(2)]
        t_dst += [(qT1[:, k, :], 0, 128, NT) for k in range(8)] + [(kT1[:, k, :], 0, 128, NT) for k in range(2)]

        def t_copies(engine, copy, act, t0, t1):
            for t in range(t0, t1):
                if by_act(t) == act:
                    dst, r0, r1, n = t_dst[t]
                    engine.wait_ge(t_done, t + 1)
                    copy(dst, ps[r0:r1, 512 * (4 + t % 4):512 * (4 + t % 4) + n]).then_inc(t_cpA if act else t_cpV, 1)

        def score_bank(u):
            return 0 if u < NU0 else (0, 1, 2, 7)[place(u)]

        def out_bank(u):
            return 5 if u < NU0 else 5 + u % 2

        def copy_keys(copy, kind, i, b):
            if kind == "As":
                copy(kcT[:, 0:2048].rearrange("p (c n) -> p c n", c=2)[:, :, 128 * i:128 * i + 128],
                     bank(b, 256).rearrange("p (c n) -> p c n", c=2))
                return copy(kcT[64:96, 2048 + 128 * i:2176 + 128 * i], ps[64:96, 512 * b + 256:512 * b + 384])
            if kind == "Bs":
                return copy(kcT[:, 0:2560].rearrange("p (j n) -> p j n", j=4)[:, :, 128 * i:128 * i + 128],
                            bank(b).rearrange("p (j n) -> p j n", j=4))
            return copy(kcT_c[:, i, :, :], bank(b, 256).rearrange("p (j n) -> p j n", j=2))

        block = ctx.enter_context(nc.Block())

        unit_at = {unit: u for u, unit in enumerate(units)}
        used = []
        for kind, j, _n in plan:
            used.append({
                "ada0": (ada_done, j + 1), "ada1": (ada_done, 13 + j), "in_ab": (z_done, 3 * (j + 1)), "q_b": (q_done, 6),
                "bk": (sc_done, unit_at.get(("Bs", j), 0) + 1),
                "bv": (pv_done, unit_at.get(("Bs", j), 0) + 1),
                "mla": (pv_done, unit_at.get(("As", j), 0) + 1),
                "out_ab": (f_done, 4 * (j + 1)), "ffd_in": (gu_done, 2 * (j + 1)), "ffd_out": (f_done, 9 + j),
                "qkv_c": (z_done, 18 + 3 * j), "c_cache": (pv_done, unit_at["Cs", NB - 1] + 1), "out_c": (f_done, 20 + 4 * j),
            }[kind])

        def slot_of(kind, j):
            return at[(kind, j)] % NSLOT

        def chunk(kind, j, off, n):
            return ring[:, slot_of(kind, j), off:off + n]

        @block.sync
        def _(sp):
            sp.dma_start(xtok[:, 0:2, :], t_in["x_prompt"][0].rearrange("(t p) d -> p t d", p=P)).then_inc(s_xload, 16)
            sp.dma_start(cst[:, :], t_in["cst"][:, :]).then_inc(s_xload, 16)
            sp.dma_start(xtok[0:NS, 2, :], t_in["x_sample"].rearrange("b t d -> (b t) d")).then_inc(s_xload, 16)
            sp.dma_start(ctok[0:1, :], t_in["c_prompt"]).then_inc(s_xload, 16)
            sp.dma_start(ctok[1:9, :], t_in["c_sample"]).then_inc(s_xload, 16)
            sp.dma_start(vecA, t_in["b_ada"].rearrange("l (m p) -> (l m) p", p=P)).then_inc(s_ldm, 16)
            for i, name in enumerate(("g_pre_mix", "g_post_mix", "g_pre_ffn", "g_post_ffn")):
                sp.dma_start(vecB[16 * i:16 * i + 16, :], t_in[name].rearrange("l (m p) -> (l m) p", p=P)).then_inc(s_ldm, 16)

            def free(n):
                if n >= NSLOT:
                    sp.wait_ge(*used[n - NSLOT])

            def ada0():
                w = t_in["w_ada"][0].rearrange("(k p) m -> p k m", p=P)
                for j in range(4):
                    sp.dma_start(chunk("ada0", j, 0, 4096).rearrange("p (k m) -> p k m", k=KD),
                                 w[:, :, 512 * j:512 * j + 512]).then_inc(s_in[j], 16)
                with sp.Fori(1, 3) as i:
                    for q in range(4):
                        sp.wait_ge(ada_done, 4 * i + (q - 3))
                        sp.dma_start(ring[:, q, :].rearrange("p (k m) -> p k m", k=KD),
                                     w[:, :, bass.ds(2048 * i + 512 * q, 512)]).then_inc(s_in[q], 16)

            def put(kind, j):
                n = at[(kind, j)]
                free(n)
                s = s_in[n % NSLOT]
                if kind == "in_ab":
                    c0, w = ((0, 384), (384, 288), (672, 512), (1184, 512), (1696, 512))[j]
                    sp.dma_start(chunk(kind, j, 0, 8 * w).rearrange("p (k m) -> p k m", k=KD),
                                 t_in["w_in_ab"][0].rearrange("(k p) m -> p k m", p=P)[:, :, c0:c0 + w]).then_inc(s, 16)
                elif kind == "ada1":
                    sp.dma_start(chunk(kind, j, 0, KD * A1).rearrange("p (k m) -> p k m", k=KD),
                                 t_in["w_ada"][1].rearrange("(k p) m -> p k m", p=P)[:, :, A1 * j:A1 * j + A1]).then_inc(s, 16)
                elif kind == "q_b":
                    sp.dma_start(chunk(kind, j, 0, 2304).rearrange("p (k m) -> p k m", k=3),
                                 t_in["w_q_b"][0].rearrange("(k p) m -> p k m", p=P)).then_inc(s, 16)
                elif kind in ("bk", "bv"):
                    src = t_in["cache_b_k" if kind == "bk" else "cache_b_v"][0, j].rearrange("s h d -> s (h d)")
                    sp.dma_start(chunk(kind, j, 0, 512),
                                 src[0:512, :].rearrange("(g r) n -> g r n", r=16)[:, 0:4, :]).then_inc(s, 16)
                    sp.dma_start(chunk(kind, j, 512, 2048), src[512:1024, :].rearrange("(p i) n -> p (i n)", i=4)).then_inc(s, 16)
                elif kind == "mla":
                    ck, kr = t_in["cache_mla_ckv"][0], t_in["cache_mla_krope"][0]
                    with sp.Fori(0, NPG) as i:
                        page = sp.value_load(ptab[0:1, bass.ds(NPG * j + i, 1)], min_val=0, max_val=ck.shape[0] - 1)
                        sp.dma_start(ring[:, n % NSLOT, bass.ds(256 * i, 256)],
                                     ck[bass.ds(page, 1), :, :].rearrange("a s c -> (a s) c")).then_inc(s, 16)
                        sp.dma_start(ring[:, n % NSLOT, bass.ds(2048 + 64 + 96 * i, 32)],
                                     kr[bass.ds(page, 1), :, :].rearrange("a s c -> (a s) c")).then_inc(s, 16)
                elif kind == "out_ab":
                    sp.dma_start(chunk(kind, j, 0, 4096).rearrange("p (k m) -> p k m", k=KD),
                                 t_in["w_out_ab"][0].rearrange("(k p) m -> p k m", p=P)[:, :, 512 * j:512 * j + 512]).then_inc(s, 16)
                elif kind == "ffd_in":
                    w = t_in["w_ffd_in"][0].rearrange("(k p) (g m) -> p k g m", p=P, g=2)
                    for g in range(2):
                        sp.dma_start(chunk(kind, j, 2048 * g, 2048).rearrange("p (k m) -> p k m", k=KD),
                                     w[:, :, g, 256 * j:256 * j + 256]).then_inc(s, 16)
                elif kind == "ffd_out":
                    sp.dma_start(chunk(kind, j, 0, 2816).rearrange("p (f m) -> p f m", f=22),
                                 t_in["w_ffd_out"][0].rearrange("(f p) m -> p f m", p=P)[:, :, 128 * j:128 * j + 128]).then_inc(s, 16)
                elif kind == "qkv_c":
                    sp.dma_start(chunk(kind, j, 0, 4096).rearrange("p (k m) -> p k m", k=KD),
                                 t_in["w_qkv_c"][0].rearrange("(k p) m -> p k m", p=P)[:, :, 512 * j:512 * j + 512]).then_inc(s, 16)
                elif kind == "c_cache":
                    for w, name in enumerate(("cache_c_k", "cache_c_v")):
                        sp.dma_start(chunk(kind, j, 2048 * w, 2048).rearrange("p (b n) -> p b n", b=NB),
                                     t_in[name][0].rearrange("b s h d -> s b (h d)")).then_inc(s, 16)
                elif kind == "out_c":
                    w = t_in["w_out_c"][0].rearrange("(b r d) m -> b d r m", r=4, d=64)
                    for a in range(2):
                        for jj in range(2):
                            sp.dma_start(ring[64 * a:64 * a + 64, n % NSLOT, 2048 * jj:2048 * jj + 2048].rearrange("p (r m) -> p r m", r=4),
                                         w[2 * jj + a, :, :, 512 * j:512 * j + 512]).then_inc(s, 16)

            ada0()
            sp.wait_ge(s_pt, 16)
            for kind, j, _n in plan[12:]:
                put(kind, j)

            wi = t_in["w_moe_in"][0].rearrange("e (k p) m -> p e k m", p=P)
            wo = t_in["w_moe_out"][0].rearrange("e (f p) m -> p e f m", p=P)

            def expert_loads(it, i, half):
                e = 2 * i + half

                def put_in(j):
                    c = 14 * half + j
                    sl = (NPLAN + c) % NSLOT
                    sp.wait_ge(e_gu, 56 * it + (2 * c + 2))
                    for g in range(2):
                        src = wi[:, bass.ds(e, 1), :, g * FE + 256 * j:g * FE + 256 * j + 256].rearrange("p a k m -> p (a k) m")
                        sp.dma_start(ring[:, sl, 2048 * g:2048 * g + 2048].rearrange("p (k m) -> p k m", k=KD),
                                     src).then_inc(s_in[sl], 16)

                def put_out(q):
                    sp.wait_ge(e_used, 16 * it + (8 * half + q + 1))
                    src = wo[:, bass.ds(e, 1), 14 * (q % 2):14 * (q % 2) + 14, 256 * (q // 2):256 * (q // 2) + 256]
                    sp.dma_start(oring[:, q % 4, :].rearrange("p (f m) -> p f m", f=14),
                                 src.rearrange("p a f m -> p (a f) m")).then_inc(e_in[q % 4], 16)

                for j in range(4):
                    put_in(j)
                for q in range(4):
                    put_out(q)
                for j in range(4, 14):
                    put_in(j)
                for q in range(4, 8):
                    put_out(q)

            def pass_body(it0):
                with sp.Fori(0, NE // 2) as i:
                    for half in range(2):
                        expert_loads(it0 + i, i, half)

            pass_body(0)
            sp.wait_ge(pass_rdy, 1)
            npass = sp.value_load(passes_i[0:1, :], min_val=1, max_val=MAXPASS)
            with sp.If(npass > 1):
                with sp.Fori(1, npass) as p_:
                    pass_body(4 * p_)

        @block.gpsimd
        def _(gp):
            gp.dma_start(ptab[:, :], t_in["page_table"].rearrange("b g -> (b g)").rearrange("(a n) -> a n", a=1)).then_inc(s_pt, 16)
            gp.dma_start(gqkv[:, 0:QL], t_in["g_q_a"].broadcast_to([P, QL])).then_inc(s_ld, 16)
            gp.dma_start(gqkv[:, QL:QL + KV], t_in["g_kv_a"].broadcast_to([P, KV])).then_inc(s_ld, 16)
            gp.dma_start(sinks[:, :], t_in["sinks_c"].broadcast_to([P, HC])).then_inc(s_ld, 16)
            gp.dma_start(brout[:, :], t_in["b_router"].broadcast_to([P, NE])).then_inc(s_ld, 16)
            with nc.allow_non_contiguous_dma(reason="64 single values"):
                gp.dma_start(sinkr[:, :], t_in["sinks_c"].rearrange("a (h o) -> h a o", o=1).broadcast_to([HC, TS, 1])).then_inc(s_ld, 16)
            gp.dma_start(wrout[:, :, :], t_in["w_router"][0].rearrange("(k p) e -> p k e", p=P)).then_inc(s_ld, 16)
            gp.dma_start(kvb[:, :, :], t_in["w_kv_b"][0].rearrange("(c p) h n -> p c (h n)", p=P)).then_inc(s_ld, 16)
            gp.dma_start(msk, t_in["msk"][:, :]).then_inc(s_ld, 16)

            def store(dst, src, s):
                gp.dma_start(dst, src).then_inc(s, 16)

            gp.wait_ge(z_rdy, 5)
            gp.wait_ge(z_cp, 15)
            store(t_out["p_ckv"].rearrange("(t p) c -> p t c", p=P), z_ckv[:, 0:2, :], s_out0)
            store(t_out["p_kr"].rearrange("(t p) c -> p t c", p=P), z_kr[:, 0:2, 64:96], s_out0)
            store(t_out["p_bk"].rearrange("(t p) c -> p t c", p=P), z_qk[:, 0:2, 512:1024], s_out0)
            store(t_out["p_bv"].rearrange("(t p) c -> p t c", p=P), z_v[:, 0:2, :], s_out0)
            store(t_out["s_ckv"][:, :], z_ckv[0:NS, 2, :], s_out0)
            store(t_out["s_kr"][:, :], z_kr[0:NS, 2, 64:96], s_out0)
            store(t_out["s_bk"][:, :], z_qk[0:NS, 2, 512:1024], s_out0)
            store(t_out["s_bv"][:, :], z_v[0:NS, 2, :], s_out0)
            gp.wait_ge(z_rdy, 11)
            gp.wait_ge(z_cp, 24)
            store(t_out["p_ck"][:, :], z_c[:, 1, 1024:1280], s_out1)
            store(t_out["p_cv"][:, :], z_c[:, 1, 1280:1536], s_out1)
            store(t_out["s_ck"][:, :], z_c[0:NS, 2, 1024:1280], s_out1)
            store(t_out["s_cv"][:, :], z_c[0:NS, 2, 1280:1536], s_out1)
            for kk in range(2):
                cols = slice(512 * kk, 512 * kk + 512)
                gp.wait_ge(y_cp, 3 * kk + 3)
                for t in range(2):
                    store(t_out["y_prompt"][128 * t:128 * t + 128, cols], htok[t][:, cols], s_out)
                store(t_out["y_sample"][:, cols], htok[2][0:NS, cols], s_out)
            gp.wait_ge(s_out0, 8 * 16)
            gp.wait_ge(s_out1, 4 * 16)
            gp.wait_ge(s_out, 6 * 16)

        @block.tensor
        def _(pe):
            mm, tp = nc.tensor.matmul, nc.tensor.transpose

            def landed(kind, j):
                n = at[(kind, j)]
                pe.wait_ge(s_in[n % NSLOT], arrived[n])

            def sums(n):
                if n % 2 or n == 0:
                    pe.wait_ge(sq_added, (n + 1) // 2 + 1)
                    mm(bank(7, NT), ones, sq[:, 0, :], start=True, stop=True).then_inc(stat_done, 1)
                    return
                for k in range(KD):
                    pe.wait_ge(sq_done, 8 * n + k + 1)
                    last = mm(bank(7, NT), ones, sq[:, k, :], start=(k == 0), stop=(k == KD - 1))
                last.then_inc(stat_done, 1)

            def ada_rows(w, b, n=512, before_last=None):
                for k in range(KD):
                    if k == KD - 1 and before_last:
                        before_last()
                    last = mm(bank(b, n, 0, 9), csT[:, k, :], w[:, k, :], start=(k == 0), stop=(k == KD - 1))
                last.then_inc(ada_done, 1)

            def ada0():
                def can_turn(i, q, first):
                    pe.wait_ge(ada_row, 4 * i + (q + 1))
                    if q >= 2 or not first:
                        pe.wait_ge(ada_add, 4 * i + (q - 1))

                def turn(q):
                    for m in range(4):
                        last = tp(bank(6 + q % 2, 9, 9 * m), mrow[0][q % 2][:, 128 * m:128 * m + 128], ident[0:9, 0:9])
                    last.then_inc(ada_tp, 1)

                def round_(i, first):
                    for q in range(4):
                        pe.wait_ge(s_in[q], 16 * i + 16)
                        if q >= 2 or not first:
                            pe.wait_ge(ada_row, 4 * i + (q - 1))
                        w = ring[:, q, :].rearrange("p (k m) -> p k m", k=KD)
                        if first and q == 0:
                            ada_rows(w, 4)
                            continue
                        before = (i, q - 1, first) if q else (i - 1, 3, False)
                        ada_rows(w, 4 + q % 2, 512, lambda: can_turn(*before))
                        turn((q - 1) % 4)

                round_(0, True)
                with pe.Fori(1, 3) as i:
                    round_(i, False)
                can_turn(2, 3, False)
                turn(3)

            def linear_out(L, kind, per, nk, rhs):
                for k in range(KD):
                    j, m = k // per, k % per
                    if m == 0:
                        landed(kind, j)
                    if L or k >= 2:
                        pe.wait_ge(f_cp, 8 * L + k - 1)
                    w = chunk(kind, j, 0, nk * per * 128).rearrange("p (f m) -> p f m", f=nk)
                    for f in range(nk):
                        last = mm(bank(4 + k % 2, NT), w[:, f, 128 * m:128 * m + 128], rhs[:, f, :],
                                  start=(f == 0), stop=(f == nk - 1))
                    last.then_inc(f_done, 1)

            pe.wait_ge(s_xload, 5 * 16)
            for k in range(KD):
                if k >= 2:
                    pe.wait_ge(x_cp, k - 1)
                for t, (t0, n) in enumerate(TILES):
                    last = tp(bank(k % 2, n, t0), xtok[0:n, t, 128 * k:128 * k + 128], ident[0:n, 0:n])
                last.then_inc(x_tp, 1)
            pe.wait_ge(c_silu, 1)
            for k in range(KD):
                last = tp(bank(2, 9, 9 * k), cstok[:, 128 * k:128 * k + 128], ident[0:9, 0:9])
            pe.wait_ge(s_ldm, 5 * 16)
            tp(bank(3, 96), vecA, ident[0:96, 0:96])
            tp(bank(3, 64, 96), vecB, ident[0:64, 0:64]).then_inc(c_tp, 1)
            sums(0)
            pe.wait_ge(c_cp, 1)
            ada0()

            nt = 0

            def t_bank():
                if nt >= 4:
                    copied(pe, nt - 4)
                return 4 + nt % 4

            pe.wait_ge(s_ld, 8 * 16)
            pe.wait_ge(ada_add, 12)
            for hp in range(4):
                b = t_bank()
                for q in range(4):
                    h, c = 2 * hp + q // 2, q % 2
                    last = tp(bank(b, 128, 128 * q, 64), kvb[:, c, 128 * h:128 * h + 64], ident)
                last.then_inc(t_done, 1)
                nt += 1

            nz = 0
            for j, w in enumerate((384, 288, 512, 512, 512)):
                landed("in_ab", j)
                wt = chunk("in_ab", j, 0, 8 * w).rearrange("p (k m) -> p k m", k=KD)
                for t, (t0, n) in enumerate(TILES):
                    if nz >= 4:
                        pe.wait_ge(z_cp, nz - 3)
                    for k in range(KD):
                        if nz == 0:
                            pe.wait_ge(h_done, k + 1)
                        last = mm(bank(nz % 4, w, 0, n), hT[:, k, t0:t0 + n], wt[:, k, :], start=(k == 0), stop=(k == KD - 1))
                    last.then_inc(z_done, 1)
                    nz += 1
            def tp_tiles(src, m):
                nonlocal nt
                b = t_bank()
                for t, (t0, n) in enumerate(TILES):
                    last = tp(bank(b, n, t0, m), src(t, n), ident[0:n, 0:n])
                last.then_inc(t_done, 1)
                nt += 1

            pe.wait_ge(z_rdy, 1)
            for k in range(3):
                tp_tiles(lambda t, n: z_qa[0:n, t, 128 * k:128 * k + 128], 128)
            pe.wait_ge(z_rdy, 2)
            for k in range(2):
                tp_tiles(lambda t, n: z_ckv[0:n, t, 128 * k:128 * k + 128], 128)
            tp_tiles(lambda t, n: z_kr[0:n, t, :], 96)
            landed("q_b", 0)
            copied(pe, T_CKV - 1)
            wt = chunk("q_b", 0, 0, 2304).rearrange("p (k m) -> p k m", k=3)
            for t, (t0, n) in enumerate(TILES):
                for hh in range(2):
                    i = 2 * t + hh
                    pe.wait_ge(z_cp, 15)
                    if i >= 4:
                        pe.wait_ge(q_cp, i - 3)
                    for k in range(3):
                        last = mm(bank(i % 4, 384, 0, n), qnT[:, k, t0:t0 + n], wt[:, k, 384 * hh:384 * hh + 384],
                                  start=(k == 0), stop=(k == 2))
                    last.then_inc(q_done, 1)
            pe.wait_ge(z_rdy, 5)
            for k in range(8):
                tp_tiles(lambda t, n: z_qk[0:n, t, 128 * k:128 * k + 128], 128)
            pe.wait_ge(q_rope, 3)
            for h in range(HA):
                tp_tiles(lambda t, n: z2[0:n, t, 96 * h:96 * h + 96], 96)
            copied(pe, nt - 1)
            for h in range(HA):
                for c in range(2):
                    b = t_bank()
                    mm(bank(b, NT), wukT[0:64, h, 128 * c:128 * c + 128], qhT[0:64, h, :], start=True, stop=True).then_inc(t_done, 1)
                    nt += 1
            copied(pe, nt - 1)
            pe.wait_ge(bd_rdy, 1)
            kt_n = [0, 0]

            def cache_tiles(u):
                kind, b = units[u]
                if kind not in ktiles_of:
                    return
                if kind == "As":
                    landed("mla", b)
                else:
                    landed("bk", b)
                for i in range(ktiles_of[kind]):
                    par = i % 2
                    bk = KT_BANKS[i % 3]
                    if i >= 3:
                        pe.wait_ge(kt_cp[1 - par], kt_n[1 - par] - 1)
                    elif i == 2:
                        n = sum(a < u - 2 for a in ada1)
                        if n:
                            pe.wait_ge(ada_add, 12 + n)
                    if kind == "As":
                        for c in range(2):
                            tp(bank(bk, 128, 128 * c), chunk("mla", b, 256 * i + 128 * c, 128), ident)
                        last = tp(bank(bk, 128, 256, 96), chunk("mla", b, 2048 + 96 * i, 96), ident)
                    else:
                        for j in range(4):
                            last = tp(bank(bk, 128, 128 * j), chunk("bk", b, 512 * i + 128 * j, 128), ident)
                    last.then_inc(kt_tp[par], 1)
                    kt_n[par] += 1


            def unit_scores(u):
                kind, i = units[u]
                if 0 < u < NU0:
                    pe.wait_ge(sc_cp, u)
                elif u >= NU0 + 4:
                    pe.wait_ge(sc_cp, u - 3)
                if kind in ("As", "Bs"):
                    for par in range(2):
                        if kt_n[par]:
                            pe.wait_ge(kt_cp[par], kt_n[par])
                if kind in ("Ap", "Bp", "Cp"):
                    for qt, (c0, nk) in enumerate(((0, 128), (128, 256))):
                        q0 = 128 * qt
                        out = bank(score_bank(u), nk, c0)
                        if kind == "Ap":
                            mm(out, qlT[:, 0, i, q0:q0 + 128], ckvT[:, 0, 0:nk], start=True, stop=False)
                            mm(out, qlT[:, 1, i, q0:q0 + 128], ckvT[:, 1, 0:nk], start=False, stop=False)
                            last = mm(out, qhT[64:96, i, q0:q0 + 128], krT[64:96, 0:nk], start=False, stop=True)
                        elif kind == "Bp":
                            r = 64 * (i % 2)
                            last = mm(out, qT0[r:r + 64, i // 2, q0:q0 + 128], kT0[r:r + 64, i // 2, 0:nk], start=True, stop=True)
                        else:
                            g = i // 4
                            r = 64 * (g % 2)
                            last = mm(out, qT1[r:r + 64, 4 * (g // 2) + i % 4, q0:q0 + 128], kT1[r:r + 64, g // 2, 0:nk],
                                      start=True, stop=True)
                elif kind == "As":
                    keys = kcT[:, 0:2048].rearrange("p (c n) -> p c n", c=2)
                    kr = kcT[64:96, 2048:3072]
                    parts = [(0, 0, 512, keys, kr, 0), (1, 0, 512, keys, kr, 512), (7, 384, 32, ckvT, krT[64:96, :], NTP)]
                    for b, c0, n, kk, rr, k0 in parts:
                        for c in range(2):
                            mm(bank(b, n, c0, 32), qls[:, c, i, :], kk[:, c, k0:k0 + n], start=(c == 0), stop=False)
                        last = mm(bank(b, n, c0, 32), qhs[64:96, i, :], rr[:, k0:k0 + n], start=False, stop=True)
                elif kind == "Bs":
                    keys = kcT[:, 0:2560].rearrange("p (j n) -> p j n", j=4)
                    for b, c0, n, kk, k0 in ((0, 0, 512, keys, 0), (1, 0, 128, keys, 512), (1, 128, 32, kT0, NTP)):
                        for j in range(4):
                            last = mm(bank(b, n, c0, 32), qbd0[:, i, j, :], kk[:, j, k0:k0 + n], start=(j == 0), stop=(j == 3))
                else:
                    keys = kcT_c[:, i, :, :]
                    for c0, n, kk, k0 in ((0, 128, keys, 0), (128, 32, kT1, NTP)):
                        for j in range(2):
                            last = mm(bank(score_bank(u), n, c0, 64), qbd1[:, i, j, :], kk[:, j, k0:k0 + n], start=(j == 0), stop=(j == 1))
                last.then_inc(sc_done, 1)

            def unit_transposes(u):
                kind, i = units[u]
                n = rows_of[kind]
                pe.wait_ge(pr_done, u + 1)
                if u >= 2:
                    pe.wait_ge(pt_cp, u - 1)
                b = 3 + u % 2
                sc = scores_of(u)
                if n == 128:
                    for q in range(3):
                        last = tp(bank(b, 128, 128 * (q if q == 0 else 1 + (q - 1))), sc[:, 128 * q:128 * q + 128], ident)
                else:
                    nk = ktiles_of[kind]
                    for q in range(nk):
                        last = tp(bank(b, n, n * q), sc[0:n, 128 * q:128 * q + 128], ident[0:n, 0:n])
                    last = tp(bank(b, n, n * nk, 32), sc[0:n, 128 * nk:128 * nk + 32], ident[0:n, 0:n])
                last.then_inc(pt_tp, 1)

            def unit_pv(u):
                kind, i = units[u]
                pe.wait_ge(pt_cp, u + 1)
                if 0 < u < NU0:
                    pe.wait_ge(pv_cp, u)
                elif u >= NU0:
                    pe.wait_ge(pv_cp, u - 1)
                pT = probsT[:, u % 2, :]
                if kind == "Ap":
                    for c in range(2):
                        v0, v1 = z_ckv[:, 0, 128 * c:128 * c + 128], z_ckv[:, 1, 128 * c:128 * c + 128]
                        mm(bank(5, 128, 256 * c), v0, pT[:, 0:128], start=True, stop=True)
                        mm(bank(5, 128, 256 * c + 128), v0, pT[:, 128:256], start=True, stop=False)
                        last = mm(bank(5, 128, 256 * c + 128), v1, pT[:, 256:384], start=False, stop=True)
                elif kind in ("Bp", "Cp"):
                    if kind == "Bp":
                        r, v0, vv = 64 * (i % 2), 64 * i, z_v
                    else:
                        r, v0, vv = 64 * (i // 4 % 2), 1280 + 64 * (i // 4), z_c
                    out = ps[r:r + 64, out_bank(u) * 512:out_bank(u) * 512 + 256]
                    mm(out[:, 0:128], vv[:, 0, v0:v0 + 64], pT[:, 0:128], start=True, stop=True)
                    mm(out[:, 128:256], vv[:, 0, v0:v0 + 64], pT[:, 128:256], start=True, stop=False)
                    last = mm(out[:, 128:256], vv[:, 1, v0:v0 + 64], pT[:, 256:384], start=False, stop=True)
                elif kind == "As":
                    for c in range(2):
                        for q in range(NPG):
                            mm(bank(5, 32, 32 * c), chunk("mla", i, 256 * q + 128 * c, 128), pT[:, 32 * q:32 * q + 32],
                               start=(q == 0), stop=False)
                        last = mm(bank(5, 32, 32 * c), z_ckv[0:32, 2, 128 * c:128 * c + 128], pT[0:32, 256:288], start=False, stop=True)
                elif kind == "Bs":
                    landed("bv", i)
                    for q in range(5):
                        mm(bank(5, 512, 0, 32), pT[:, 32 * q:32 * q + 32], chunk("bv", i, 512 * q, 512), start=(q == 0), stop=False)
                    mm(bank(5, 512, 0, 32), pT[0:32, 160:192], z_v[0:32, 2, :], start=False, stop=True).then_inc(ob_done, 1)
                    return
                else:
                    for j in range(2):
                        mm(bank(out_bank(u), 64, 64 * j), chunk("c_cache", 0, 2048 + 256 * i + 128 * j, 128), pT[:, 0:64], start=True, stop=False)
                        last = mm(bank(out_bank(u), 64, 64 * j), z_c[0:32, 2, 1280 + 128 * j:1408 + 128 * j], pT[0:32, 64:128],
                                  start=False, stop=True)
                last.then_inc(pv_done, 1)

            def unit_turn(u):
                kind, i = units[u]
                if kind != "Bs":
                    return
                pe.wait_ge(ob_cp, i + 1)
                for j in range(4):
                    last = tp(bank(3 + u % 2, 32, 32 * j), scores[0:32, u % 2, 128 * j:128 * j + 128], ident[0:32, 0:32])
                last.then_inc(pv_done, 1)

            def ada1_rows(j):
                landed("ada1", j)
                if j:
                    pe.wait_ge(ada_add, 12 + j)
                ada_rows(chunk("ada1", j, 0, KD * A1).rearrange("p (k m) -> p k m", k=KD), 2, A1)

            def ada1_turn(j):
                pe.wait_ge(ada_row, 13 + j)
                for m in range(A1 // P):
                    last = tp(bank(2, 9, 9 * m), mrow[1][j % 2][:, 128 * m:128 * m + 128], ident[0:9, 0:9])
                last.then_inc(ada_tp, 1)

            def attention0():
                u0, u1 = 0, NU0
                cache_tiles(0)
                unit_scores(0)
                ada1_rows(ada1[-1])
                for u in range(u0, u1):
                    unit_transposes(u)
                    if u - 1 in ada1:
                        ada1_turn(ada1[u - 1])
                    if u + 1 < u1:
                        unit_scores(u + 1)
                    unit_pv(u)
                    if u in ada1:
                        ada1_rows(ada1[u])
                    if u + 2 < u1:
                        cache_tiles(u + 2)
                    unit_turn(u)

            def attention1():
                landed("c_cache", 0)
                for b in range(NB):
                    par = b % 2
                    pe.wait_ge(kt_cp[par], kt_n[par])
                    for j in range(2):
                        last = tp(bank(7 - par, 128, 128 * j), chunk("c_cache", 0, 256 * b + 128 * j, 128), ident)
                    last.then_inc(kt_tp[par], 1)
                    kt_n[par] += 1
                for par in range(2):
                    pe.wait_ge(kt_cp[par], kt_n[par])
                for u in range(NU0, NU0 + 3):
                    unit_scores(u)
                for u in range(NU0, NU):
                    unit_transposes(u)
                    if u + 3 < NU:
                        unit_scores(u + 3)
                    unit_pv(u)

            attention0()
            pe.wait_ge(pv_cp, NU0)
            for h in range(HA):
                if h >= 4:
                    pe.wait_ge(oa_cp[h % 2], h // 2 - 1)
                r = 64 * (h % 2)
                for c in range(2):
                    last = mm(ps[r:r + 64, 512 * (h % 4):512 * (h % 4) + NT], kvb[:, c, 128 * h + 64:128 * h + 128],
                              qlT[:, c, h, :], start=(c == 0), stop=(c == 1))
                last.then_inc(oa_done, 1)
            for par in range(2):
                pe.wait_ge(oa_cp[par], 4)
            linear_out(0, "out_ab", 4, KD, oT)
            sums(1)
            sums(2)
            for j in range(11):
                landed("ffd_in", j)
                w = chunk("ffd_in", j, 0, 4096).rearrange("p (g k m) -> p g k m", g=2, k=KD)
                for fb in range(2):
                    f = 2 * j + fb
                    if f >= 2:
                        pe.wait_ge(act_done, f - 1)
                    for g in range(2):
                        for k in range(KD):
                            if f == 0 and g == 0:
                                pe.wait_ge(h_done, 8 + k + 1)
                            last = mm(bank(2 * (f % 2) + g, NT), w[:, g, k, 128 * fb:128 * fb + 128], hT[:, k, :],
                                      start=(k == 0), stop=(k == KD - 1))
                    last.then_inc(gu_done, 1)
            pe.wait_ge(act_done, NFD)
            linear_out(1, "ffd_out", 1, 22, actd)
            sums(3)
            sums(4)
            for j in range(3):
                landed("qkv_c", j)
                wt = chunk("qkv_c", j, 0, 4096).rearrange("p (k m) -> p k m", k=KD)
                for t, (t0, n) in enumerate(TILES):
                    if nz >= 19:
                        pe.wait_ge(z_cp, nz - 3)
                    for k in range(KD):
                        if nz == 15:
                            pe.wait_ge(h_done, 16 + k + 1)
                        last = mm(bank(nz % 4, 512, 0, n), hT[:, k, t0:t0 + n], wt[:, k, :], start=(k == 0), stop=(k == KD - 1))
                    last.then_inc(z_done, 1)
                    nz += 1
            mm(bank(7, 4), ident, ones[:, 0:4], start=True, stop=True).then_inc(e_gu, 2)
            pe.wait_ge(z_rdy, 8)
            for k in range(8):
                tp_tiles(lambda t, n: z_c[0:n, t, 128 * k:128 * k + 128], 128)
            pe.wait_ge(z_rdy, 11)
            for k in range(2):
                tp_tiles(lambda t, n: z_c[0:n, t, 1024 + 128 * k:1152 + 128 * k], 128)
            copied(pe, nt - 1)
            pe.wait_ge(bd_rdy, 2)
            attention1()
            pe.wait_ge(pv_cp, NU)
            mm(bank(3, 4), ident, ones[:, 0:4], start=True, stop=True).then_inc(e_used, 4)
            mm(bank(3, 4), ident, ones[:, 0:4], start=True, stop=True).then_inc(e_gu, 2)
            linear_out(2, "out_c", 4, KD, oT)
            mm(bank(3, 4), ident, ones[:, 0:4], start=True, stop=True).then_inc(e_gu, 4)
            sums(5)
            sums(6)

            for t, (t0, n) in enumerate(TILES):
                for k in range(KD):
                    if t == 0:
                        pe.wait_ge(h_done, 24 + k + 1)
                    last = mm(bank(0, 8, 8 * t, n), hT[:, k, t0:t0 + n], wrout[:, k, :], start=(k == 0), stop=(k == KD - 1))
            last.then_inc(lg_done, 1)
            for t, (t0, n) in enumerate(TILES):
                for kk in range(2):
                    i = 2 * t + kk
                    if i >= 2:
                        pe.wait_ge(htok_cp, i - 1)
                    for k in range(4):
                        last = tp(bank(4 + i % 2, 128, 128 * k, n), hT[:, 4 * kk + k, t0:t0 + n], ident)
                    last.then_inc(htok_tp, 1)
            pe.wait_ge(msk_done, 1)
            for t in range(3):
                for tt in range(t + 1):
                    last = mm(bank(1, 8, 8 * t), cst[:, C_UP:C_UP + 128] if tt == t else ones, mask[:, tt, :],
                              start=(tt == 0), stop=(tt == t))
            for tt in range(3):
                last = mm(bank(1, 8, 24), ones, mask[:, tt, :], start=(tt == 0), stop=(tt == 2))
            last.then_inc(pos_done, 1)

            def gather(idx, k0=0, k1=KD):
                pe.wait_ge(e_pick, idx)
                for k in range(k0, k1):
                    for t, (t0, n) in enumerate(TILES):
                        last = mm(bank(k // 3, CAP, CAP * (k % 3)), htok[t][0:n, 128 * k:128 * k + 128], pick[0:n, t, :],
                                  start=(t == 0), stop=(t == 2))
                if k1 == KD:
                    last.then_inc(e_gat, 1)

            def turn_choice(adds):
                pe.wait_ge(e_add, adds)
                for w, (c0, c) in enumerate(((0, P), (P, CX))):
                    for t, (t0, n) in enumerate(TILES):
                        tp(bank(6 + w, n, t0, c), pick[0:n, t, c0:c0 + c], ident[0:n, 0:n])
                    for t, (t0, n) in enumerate(TILES):
                        last = mm(bank(6 + w, 1, 300, c), pick[0:n, t, c0:c0 + c], cur[0:n, 1, t:t + 1], start=(t == 0), stop=(t == 2))
                last.then_inc(e_ptp, 1)

            def ffn_in(it, half, rows):
                for j in range(14):
                    c = 14 * half + j
                    sl = (NPLAN + c) % NSLOT
                    times = sum(1 for q in range(c + 1) if q % NSLOT == c % NSLOT)
                    pe.wait_ge(s_in[sl], 224 * it + (ring_total[sl] + 32 * times))
                    w = ring[:, sl, :].rearrange("p (g k m) -> p g k m", g=2, k=KD)
                    for fb in range(2):
                        f = 2 * j + fb
                        pe.wait_ge(e_act, 56 * it + (28 * half + f + 1))
                        for g in range(2):
                            for k in range(KD):
                                last = mm(bank(f % 4, rows, CAP * g), w[:, g, k, 128 * fb:128 * fb + 128], hsel[:, k, 0:rows],
                                          start=(k == 0), stop=(k == KD - 1))
                        last.then_inc(e_gu, 1)
                    if j == 6:
                        turn_choice(16 * it + (8 * half + 2))

            def ffn_out(it, half, rows):
                for q in range(8):
                    pr, f2 = q // 2, q % 2
                    pe.wait_ge(e_in[q % 4], 64 * it + (32 * half + 16 * (q // 4) + 16))
                    pe.wait_ge(e_act, 56 * it + (28 * half + 14 * f2 + 14 + 4))
                    w = oring[:, q % 4, :].rearrange("p (f m) -> p f m", f=14)
                    for m in range(2):
                        if f2 == 0 and pr:
                            pe.wait_ge(e_ocp, 16 * it + (8 * half + 2 * pr + m - 1))
                        for f in range(14):
                            last = mm(bank(4 + m, rows), w[:, f, 128 * m:128 * m + 128], acte[:, 14 * f2 + f, 0:rows],
                                      start=(f2 == 0 and f == 0), stop=(f2 == 1 and f == 13))
                        if f2 == 1 and m == 0:
                            last.then_inc(e_half, 1)
                    last.then_inc(e_used, 1)

            def out_transposes(it, half):
                pe.wait_ge(e_ocp, 16 * it + (8 * half + 8))
                pe.wait_ge(e_pcp, 2 * it + (half + 1))
                for k in range(KD):
                    tp(bank(6 + k // 4, 128, 128 * (k % 4)), oeT[:, k, 0:P], ident)
                    last = tp(bank(3 + 2 * (k // 4), 128, 128 * (k % 4), CX), oeT[:, k, P:CAP], ident)
                last.then_inc(e_tp, 1)

            def combine(it, half, wide):
                pe.wait_ge(e_tcpA, 4 * it + (2 * half + 2))
                pe.wait_ge(e_tcpV, 4 * it + (2 * half + 2))
                for k in range(KD):
                    if k >= 3:
                        pe.wait_ge(e_add, 16 * it + (8 * half + k))
                    out = bank((6, 7, 5)[k % 3], NT)
                    last = mm(out, otok[0][:, 128 * k:128 * k + 128], putT[0], start=True, stop=not wide)
                    if wide:
                        last = mm(out, otok[1][:, 128 * k:128 * k + 128], putT[1], start=False, stop=True)
                    last.then_inc(e_cb, 1)

            def expert(it, i, p_, half):
                pe.wait_ge(e_gcpA, 2 * it + p_ + (half + 1))
                pe.wait_ge(e_gcpV, 2 * it + p_ + (half + 1))
                wide = pe.value_load(cnt_i[0:1, bass.ds(2 * i + half, 1)], min_val=0, max_val=NT) > p_ * CAP + P

                def body(rows):
                    ffn_in(it, half, rows)
                    ffn_out(it, half, rows)
                    gather(2 * it + p_ + (half + 2), 0, 3)
                    out_transposes(it, half)
                    gather(2 * it + p_ + (half + 2), 3, KD)
                    combine(it, half, rows > P)

                with pe.If(wide):
                    body(CAP)
                with pe.Else():
                    body(P)

            def pass_body(it0, p_):
                with pe.Fori(0, NE // 2) as i:
                    for half in range(2):
                        expert(it0 + i, i, p_, half)

            pe.wait_ge(pass_rdy, 1)
            gather(1)
            pass_body(0, 0)
            npass = pe.value_load(passes_i[0:1, :], min_val=1, max_val=MAXPASS)
            with pe.If(npass > 1):
                with pe.Fori(1, npass) as p_:
                    pe.wait_ge(e_gcpA, 9 * p_)
                    pe.wait_ge(e_gcpV, 9 * p_)
                    gather(9 * p_ + 1)
                    pass_body(4 * p_, p_)
            pe.wait_ge(e_add, 64 * npass + 2)
            sums(7)
            for kk in range(2):
                pe.wait_ge(x_upd, 24 + 4 * kk + 4)
                for t, (t0, n) in enumerate(TILES):
                    for k in range(4):
                        last = tp(bank(3 * kk + t, 128, 128 * k, n), xT[:, 4 * kk + k, t0:t0 + n], ident)
                    last.then_inc(y_tp, 1)

        @block.scalar
        def _(act):
            def fn(out, in_, f, **kw):
                return nc.scalar.activation(out, in_, f, **kw)

            def fn_copy(out, in_):
                return fn(out, in_, ACT.Copy)

            def std(n):
                act.wait_ge(stat_done, n + 1)
                fn(rstd[:, :], bank(7, NT), ACT.Sqrt, scale=1.0 / D, bias=cst[:, C_EPS:C_EPS + 1]).then_inc(std_done, 1)

            def add_shift(n, l, w):
                for k in range(KD):
                    act.wait_ge(h_part, 9 * n + k + 2)
                    fn(hT[:, k, 0:NTP], hT[:, k, 0:NTP], ACT.Identity, bias=mod[:, l, 24 * w + k, 0:1]).then_inc(h_done, 1)

            def f_out(L, n):
                for k in range(KD):
                    act.wait_ge(f_done, 8 * L + k + 1)
                    fn(sq[:, k, :], bank(4 + k % 2, NT), ACT.Square).then_inc(sq_done, 1)
                    fn(fT[:, k, :], bank(4 + k % 2, NT), ACT.Copy).then_inc(f_cp, 1)
                std(n)

            def x_squares(m):
                for k in range(KD):
                    act.wait_ge(x_upd, 8 * m + k + 1)
                    fn(sq[:, k, :], xT[:, k, :], ACT.Square).then_inc(sq_done, 1)
                std(2 * m + 2)

            act.wait_ge(s_xload, 5 * 16)
            fn(cstok, ctok, ACT.Silu).then_inc(c_silu, 1)
            for k in range(KD):
                act.wait_ge(x_tp, k + 1)
                fn(sq[:, k, :], bank(k % 2, NT), ACT.Square).then_inc(sq_done, 1)
                fn(xT[:, k, :], bank(k % 2, NT), ACT.Copy).then_inc(x_cp, 1)
            std(0)
            for j in range(12):
                act.wait_ge(ada_done, j + 1)
                if j >= 2:
                    act.wait_ge(ada_tp, j - 1)
                fn(mrow[0][j % 2], bank(4 + j % 2, 512, 0, 9), ACT.Copy).then_inc(ada_row, 1)
            t_copies(act, fn_copy, True, 0, 4)
            add_shift(0, 0, 0)

            nz = 0
            for j, w in enumerate((384, 288, 512, 512, 512)):
                for t, (t0, n) in enumerate(TILES):
                    act.wait_ge(z_done, nz + 1)
                    b = nz % 4
                    if j == 0:
                        fn(z_qa[0:n, t, :], bank(b, 384, 0, n), ACT.Copy)
                        fn(bank(b, 384, 0, n), bank(b, 384, 0, n), ACT.Square, accum_out=ss[0:n, t, 0:1]).then_inc(z_cp, 1)
                    elif j == 1:
                        fn(z_ckv[0:n, t, :], bank(b, 256, 0, n), ACT.Copy)
                        fn(z_kr[0:n, t, 64:96], bank(b, 32, 256, n), ACT.Copy)
                        fn(bank(b, 256, 0, n), bank(b, 256, 0, n), ACT.Square, accum_out=ss[0:n, t, 1:2]).then_inc(z_cp, 1)
                    elif j < 4:
                        fn(z_qk[0:n, t, 512 * (j - 2):512 * (j - 1)], bank(b, 512, 0, n), ACT.Copy).then_inc(z_cp, 1)
                    else:
                        fn(z_v[0:n, t, :], bank(b, 512, 0, n), ACT.Copy).then_inc(z_cp, 1)
                    nz += 1
                if j < 2:
                    act.wait_ge(z_cp, nz)
                    for t, (t0, n) in enumerate(TILES):
                        last = fn(ss[0:n, t, 2 + j:3 + j], ss[0:n, t, j:j + 1], ACT.Sqrt, scale=1.0 / (QL, KV)[j],
                                  bias=cst[0:n, C_EPS:C_EPS + 1])
                    last.then_inc(qn_rdy, 1)
            for t, (t0, n) in enumerate(TILES):
                for hh in range(2):
                    act.wait_ge(q_done, 2 * t + hh + 1)
                    fn(z2[0:n, t, 384 * hh:384 * hh + 384], bank((2 * t + hh) % 4, 384, 0, n), ACT.Copy).then_inc(q_cp, 1)
            t_copies(act, fn_copy, True, T_QK, T_1)

            kt_n = [0, 0]

            def cache_tiles(u):
                kind, b = units[u]
                for i in range(ktiles_of.get(kind, 0)):
                    par = i % 2
                    kt_n[par] += 1
                    if par:
                        continue
                    act.wait_ge(kt_tp[0], kt_n[0])
                    copy_keys(fn_copy, kind, i, KT_BANKS[i % 3]).then_inc(kt_cp[0], 1)

            def unit_exp(u):
                kind, i = units[u]
                n = rows_of[kind]
                sc = scores_of(u)
                act.wait_ge(mx_done, u + 1)
                if n == 128:
                    fn(sc[:, 0:128], sc[:, 0:128], ACT.Exp, bias=nmax[:, place(u), 0:1], accum_out=lsum[:, place(u), 0:1])
                    last = fn(sc[:, 128:384], sc[:, 128:384], ACT.Exp, bias=nmax[:, place(u), 1:2], accum_out=lsum[:, place(u), 1:2])
                    if kind == "Cp":
                        for q in range(2):
                            last = fn(lsum[:, place(u), 2 + q:3 + q], sinks[:, i:i + 1], ACT.Exp, bias=nmax[:, place(u), q:q + 1])
                else:
                    w = 128 * ktiles_of[kind] + 32
                    last = fn(sc[0:n, 0:w], sc[0:n, 0:w], ACT.Exp, bias=nmax[0:n, place(u), 0:1], accum_out=lsum[0:n, place(u), 0:1])
                    if kind == "Cs":
                        last = fn(lsum[0:n, place(u), 2:3], sinkr[:, :], ACT.Exp, bias=nmax[0:n, place(u), 0:1])
                last.then_inc(ex_done, 1)

            def unit_copies(u):
                kind, i = units[u]
                n = rows_of[kind]
                act.wait_ge(pt_tp, u + 1)
                b = 3 + u % 2
                pT = probsT[:, u % 2, :]
                if n == 128:
                    fn(pT[:, 0:384], bank(b, 384), ACT.Copy).then_inc(pt_cp, 1)
                else:
                    w = n * ktiles_of[kind]
                    fn(pT[:, 0:w], bank(b, w), ACT.Copy)
                    fn(pT[0:32, w:w + n], bank(b, n, w, 32), ACT.Copy).then_inc(pt_cp, 1)

            def unit_rows(u):
                kind, i = units[u]
                if kind == "Bs":
                    act.wait_ge(ob_done, i + 1)
                    fn(scores[0:32, u % 2, 0:512], bank(5, 512, 0, 32), ACT.Copy).then_inc(ob_cp, 1)

            def unit_out(u):
                kind, i = units[u]
                act.wait_ge(pv_done, u + 1)
                tok = NTP + TS * i
                if kind == "Ap":
                    last = fn(qlT[:, :, i, 0:256], bank(5).rearrange("p (c n) -> p c n", c=2), ACT.Copy)
                elif kind == "Bp":
                    r = 64 * (i % 2)
                    last = fn(oT[r:r + 64, 4 + i // 2, 0:256], ps[r:r + 64, 2560:2816], ACT.Copy)
                elif kind == "Cp":
                    g = i // 4
                    r = 64 * (g % 2)
                    last = fn(oT[r:r + 64, 4 * (g // 2) + i % 4, 0:256], ps[r:r + 64, 512 * out_bank(u):512 * out_bank(u) + 256], ACT.Copy)
                elif kind == "As":
                    for c in range(2):
                        last = fn(qlT[:, c, :, tok:tok + TS], bank(5, 32, 32 * c).rearrange("p (h t) -> p h t", t=TS), ACT.Copy)
                elif kind == "Bs":
                    for r in range(2):
                        for j in range(4):
                            c0 = 512 * (3 + u % 2) + 32 * j + 4 * (2 * j + r)
                            last = fn(oT[64 * r:64 * r + 64, 4 + j, tok:tok + TS], ps[64 * r:64 * r + 64, c0:c0 + 4], ACT.Copy)
                else:
                    for r in range(2):
                        for j in range(2):
                            c0 = 512 * out_bank(u) + 64 * j + 16 * (2 * j + r)
                            last = fn(oT[64 * r:64 * r + 64, 4 * j:4 * j + 4, tok:tok + TS],
                                      ps[64 * r:64 * r + 64, c0:c0 + 16].rearrange("p (r t) -> p r t", t=TS), ACT.Copy)
                last.then_inc(pv_cp, 1)

            def ada1_copy(j):
                act.wait_ge(ada_done, 13 + j)
                act.wait_ge(ada_tp, 11 + j)
                fn(mrow[1][j % 2][:, 0:A1], bank(2, A1, 0, 9), ACT.Copy).then_inc(ada_row, 1)

            def attention0():
                u0, u1 = 0, NU0
                cache_tiles(0)
                unit_exp(0)
                ada1_copy(ada1[-1])
                for u in range(u0, u1):
                    unit_copies(u)
                    if u + 1 < u1:
                        unit_exp(u + 1)
                    unit_rows(u)
                    if units[u][0] != "Bs":
                        unit_out(u)
                    if u in ada1:
                        ada1_copy(ada1[u])
                    if u + 2 < u1:
                        cache_tiles(u + 2)
                    if units[u][0] == "Bs":
                        unit_out(u)

            def attention1():
                for b in range(0, NB, 2):
                    kt_n[0] += 1
                    act.wait_ge(kt_tp[0], kt_n[0])
                    copy_keys(fn_copy, "Cs", b, 7).then_inc(kt_cp[0], 1)
                for u in range(NU0, NU0 + 3):
                    unit_exp(u)
                unit_copies(NU0)
                for u in range(NU0, NU):
                    unit_out(u)
                    if u + 1 < NU:
                        unit_copies(u + 1)
                    if u + 3 < NU:
                        unit_exp(u + 3)

            act.wait_ge(s_out0, 8 * 16)
            attention0()
            for h in range(0, HA, 2):
                act.wait_ge(oa_done, h + 1)
                fn(oT[0:64, h // 2, :], ps[0:64, 512 * (h % 4):512 * (h % 4) + NT], ACT.Copy).then_inc(oa_cp[0], 1)
            f_out(0, 1)
            x_squares(0)
            add_shift(1, 0, 1)
            for f in range(NFD):
                act.wait_ge(gu_done, f + 1)
                if f:
                    act.wait_ge(act_done, f)
                fn(silu_d, bank(2 * (f % 2), NT), ACT.Silu).then_inc(si_done, 1)
            f_out(1, 3)
            x_squares(1)
            add_shift(2, 1, 0)
            for j in range(3):
                for t, (t0, n) in enumerate(TILES):
                    act.wait_ge(z_done, nz + 1)
                    out, src = z_c[0:n, t, 512 * j:512 * j + 512], bank(nz % 4, 512, 0, n)
                    if j < 2:
                        out = out.rearrange("p (r a d) -> p a r d", a=2, r=4)
                        src = src.rearrange("p (a r d) -> p a r d", a=2, r=4)
                    fn(out, src, ACT.Copy).then_inc(z_cp, 1)
                    nz += 1
            t_copies(act, fn_copy, True, T_1, len(t_dst))
            attention1()
            f_out(2, 5)
            x_squares(2)
            add_shift(3, 1, 1)

            act.wait_ge(s_out1, 4 * 16)
            for t, (t0, n) in enumerate(TILES):
                for kk in range(2):
                    i = 2 * t + kk
                    act.wait_ge(htok_tp, i + 1)
                    fn(htok[t][0:n, 512 * kk:512 * kk + 512], bank(4 + i % 2, 512, 0, n), ACT.Copy).then_inc(htok_cp, 1)
            act.wait_ge(lg_cp, 1)
            fn(gate[:, :, 1:2], gate[:, :, 0:1], ACT.Exp).then_inc(ge_done, 1)

            def gather_copy(idx):
                act.wait_ge(e_gat, idx)
                fn(hsel[:, 0:3, :], bank(0, 3 * CAP).rearrange("p (k n) -> p k n", k=3), ACT.Copy)
                fn(hsel[:, 6:8, :], bank(2, 2 * CAP).rearrange("p (k n) -> p k n", k=2), ACT.Copy).then_inc(e_gcpA, 1)

            def expert(it, p_, half):
                for f in range(NFE):
                    act.wait_ge(e_gu, 56 * it + (28 * half + f + 9))
                    act.wait_ge(e_act, 56 * it + (28 * half + f + 3))
                    fn(sil[:, f % 2, :], bank(f % 4, CAP), ACT.Silu).then_inc(e_si, 1)
                    if f == 15:
                        act.wait_ge(e_ptp, 2 * it + (half + 1))
                        for w, c in enumerate((P, CX)):
                            fn(putT[w], bank(6 + w, NT, 0, c), ACT.Copy)
                            last = fn(gpl[0:c, w:w + 1], bank(6 + w, 1, 300, c), ACT.Copy)
                        last.then_inc(e_pcp, 1)
                for pr in range(4):
                    act.wait_ge(e_half, 8 * it + (4 * half + pr + 1))
                    fn(oeT[:, 2 * pr, :], bank(4, CAP), ACT.Copy).then_inc(e_ocp, 1)
                    act.wait_ge(e_used, 16 * it + (8 * half + 2 * pr + 6))
                    fn(oeT[:, 2 * pr + 1, :], bank(5, CAP), ACT.Copy).then_inc(e_ocp, 1)
                act.wait_ge(e_pcp, 2 * it + (half + 1))
                act.wait_ge(e_tp, 2 * it + (half + 1))
                for kk in range(2):
                    fn(otok[0][:, 512 * kk:512 * kk + 512], bank(6 + kk), ACT.Copy, scale=gpl[:, 0:1]).then_inc(e_tcpA, 1)
                gather_copy(2 * it + p_ + (half + 2))

            def pass_body(it0, p_):
                with act.Fori(0, NE // 2) as i:
                    for half in range(2):
                        expert(it0 + i, p_, half)

            gather_copy(1)
            pass_body(0, 0)
            act.wait_ge(pass_rdy, 1)
            npass = act.value_load(passes_i[0:1, :], min_val=1, max_val=MAXPASS)
            with act.If(npass > 1):
                with act.Fori(1, npass) as p_:
                    gather_copy(9 * p_ + 1)
                    pass_body(4 * p_, p_)
            act.wait_ge(e_add, 64 * npass + 2)
            for k in range(KD):
                fn(sq[:, k, :], fT[:, k, :], ACT.Square).then_inc(sq_done, 1)
            std(7)
            for i in range(6):
                kk, t = i // 3, i % 3
                n = TILES[t][1]
                act.wait_ge(y_tp, i + 1)
                fn(htok[t][0:n, 512 * kk:512 * kk + 512], bank(i, 512, 0, n), ACT.Copy).then_inc(y_cp, 1)

        @block.vector
        def _(dve):
            V = nc.vector
            nv = [0]

            def link(ins):
                nv[0] += 1
                ins.then_inc(chain_v, 1)
                dve.wait_ge(chain_v, nv[0])

            def sample(t, k0=0, k1=KD):
                return t[:, k0:k1, NTP:NT].rearrange("p k (b t) -> p k b t", t=TS)

            def per_batch(t):
                return t[:, :, 1:9].unsqueeze(3).broadcast_to([P, KD, NB, TS])

            def pre_norm(n, l, w):
                sh = mod[:, l, 24 * w:24 * w + 8, :]
                if n:
                    dve.wait_ge(x_upd, 4 * n)
                else:
                    dve.wait_ge(x_cp, KD)
                link(V.tensor_tensor(sample(hT), sample(xT), per_batch(coef[:, 2 * w, :, :]), ALU.mult))
                dve.wait_ge(std_done, n + 1)
                link(V.reciprocal(rinv[:, :], rstd[:, :]))
                link(V.tensor_tensor(sample(hT), sample(hT), sample_rinv(), ALU.mult))
                V.tensor_tensor(sample(hT), sample(hT), per_batch(sh), ALU.add).then_inc(h_part, 1)
                for k in range(KD):
                    V.scalar_tensor_tensor(out=hT[:, k, 0:NTP], in0=xT[:, k, 0:NTP], scalar=coef[:, 2 * w, k, 0:1],
                                           in1=rinv[:, 0:NTP], op0=ALU.mult, op1=ALU.mult).then_inc(h_part, 1)

            def sample_rinv():
                return rinv[:, NTP:NT].rearrange("p (b t) -> p b t", t=TS).unsqueeze(1).broadcast_to([P, KD, NB, TS])

            def add_square(n, k):
                if k == 0:
                    return
                dve.wait_ge(sq_done, 8 * n + k + 1)
                ins = V.tensor_tensor(sq[:, 0, :], sq[:, 0, :], sq[:, k, :], ALU.add)
                if k < KD - 1:
                    link(ins)
                else:
                    ins.then_inc(sq_added, 1)

            def post_norm(n, m, w):
                g = coef[:, 2 * w + 1, :, :]
                for k in range(KD):
                    if m == 3:
                        dve.wait_ge(sq_done, 8 * n + k + 1)
                    else:
                        dve.wait_ge(f_cp, 8 * m + k + 1)
                    add_square(n, k)
                    V.tensor_scalar(fT[:, k, 0:NTP], fT[:, k, 0:NTP], g[:, k, 0:1], None, ALU.mult)
                    last = V.tensor_tensor(fT[:, k, NTP:NT].rearrange("p (b t) -> p b t", t=TS),
                                           fT[:, k, NTP:NT].rearrange("p (b t) -> p b t", t=TS),
                                           g[:, k, 1:9].unsqueeze(2).broadcast_to([P, NB, TS]), ALU.mult)
                link(last)
                dve.wait_ge(std_done, n + 1)
                link(V.reciprocal(rinv[:, :], rstd[:, :]))
                base = nv[0]

                def scaled(k):
                    nv[0] += 1
                    V.tensor_tensor(fT[:, k, :], fT[:, k, :], rinv[:, :], ALU.mult).then_inc(chain_v, 1)

                scaled(0)
                for k in range(KD):
                    if k + 1 < KD:
                        scaled(k + 1)
                    dve.wait_ge(chain_v, base + k + 1)
                    V.tensor_tensor(xT[:, k, :], xT[:, k, :], fT[:, k, :], ALU.add).then_inc(x_upd, 1)

            def ada_bias(l, m0, m):
                return vecT[:, 48 * l + m0:48 * l + m0 + m].unsqueeze(2).broadcast_to([P, m, 9])

            def coefficients(l):
                for w in range(2):
                    for i, (name, blk) in enumerate((("pre", 8), ("post", 16))):
                        g = vecT[:, 96 + 32 * w + 16 * i + 8 * l:96 + 32 * w + 16 * i + 8 * l + 8].unsqueeze(2).broadcast_to([P, 8, 9])
                        src = mod[:, l, 24 * w + blk:24 * w + blk + 8, :]
                        if name == "pre":
                            V.scalar_tensor_tensor(out=coef[:, 2 * w, :, :], in0=src, scalar=1.0, in1=g, op0=ALU.add, op1=ALU.mult)
                        else:
                            last = V.tensor_tensor(coef[:, 2 * w + 1, :, :], src, g, ALU.mult)
                link(last)

            def rope(x, n, heads, half, tab, ta, tb, done=None, value=0):
                c = tab[0:n, 0:2 * half].unsqueeze(1).broadcast_to([n, heads, 2 * half])
                s1 = tab[0:n, 2 * half:3 * half].unsqueeze(1).broadcast_to([n, heads, half])
                s2 = tab[0:n, 3 * half:4 * half].unsqueeze(1).broadcast_to([n, heads, half])
                V.tensor_tensor(ta, x[:, :, 0:2 * half], c, ALU.mult)
                V.tensor_tensor(tb[:, :, 0:half], x[:, :, half:2 * half], s1, ALU.mult)
                link(V.tensor_tensor(tb[:, :, half:2 * half], x[:, :, 0:half], s2, ALU.mult))
                last = V.tensor_tensor(x[:, :, 0:2 * half], ta, tb, ALU.add)
                if done is None:
                    link(last)
                else:
                    last.then_inc(done, 1)
                    dve.wait_ge(done, value)

            def rope_tmp(region, n, heads, w):
                a = region[0:n, 0:heads * w].rearrange("p (h w) -> p h w", h=heads)
                b = region[0:n, heads * w:2 * heads * w].rearrange("p (h w) -> p h w", h=heads)
                return a, b

            for k in range(KD):
                add_square(0, k)
            dve.wait_ge(c_tp, 1)
            V.tensor_copy(csT[:, :, :], bank(2, 72).rearrange("p (k c) -> p k c", c=9)).then_inc(c_cp, 1)
            link(V.tensor_copy(vecT[:, :], bank(3, 160)))
            V.memset(z_kr[:, :, 0:64], 0.0)
            link(V.memset(qbd, 0.0))
            with dve.Fori(0, 3) as i:
                for q in range(4):
                    dve.wait_ge(ada_tp, 4 * i + (q + 1))
                    V.tensor_tensor(mod[:, 0, bass.ds(16 * i + 4 * q, 4), :], bank(6 + q % 2, 36).rearrange("p (m c) -> p m c", c=9),
                                    vecT[:, bass.ds(16 * i + 4 * q, 4)].unsqueeze(2).broadcast_to([P, 4, 9]), ALU.add).then_inc(ada_add, 1)
            dve.wait_ge(s_ld, 8 * 16)
            V.tensor_scalar(nsinks[:, :], sinks[:, :], -1.0, None, ALU.mult)
            link(V.tensor_scalar(nsinkr[:, :], sinkr[:, :], -1.0, None, ALU.mult))
            dve.wait_ge(ada_add, 12)
            coefficients(0)
            pre_norm(0, 0, 0)

            for j, (zz, width, g0) in enumerate(((z_qa, QL, 0), (z_ckv, KV, QL))):
                dve.wait_ge(qn_rdy, j + 1)
                for t, (t0, n) in enumerate(TILES):
                    last = V.reciprocal(ss[0:n, t, 4 + j:5 + j], ss[0:n, t, 2 + j:3 + j])
                link(last)
                if j == 1:
                    for t, (t0, n) in enumerate(TILES):
                        kr = z_kr[0:n, t:t + 1, 64:96]
                        ta, tb = rope_tmp(rtmp2[:, 640:960], n, 1, 32)
                        rope(kr, n, 1, 16, cst[:, C_RA + 64 * t:C_RA + 64 * t + 64], ta, tb)
                for t, (t0, n) in enumerate(TILES):
                    last = V.scalar_tensor_tensor(out=zz[0:n, t, :], in0=zz[0:n, t, :], scalar=ss[0:n, t, 4 + j:5 + j],
                                                  in1=gqkv[0:n, g0:g0 + width], op0=ALU.mult, op1=ALU.mult)
                last.then_inc(z_rdy, 1)
            t_copies(dve, V.tensor_copy, False, T_QN, T_QK)
            dve.wait_ge(z_cp, 12)
            for t, (t0, n) in enumerate(TILES):
                ta, tb = rope_tmp(rtmp2, n, 16, 16)
                rope(z_qk[0:n, t, :].rearrange("p (h d) -> p h d", h=16), n, 16, 8, cst[:, C_RB + 32 * t:C_RB + 32 * t + 32], ta, tb, z_rdy, 3 + t)
            for t, (t0, n) in enumerate(TILES):
                dve.wait_ge(q_cp, 2 * t + 2)
                ta, tb = rope_tmp(rtmp2, n, 8, 32)
                rope(z2[0:n, t, :].rearrange("p (h d) -> p h d", h=8)[:, :, 64:96], n, 8, 16,
                     cst[:, C_RA + 64 * t:C_RA + 64 * t + 64], ta, tb, q_rope, t + 1)
            t_copies(dve, V.tensor_copy, False, T_QK, T_1)
            copied(dve, T_1 - 1)
            for c in range(2):
                V.tensor_copy(qls[:, c, :, :].rearrange("p b (h t) -> p h b t", t=TS),
                              qlT[:, c, :, NTP:NT].rearrange("p h (b t) -> p h b t", t=TS))
            V.tensor_copy(qhs[64:96, :, :].rearrange("p b (h t) -> p h b t", t=TS),
                          qhT[64:96, :, NTP:NT].rearrange("p h (b t) -> p h b t", t=TS))
            for j in range(4):
                for r in range(2):
                    h = 2 * j + r
                    last = V.tensor_copy(qbd0[64 * r:64 * r + 64, :, j, 4 * h:4 * h + 4],
                                         qT0[64 * r:64 * r + 64, j, NTP:NT].rearrange("p (b t) -> p b t", t=TS))
            last.then_inc(bd_rdy, 1)
            dve.wait_ge(s_out0, 8 * 16)

            kt_n = [0, 0]

            def cache_tiles(u, before_last=None):
                kind, b = units[u]
                for i in range(ktiles_of.get(kind, 0)):
                    par = i % 2
                    kt_n[par] += 1
                    if not par:
                        continue
                    if before_last and i + 2 >= ktiles_of[kind]:
                        before_last()
                    dve.wait_ge(kt_tp[1], kt_n[1])
                    copy_keys(V.tensor_copy, kind, i, KT_BANKS[i % 3]).then_inc(kt_cp[1], 1)

            def unit_max(u):
                kind, i = units[u]
                n = rows_of[kind]
                sc = scores_of(u)
                dve.wait_ge(sc_done, u + 1)
                if u >= NU0 + 4:
                    dve.wait_ge(pt_tp, u - 3)
                elif u < NU0 and u >= 2:
                    if units[u - 2][0] == "Bs":
                        dve.wait_ge(pv_done, u - 1)
                    else:
                        dve.wait_ge(pt_tp, u - 1)
                scale = MLA_SCALE if kind[0] == "A" else HD_SCALE

                def masked(out, src, m):
                    return V.scalar_tensor_tensor(out=out, in0=src, scalar=scale, in1=m, op0=ALU.mult, op1=ALU.add)

                if n == 128:
                    m0 = {"A": M_A, "B": M_B, "C": M_C}[kind[0]]
                    last = masked(sc[:, 0:384], bank(score_bank(u), 384), msk[:, m0:m0 + 384])
                    w = 384
                elif kind == "As":
                    V.tensor_scalar(sc[0:32, 0:1024], ps[0:32, 0:1024], scale, None, ALU.mult)
                    last = masked(sc[0:32, 1024:1056], bank(7, 32, 384, 32), msk[0:32, M_NA + 32 * i:M_NA + 32 * i + 32])
                    w = 1056
                elif kind == "Bs":
                    masked(sc[0:32, 0:640], ps[0:32, 0:640], msk[0:32, M_SB:M_SB + 640])
                    last = masked(sc[0:32, 640:672], ps[0:32, 640:672], msk[0:32, M_NB + 32 * i:M_NB + 32 * i + 32])
                    w = 672
                else:
                    masked(sc[0:64, 0:128], bank(score_bank(u), 128, 0, 64), cst[0:64, C_CM:C_CM + 128])
                    last = masked(sc[0:64, 128:160], bank(score_bank(u), 32, 128, 64), msk[0:64, M_NA + 32 * i:M_NA + 32 * i + 32])
                    w = 160
                last.then_inc(sc_cp, 1)
                dve.wait_ge(sc_cp, u + 1)
                nm = nmax[:, place(u), :]
                if n == 128:
                    V.tensor_reduce(nm[:, 0:1], sc[:, 0:128], AX_X, ALU.max, negate=True)
                    last = V.tensor_reduce(nm[:, 1:2], sc[:, 128:384], AX_X, ALU.max, negate=True)
                    if kind == "Cp":
                        link(last)
                        last = V.tensor_scalar(nm[:, 0:2], nm[:, 0:2], nsinks[:, i:i + 1], None, ALU.min)
                else:
                    last = V.tensor_reduce(nm[0:n, 0:1], sc[0:n, 0:w], AX_X, ALU.max, negate=True)
                    if kind == "Cs":
                        link(last)
                        last = V.tensor_scalar(nm[0:n, 0:1], nm[0:n, 0:1], nsinkr[:, :], None, ALU.min)
                last.then_inc(mx_done, 1)

            def unit_probs(u):
                kind, i = units[u]
                n = rows_of[kind]
                sc = scores_of(u)
                ls, r = lsum[:, place(u), :], rl[:, place(u), :]
                dve.wait_ge(ex_done, u + 1)
                nh = 2 if n == 128 else 1
                if kind[0] == "C":
                    link(V.tensor_tensor(ls[0:n, 0:nh], ls[0:n, 0:nh], ls[0:n, 2:2 + nh], ALU.add))
                link(V.reciprocal(r[0:n, 0:nh], ls[0:n, 0:nh]))
                if nh == 2:
                    V.tensor_scalar(sc[:, 0:128], sc[:, 0:128], r[:, 0:1], None, ALU.mult)
                    V.tensor_scalar(sc[:, 128:384], sc[:, 128:384], r[:, 1:2], None, ALU.mult).then_inc(pr_done, 1)
                else:
                    w = 128 * ktiles_of[kind] + 32
                    V.tensor_scalar(sc[0:n, 0:w], sc[0:n, 0:w], r[0:n, 0:1], None, ALU.mult).then_inc(pr_done, 1)

            def ada1_add(j):
                m = A1 // P
                dve.wait_ge(ada_tp, 13 + j)
                V.tensor_tensor(mod[:, 1, m * j:m * j + m, :], bank(2, 9 * m).rearrange("p (m c) -> p m c", c=9),
                                ada_bias(1, m * j, m), ALU.add).then_inc(ada_add, 1)

            def attention0():
                u0, u1 = 0, NU0
                cache_tiles(0)
                unit_max(0)
                unit_probs(0)
                ada1_add(ada1[-1])
                for u in range(u0, u1):
                    if u + 1 < u1:
                        unit_max(u + 1)
                    if u + 2 < u1 and units[u + 2][0] in ktiles_of:
                        cache_tiles(u + 2, lambda: unit_probs(u + 1))
                    elif u + 1 < u1:
                        unit_probs(u + 1)
                    if u in ada1:
                        ada1_add(ada1[u])

            def attention1():
                for b in range(1, NB, 2):
                    kt_n[1] += 1
                    dve.wait_ge(kt_tp[1], kt_n[1])
                    copy_keys(V.tensor_copy, "Cs", b, 6).then_inc(kt_cp[1], 1)
                for u in range(NU0, NU0 + 3):
                    unit_max(u)
                unit_probs(NU0)
                for u in range(NU0, NU):
                    if u + 1 < NU:
                        unit_probs(u + 1)
                    if u + 3 < NU:
                        unit_max(u + 3)

            attention0()
            for h in range(1, HA, 2):
                dve.wait_ge(oa_done, h + 1)
                V.tensor_copy(oT[64:128, h // 2, :], ps[64:128, 512 * (h % 4):512 * (h % 4) + NT]).then_inc(oa_cp[1], 1)
            post_norm(1, 0, 0)
            pre_norm(2, 0, 1)
            for f in range(NFD):
                dve.wait_ge(si_done, f + 1)
                V.tensor_tensor(actd[:, f, :], bank(2 * (f % 2) + 1, NT), silu_d, ALU.mult).then_inc(act_done, 1)
            post_norm(3, 1, 1)
            link(V.memset(qbd, 0.0))
            dve.wait_ge(ada_add, 12 + NA1)
            coefficients(1)
            pre_norm(4, 1, 0)
            for (c0, heads), cps, z0 in (((0, 16), 21, 6), ((1024, 4), 24, 9)):
                dve.wait_ge(z_cp, cps)
                for t, (t0, n) in enumerate(TILES):
                    ta, tb = rope_tmp(rtmp2, n, heads, 16)
                    rope(z_c[0:n, t, c0:c0 + 64 * heads].rearrange("p (h d) -> p h d", h=heads), n, heads, 8,
                         cst[:, C_RB + 32 * t:C_RB + 32 * t + 32], ta, tb, z_rdy, z0 + t)
            t_copies(dve, V.tensor_copy, False, T_1, len(t_dst))
            copied(dve, len(t_dst) - 1)
            for j in range(2):
                for r in range(2):
                    g = 2 * j + r
                    for b in range(NB):
                        last = V.tensor_copy(qbd1[64 * r:64 * r + 64, b, j, 16 * g:16 * g + 16].rearrange("p (r t) -> p r t", t=TS),
                                             qT1[64 * r:64 * r + 64, 4 * j:4 * j + 4, NTP + TS * b:NTP + TS * b + TS])
            last.then_inc(bd_rdy, 1)
            attention1()
            post_norm(5, 2, 0)
            pre_norm(6, 1, 1)

            V.memset(oh, 0.0)
            V.memset(gate, 0.0)
            V.memset(posm, -1.0)
            V.memset(topf, 0.0)
            V.memset(gates, 0.0).then_inc(e_add, 2)
            V.memset(cnt, 0.0).then_inc(e_act, 4)
            link(V.memset(fT, 0.0))
            dve.wait_ge(lg_done, 1)
            for t, (t0, n) in enumerate(TILES):
                last = V.tensor_tensor(logit[0:n, t, :], bank(0, 8, 8 * t, n), brout[0:n, :], ALU.add)
            link(last)
            for t, (t0, n) in enumerate(TILES):
                last = V.max(top[0:n, t, :], logit[0:n, t, :])
            link(last)
            for t, (t0, n) in enumerate(TILES):
                V.max_index(topi[0:n, t, :], top[0:n, t, :], logit[0:n, t, :])
                last = V.tensor_tensor(gate[0:n, t, 0:1], top[0:n, t, 1:2], top[0:n, t, 0:1], ALU.subtract)
            last.then_inc(lg_cp, 1)
            dve.wait_ge(lg_cp, 1)
            for t, (t0, n) in enumerate(TILES):
                last = V.tensor_copy(topf[0:n, t, :], topi[0:n, t, 0:2])
            link(last)
            for t, (t0, n) in enumerate(TILES):
                for w in range(2):
                    last = V.tensor_scalar(oh[0:n, w, t, :], cst[0:n, C_I8:C_I8 + 8], topf[0:n, t, w:w + 1], None, ALU.is_equal)
            link(last)
            V.tensor_tensor(mask, oh[:, 0, :, :], oh[:, 1, :, :], ALU.add).then_inc(msk_done, 1)
            dve.wait_ge(ge_done, 1)
            link(V.tensor_scalar(gate[:, :, 2:3], gate[:, :, 1:2], 1.0, None, ALU.add))
            link(V.reciprocal(gate[:, :, 2:3], gate[:, :, 2:3]))
            link(V.tensor_tensor(gate[:, :, 3:4], gate[:, :, 2:3], gate[:, :, 1:2], ALU.mult))
            for w in range(2):
                last = V.tensor_tensor(oh[:, w, :, :], oh[:, w, :, :], gate[:, :, 2 + w:3 + w].broadcast_to([P, 3, NE]), ALU.mult)
            link(last)
            link(V.tensor_tensor(gates[:, 0:NE, :].rearrange("p n t -> p t n"), oh[:, 0, :, :], oh[:, 1, :, :], ALU.add))
            dve.wait_ge(msk_done, 1)
            dve.wait_ge(pos_done, 1)
            link(V.scalar_tensor_tensor(out=pm_t, in0=bank(1, 24).rearrange("p (t n) -> p t n", t=3), scalar=1.0, in1=mask,
                                        op0=ALU.add, op1=ALU.mult))
            link(V.tensor_scalar(posm[:, 0:NE, :].rearrange("p n t -> p t n"), pm_t, -1.0, None, ALU.add))
            link(V.tensor_reduce(passes, bank(1, 8, 24), AX_X, ALU.max))
            for q in range(1, MAXPASS):
                V.tensor_scalar(cnt[:, q:q + 1], passes, float(CAP * q), None, ALU.is_gt)
            V.memset(cnt[:, MAXPASS:MAXPASS + 1], 1.0)
            link(V.memset(cnt[:, 0:1], 0.0))
            link(V.tensor_reduce(passes, cnt[:, 1:MAXPASS + 1], AX_X, ALU.add))
            V.tensor_copy(cnt_i, bank(1, 8, 24, 1))
            V.tensor_copy(passes_i, passes).then_inc(pass_rdy, 1)

            ne = [0]

            def elink(ins, base):
                ne[0] += 1
                ins.then_inc(chain_e, 1)
                dve.wait_ge(chain_e, base + ne[0])

            def choose(e, gathered, turned, base):
                if gathered is not None:
                    dve.wait_ge(e_gat, gathered)
                    dve.wait_ge(e_ptp, turned)
                V.tensor_copy(cur[:, 0:1, :], posm[:, bass.ds(e, 1), :])
                elink(V.tensor_copy(cur[:, 1:2, :], gates[:, bass.ds(e, 1), :]), base)
                for t in range(3):
                    last = V.tensor_scalar(pick[:, t, :], iota_c, cur[:, 0, t:t + 1], None, ALU.is_equal)
                last.then_inc(e_pick, 1)

            def gather_copy(idx):
                dve.wait_ge(e_gat, idx)
                V.tensor_copy(hsel[:, 3:6, :], bank(1, 3 * CAP).rearrange("p (k n) -> p k n", k=3)).then_inc(e_gcpV, 1)

            def expert(it, i, p_, half, base):
                for f in range(NFE):
                    dve.wait_ge(e_si, 56 * it + (28 * half + f + 1))
                    V.tensor_tensor(acte[:, f, :], bank(f % 4, CAP, CAP), sil[:, f % 2, :], ALU.mult).then_inc(e_act, 1)
                    if f == 17:
                        choose(2 * i + (half + 1), 2 * it + p_ + (half + 1), 2 * it + (half + 1), base)
                dve.wait_ge(e_pcp, 2 * it + (half + 1))
                dve.wait_ge(e_tp, 2 * it + (half + 1))
                for kk in range(2):
                    V.tensor_scalar(otok[1][:, 512 * kk:512 * kk + 512], bank(3 + 2 * kk, 512, 0, CX), gpl[0:CX, 1:2], None,
                                    ALU.mult).then_inc(e_tcpV, 1)
                gather_copy(2 * it + p_ + (half + 2))
                for k in range(KD):
                    dve.wait_ge(e_cb, 16 * it + (8 * half + k + 1))
                    V.tensor_tensor(fT[:, k, :], bank((6, 7, 5)[k % 3], NT), fT[:, k, :], ALU.add).then_inc(e_add, 1)

            def pass_body(it0, p_, base):
                with dve.Fori(0, NE // 2) as i:
                    ne[0] = 0
                    for half in range(2):
                        expert(it0 + i, i, p_, half, base + 2 * i)
                assert ne[0] == 2

            ne[0] = 0
            choose(0, None, None, 0)
            gather_copy(1)
            pass_body(0, 0, 1)
            dve.wait_ge(pass_rdy, 1)
            npass = dve.value_load(passes_i[0:1, :], min_val=1, max_val=MAXPASS)
            with dve.If(npass > 1):
                with dve.Fori(1, npass) as p_:
                    dve.wait_ge(e_pick, 9 * p_)
                    ne[0] = 0
                    base = 10 * p_ - 1
                    elink(V.tensor_scalar(posm[:, :, :], posm[:, :, :], float(-CAP), None, ALU.add), base)
                    choose(0, 9 * p_, 8 * p_, base)
                    gather_copy(9 * p_ + 1)
                    pass_body(4 * p_, p_, 10 * p_ + 1)
            dve.wait_ge(e_add, 64 * npass + 2)
            post_norm(7, 3, 1)

    return nc


_INS = ["x_prompt", "x_sample", "c_prompt", "c_sample", "cache_mla_ckv", "cache_mla_krope", "cache_b_k", "cache_b_v",
        "cache_c_k", "cache_c_v", "page_table", "w_ada", "b_ada", "g_pre_mix", "g_post_mix", "g_pre_ffn", "g_post_ffn",
        "w_in_ab", "g_q_a", "w_q_b", "g_kv_a", "w_kv_b", "w_out_ab", "w_ffd_in", "w_ffd_out", "w_qkv_c", "sinks_c",
        "w_out_c", "w_router", "b_router", "w_moe_in", "w_moe_out"]
_OUTS = [("y_prompt", (NTP, D), (1, NTP, D)), ("y_sample", (NS, D), (NB, TS, D)),
         ("p_ckv", (NTP, KV), (1, 1, NTP, KV)), ("p_kr", (NTP, RA), (1, 1, NTP, RA)),
         ("p_bk", (NTP, 512), (1, 1, NTP, 8, HD)), ("p_bv", (NTP, 512), (1, 1, NTP, 8, HD)),
         ("p_ck", (128, 256), (1, 1, 128, GC, HD)), ("p_cv", (128, 256), (1, 1, 128, GC, HD)),
         ("s_ckv", (NS, KV), (1, NB, TS, KV)), ("s_kr", (NS, RA), (1, NB, TS, RA)),
         ("s_bk", (NS, 512), (1, NB, TS, 8, HD)), ("s_bv", (NS, 512), (1, NB, TS, 8, HD)),
         ("s_ck", (NS, 256), (1, NB, TS, GC, HD)), ("s_cv", (NS, 256), (1, NB, TS, GC, HD))]


def kernel(**inputs):
    import concourse.bacc as bacc
    from concourse.bass_utils import run_bass_kernel_spmd as run

    nc = bacc.Bacc("TRN2", target_bir_lowering=False, num_devices=1)
    arrays, t_in, t_out = {}, {}, {}
    cst, msk = shape_constants()
    for name, a in [(n, inputs[n]) for n in _INS] + [("cst", cst), ("msk", msk)]:
        a = np.ascontiguousarray(a)
        arrays[f"in_{name}"] = a
        t_in[name] = nc.dram_tensor(f"in_{name}", a.shape, mybir.dt.from_np(a.dtype), kind="ExternalInput").ap()
    for name, shape, _ in _OUTS:
        t_out[name] = nc.dram_tensor(f"out_{name}", shape, F32, kind="ExternalOutput").ap()
    build(nc, t_in, t_out)
    r = run(nc, [arrays], core_ids=[0])
    return tuple(r.results[0][f"out_{name}"].reshape(shape) for name, _, shape in _OUTS)
```
